# Optimizing a Trainium2 kernel written in Bass

```python
import math
import jax, jax.numpy as jnp
from jax import lax
import numpy as np

D_MODEL = 1024
BATCH = 1
SEQ = 1024
DEPTH = 1

N_MEM = 256
D_MIX = D_MODEL
RET_WIDTH = D_MIX // 2
RET_HEADS = 4
RET_HEAD_DIM = RET_WIDTH // RET_HEADS
POOL_WIDTH = D_MIX - RET_WIDTH
POOL_WINDOWS = (2, 4, 8, 16)
POOL_GROUP = POOL_WIDTH // len(POOL_WINDOWS)
IN_COLS = 4 * RET_WIDTH + POOL_WIDTH
CHUNK = 128
ROPE_BASE = 10000.0
XA_HEADS = 4
XA_HEAD_DIM = D_MODEL // XA_HEADS
D_FF = ((8 * D_MODEL // 3 + 255) // 256) * 256
CONV_WIDTH = 3
EPS = 1e-6


def rmsnorm(x, g):
    x32 = x.astype(jnp.float32)
    y = x32 * lax.rsqrt(jnp.mean(x32 * x32, axis=-1, keepdims=True) + EPS)
    return (y * g.astype(jnp.float32)).astype(x.dtype)

def rope(t, positions):
    dh = t.shape[-1]
    inv_freq = jnp.exp(-math.log(ROPE_BASE) * jnp.arange(0, dh, 2, dtype=jnp.float32) / dh)
    ang = positions.astype(jnp.float32)[..., None] * inv_freq
    cos = jnp.cos(ang)[:, :, None, :].astype(t.dtype)
    sin = jnp.sin(ang)[:, :, None, :].astype(t.dtype)
    t1, t2 = jnp.split(t, 2, axis=-1)
    return jnp.concatenate([t1 * cos - t2 * sin, t2 * cos + t1 * sin], axis=-1)

def retention(q, k, v, positions):
    B, S, _ = q.shape
    H, Dh = RET_HEADS, RET_HEAD_DIM
    dt = q.dtype
    N = S // CHUNK
    q = rope(q.reshape(B, S, H, Dh), positions)
    k = rope(k.reshape(B, S, H, Dh), positions) * (Dh ** -0.5)
    v = v.reshape(B, S, H, Dh)

    def to_chunks(t):
        return t.reshape(B, N, CHUNK, H, Dh).transpose(0, 3, 1, 2, 4)

    qc, kc, vc = to_chunks(q), to_chunks(k), to_chunks(v)
    lg = jnp.log1p(-jnp.exp2(-5.0 - jnp.arange(H, dtype=jnp.float32)))
    idx = jnp.arange(CHUNK, dtype=jnp.float32)
    diff = idx[:, None] - idx[None, :]
    dmat = jnp.where(diff >= 0, jnp.exp(lg[:, None, None] * jnp.maximum(diff, 0.0)), 0.0).astype(dt)
    zeta = jnp.exp(lg[:, None] * (CHUNK - 1 - idx)).astype(dt)
    xi = jnp.exp(lg[:, None] * (idx + 1.0)).astype(dt)
    chunk_decay = jnp.exp(lg * CHUNK).astype(dt)

    scores = jnp.einsum('bhnid,bhnjd->bhnij', qc, kc) * dmat[:, None]
    intra = jnp.einsum('bhnij,bhnjv->bhniv', scores, vc)
    kv = jnp.einsum('bhnjd,bhnjv->nbhdv', kc * zeta[:, None, :, None], vc)

    def step(state, kv_n):
        return state * chunk_decay[None, :, None, None] + kv_n, state

    _, states_before = lax.scan(step, jnp.zeros((B, H, Dh, Dh), dt), kv)
    cross = jnp.einsum('bhnid,nbhdv->bhniv', qc, states_before) * xi[:, None, :, None]
    return (intra + cross).transpose(0, 2, 3, 1, 4).reshape(B, S, H, Dh)

def head_rmsnorm(y, g):
    B, S, H, Dh = y.shape
    y32 = y.astype(jnp.float32)
    y32 = y32 * lax.rsqrt(jnp.mean(y32 * y32, axis=-1, keepdims=True) + EPS)
    return (y32.reshape(B, S, H * Dh) * g.astype(jnp.float32)).astype(y.dtype)

def pool_mixer(u, w, scale):
    B, S, _ = u.shape
    u32 = u.astype(jnp.float32)
    cs = jnp.cumsum(u32, axis=1)
    t1 = jnp.arange(1, S + 1, dtype=jnp.int32)
    groups = []
    for gi, wlen in enumerate(POOL_WINDOWS):
        c = cs[:, :, gi * POOL_GROUP:(gi + 1) * POOL_GROUP]
        lower = jnp.concatenate([jnp.zeros((B, wlen, POOL_GROUP), jnp.float32), c[:, :S - wlen]], axis=1)
        count = jnp.minimum(t1, wlen).astype(jnp.float32)[None, :, None]
        mean = (c - lower) / count
        groups.append(mean - u32[:, :, gi * POOL_GROUP:(gi + 1) * POOL_GROUP])
    pooled = jnp.stack(groups, axis=2).astype(u.dtype)
    out = jnp.einsum('bsgc,gcd->bsgd', pooled, w).reshape(B, S, POOL_WIDTH)
    return out * scale

def cross_attn(h, mem_n, wq, wkv, wo):
    B, S, _ = h.shape
    q = (h @ wq).reshape(B, S, XA_HEADS, XA_HEAD_DIM)
    k, v = jnp.split(mem_n @ wkv, 2, axis=-1)
    k = k.reshape(B, N_MEM, XA_HEADS, XA_HEAD_DIM)
    v = v.reshape(B, N_MEM, XA_HEADS, XA_HEAD_DIM)
    s = jnp.einsum('bshd,bmhd->bhsm', q, k).astype(jnp.float32) * (XA_HEAD_DIM ** -0.5)
    p = jax.nn.softmax(s, axis=-1).astype(v.dtype)
    o = jnp.einsum('bhsm,bmhd->bshd', p, v).reshape(B, S, D_MODEL)
    return o @ wo

def conv_glu_ffn(h, w_up, conv_w, conv_b, w_down):
    a = h @ w_up
    S = a.shape[1]
    a1 = jnp.pad(a, ((0, 0), (1, 0), (0, 0)))[:, :S]
    a2 = jnp.pad(a, ((0, 0), (2, 0), (0, 0)))[:, :S]
    c = conv_w[0] * a2 + conv_w[1] * a1 + conv_w[2] * a + conv_b
    gate, val = jnp.split(c, 2, axis=-1)
    return (jax.nn.silu(gate) * val) @ w_down

def first_inputs(seed: int = 0) -> dict:
    key = jax.random.key(seed)
    ks = jax.random.split(key, 24)

    def nrm(k, shape, scale):
        return jax.random.normal(k, shape, jnp.float32) * scale

    L = DEPTH
    x = nrm(ks[0], (BATCH, SEQ, D_MODEL), 1.0)
    mem = nrm(ks[1], (BATCH, N_MEM, D_MODEL), 1.0)
    offs = jax.random.randint(ks[2], (BATCH, 1), 0, 1024, dtype=jnp.int32)
    positions = (offs + jnp.arange(SEQ, dtype=jnp.int32)[None, :]).astype(jnp.int32)
    return {
        "x": x,
        "mem": mem,
        "positions": positions,
        "mix_norm_g": 1.0 + nrm(ks[3], (L, D_MODEL), 0.02),
        "w_in": nrm(ks[4], (L, D_MODEL, IN_COLS), D_MODEL ** -0.5),
        "ret_gn_g": 1.0 + nrm(ks[5], (L, RET_WIDTH), 0.02),
        "pool_w": nrm(ks[6], (L, len(POOL_WINDOWS), POOL_GROUP, POOL_GROUP), POOL_GROUP ** -0.5),
        "pool_scale": 0.5 + nrm(ks[7], (L, POOL_WIDTH), 0.1),
        "w_out": nrm(ks[8], (L, D_MIX, D_MODEL), (2.0 * D_MIX) ** -0.5),
        "xa_norm_g": 1.0 + nrm(ks[9], (L, D_MODEL), 0.02),
        "mem_norm_g": 1.0 + nrm(ks[10], (D_MODEL,), 0.02),
        "xa_wq": nrm(ks[11], (L, D_MODEL, D_MODEL), D_MODEL ** -0.5),
        "xa_wkv": nrm(ks[12], (L, D_MODEL, 2 * D_MODEL), D_MODEL ** -0.5),
        "xa_wo": nrm(ks[13], (L, D_MODEL, D_MODEL), (2.0 * D_MODEL) ** -0.5),
        "ffn_norm_g": 1.0 + nrm(ks[14], (L, D_MODEL), 0.02),
        "ffn_w_up": nrm(ks[15], (L, D_MODEL, 2 * D_FF), D_MODEL ** -0.5),
        "ffn_conv_w": nrm(ks[16], (L, CONV_WIDTH, 2 * D_FF), CONV_WIDTH ** -0.5),
        "ffn_conv_b": nrm(ks[17], (L, 2 * D_FF), 0.01),
        "ffn_w_down": nrm(ks[18], (L, D_FF, D_MODEL), (2.0 * D_FF) ** -0.5),
        "final_norm_g": 1.0 + nrm(ks[19], (D_MODEL,), 0.02),
    }

def first_block(x, mem, positions, mix_norm_g, w_in, ret_gn_g, pool_w, pool_scale, w_out,
              xa_norm_g, mem_norm_g, xa_wq, xa_wkv, xa_wo, ffn_norm_g, ffn_w_up,
              ffn_conv_w, ffn_conv_b, ffn_w_down, final_norm_g):
    mem_n = rmsnorm(mem, mem_norm_g)
    R = RET_WIDTH
    for l in range(DEPTH):
        h = rmsnorm(x, mix_norm_g[l])
        proj = h @ w_in[l]
        q, k, v, g, u = jnp.split(proj, [R, 2 * R, 3 * R, 4 * R], axis=-1)
        y_ret = jax.nn.silu(g) * head_rmsnorm(retention(q, k, v, positions), ret_gn_g[l])
        y_pool = pool_mixer(u, pool_w[l], pool_scale[l])
        x = x + jnp.concatenate([y_ret, y_pool], axis=-1) @ w_out[l]
        x = x + cross_attn(rmsnorm(x, xa_norm_g[l]), mem_n, xa_wq[l], xa_wkv[l], xa_wo[l])
        x = x + conv_glu_ffn(rmsnorm(x, ffn_norm_g[l]), ffn_w_up[l], ffn_conv_w[l],
                             ffn_conv_b[l], ffn_w_down[l])
    return rmsnorm(x, final_norm_g)


DEPTH_2 = 2

N_A_LAYERS = DEPTH_2 // 2
N_B_LAYERS = DEPTH_2 - N_A_LAYERS

HEAD_DIM = 128
GDN_HEADS = D_MODEL // HEAD_DIM
GDN_DK = HEAD_DIM
GDN_DV = HEAD_DIM
GDN_WIDTH = GDN_HEADS * HEAD_DIM
CONV_K = 4
CHUNK_2 = 64
FOX_HEADS = D_MODEL // HEAD_DIM
FOX_WIDTH = FOX_HEADS * HEAD_DIM
Q_BLOCK = 128


def rms_norm(x, g):
    xf = x.astype(jnp.float32)
    y = xf * lax.rsqrt(jnp.mean(xf * xf, axis=-1, keepdims=True) + EPS)
    return (y * g.astype(jnp.float32)).astype(x.dtype)

def l2_norm(x):
    xf = x.astype(jnp.float32)
    return (xf * lax.rsqrt(jnp.sum(xf * xf, axis=-1, keepdims=True) + EPS)).astype(x.dtype)

def causal_depthwise_conv(x, w):
    rhs = w[:, None, :].astype(x.dtype)
    return lax.conv_general_dilated(
        x, rhs, window_strides=(1,), padding=((CONV_K - 1, 0),),
        dimension_numbers=("NWC", "WIO", "NWC"), feature_group_count=x.shape[-1])

def chunk_gated_delta_rule(q, k, v, g, beta):
    B, L, H, Dk = q.shape
    Dv = v.shape[-1]
    N = L // CHUNK_2
    f32 = jnp.float32
    out_dtype = v.dtype

    def chunks(t):
        t = jnp.moveaxis(t.astype(f32), 2, 1)
        return t.reshape((B, H, N, CHUNK_2) + t.shape[3:])

    qc = chunks(q) * (Dk ** -0.5)
    kc, vc = chunks(k), chunks(v)
    gc, bc = chunks(g), chunks(beta)
    gcum = jnp.cumsum(gc, axis=-1)
    causal = jnp.tril(jnp.ones((CHUNK_2, CHUNK_2), dtype=bool))
    strict = jnp.tril(jnp.ones((CHUNK_2, CHUNK_2), dtype=bool), -1)
    diff = gcum[..., :, None] - gcum[..., None, :]
    decay = jnp.where(causal, jnp.exp(jnp.where(causal, diff, 0.0)), 0.0)

    kb = kc * bc[..., None]
    a_mat = jnp.where(strict, jnp.einsum('bhncd,bhnsd->bhncs', kb, kc) * decay, 0.0)
    rhs = jnp.concatenate([vc * bc[..., None], kb * jnp.exp(gcum)[..., None]], axis=-1)
    sol = lax.linalg.triangular_solve(a_mat, rhs, left_side=True, lower=True,
                                      unit_diagonal=True)
    u, w = sol[..., :Dv], sol[..., Dv:]
    attn = jnp.einsum('bhncd,bhnsd->bhncs', qc, kc) * decay

    def step(S, inp):
        q_i, k_i, u_i, w_i, g_i, attn_i = inp
        v_new = u_i - jnp.einsum('bhck,bhkv->bhcv', w_i, S)
        o = (jnp.einsum('bhck,bhkv->bhcv', q_i * jnp.exp(g_i)[..., None], S)
             + jnp.einsum('bhcs,bhsv->bhcv', attn_i, v_new))
        g_last = g_i[..., -1]
        k_dec = k_i * jnp.exp(g_last[..., None] - g_i)[..., None]
        S = S * jnp.exp(g_last)[..., None, None] + jnp.einsum('bhck,bhcv->bhkv', k_dec, v_new)
        return S, o

    xs = tuple(jnp.moveaxis(t, 2, 0) for t in (qc, kc, u, w, gcum, attn))
    S0 = jnp.zeros((B, H, Dk, Dv), f32)
    _, o = lax.scan(step, S0, xs)
    o = o.transpose(1, 0, 3, 2, 4).reshape(B, L, H, Dv)
    return o.astype(out_dtype)

def gdn_mixer(h, w_in, conv_w, a_log, dt_bias, o_norm, w_out):
    B, L, _ = h.shape
    W, H = GDN_WIDTH, GDN_HEADS
    proj = h @ w_in
    qkv, z, a, b = jnp.split(proj, [3 * W, 4 * W, 4 * W + H], axis=-1)
    qkv = jax.nn.silu(causal_depthwise_conv(qkv, conv_w))
    q, k, v = jnp.split(qkv, 3, axis=-1)
    q = l2_norm(q.reshape(B, L, H, GDN_DK))
    k = l2_norm(k.reshape(B, L, H, GDN_DK))
    v = v.reshape(B, L, H, GDN_DV)
    beta = jax.nn.sigmoid(b.astype(jnp.float32))
    g = -jnp.exp(a_log.astype(jnp.float32)) * jax.nn.softplus(a.astype(jnp.float32) + dt_bias.astype(jnp.float32))
    o = chunk_gated_delta_rule(q, k, v, g, beta)
    o = rms_norm(o, o_norm) * jax.nn.silu(z.reshape(B, L, H, GDN_DV))
    return o.reshape(B, L, W) @ w_out

def shared_kv(h, kv_norm, kv_w, kv_forget_bias, kv_k_norm):
    B, L, _ = h.shape
    u = rms_norm(h, kv_norm)
    k, v, f = jnp.split(u @ kv_w, [FOX_WIDTH, 2 * FOX_WIDTH], axis=-1)
    k = rms_norm(k.reshape(B, L, FOX_HEADS, HEAD_DIM), kv_k_norm)
    v = v.reshape(B, L, FOX_HEADS, HEAD_DIM)
    log_f = jax.nn.log_sigmoid(f.astype(jnp.float32) + kv_forget_bias.astype(jnp.float32))
    c = jnp.cumsum(log_f, axis=1)
    return k, v, c

def fox_attention(q, k, v, c):
    B, L, H, D = q.shape
    nb = L // Q_BLOCK
    qb = q.reshape(B, nb, Q_BLOCK, H, D).transpose(1, 0, 2, 3, 4)
    cT = jnp.transpose(c, (0, 2, 1))
    cb = cT.reshape(B, H, nb, Q_BLOCK).transpose(2, 0, 1, 3)
    kpos = jnp.arange(L)
    scale = D ** -0.5

    def block(args):
        i, q_i, c_i = args
        s = jnp.einsum('bqhd,bkhd->bhqk', q_i, k, preferred_element_type=jnp.float32) * scale
        s = s + (c_i[..., :, None] - cT[..., None, :])
        qpos = i * Q_BLOCK + jnp.arange(Q_BLOCK)
        s = jnp.where(kpos[None, :] <= qpos[:, None], s, -jnp.inf)
        p = jax.nn.softmax(s, axis=-1)
        return jnp.einsum('bhqk,bkhd->bqhd', p.astype(v.dtype), v)

    o = lax.map(block, (jnp.arange(nb), qb, cb))
    return o.transpose(1, 0, 2, 3, 4).reshape(B, L, H, D)

def fox_mixer(h, k, v, c, w_in, q_norm, w_out):
    B, L, _ = h.shape
    q, z = jnp.split(h @ w_in, [FOX_WIDTH], axis=-1)
    q = rms_norm(q.reshape(B, L, FOX_HEADS, HEAD_DIM), q_norm)
    o = fox_attention(q, k, v, c)
    o = o * jax.nn.silu(z.reshape(B, L, FOX_HEADS, HEAD_DIM))
    return o.reshape(B, L, FOX_WIDTH) @ w_out

def second_inputs(seed: int = 0) -> dict:
    key = jax.random.key(seed)
    ks = jax.random.split(key, 24)
    D, W, H = D_MODEL, GDN_WIDTH, GDN_HEADS
    nA, nB = N_A_LAYERS, N_B_LAYERS

    def nrm(k, shape, fan_in):
        return jax.random.normal(k, shape, jnp.float32) * (fan_in ** -0.5)

    def gain(k, shape):
        return 1.0 + 0.05 * jax.random.normal(k, shape, jnp.float32)

    dt = jnp.exp(jax.random.uniform(ks[5], (nA, H), jnp.float32, math.log(1e-3), math.log(1e-1)))
    return {
        "x": jax.random.normal(ks[0], (BATCH, SEQ, D), jnp.float32),
        "gdn_pre_norm": gain(ks[1], (nA, D)),
        "gdn_w_in": nrm(ks[2], (nA, D, 4 * W + 2 * H), D),
        "gdn_conv_w": nrm(ks[3], (nA, CONV_K, 3 * W), CONV_K),
        "gdn_a_log": jnp.log(jax.random.uniform(ks[4], (nA, H), jnp.float32, 1.0, 16.0)),
        "gdn_dt_bias": dt + jnp.log(-jnp.expm1(-dt)),
        "gdn_o_norm": gain(ks[6], (nA, GDN_DV)),
        "gdn_w_out": nrm(ks[7], (nA, W, D), W),
        "gdn_post_norm": gain(ks[8], (nA, D)),
        "kv_norm": gain(ks[9], (D,)),
        "kv_w": nrm(ks[10], (D, 2 * FOX_WIDTH + FOX_HEADS), D),
        "kv_forget_bias": 1.0 + 0.5 * jax.random.normal(ks[11], (FOX_HEADS,), jnp.float32),
        "kv_k_norm": gain(ks[12], (HEAD_DIM,)),
        "fox_pre_norm": gain(ks[13], (nB, D)),
        "fox_w_in": nrm(ks[14], (nB, D, 2 * FOX_WIDTH), D),
        "fox_q_norm": gain(ks[15], (nB, HEAD_DIM)),
        "fox_w_out": nrm(ks[16], (nB, FOX_WIDTH, D), FOX_WIDTH),
        "fox_post_norm": gain(ks[17], (nB, D)),
    }

def second_block(x, gdn_pre_norm, gdn_w_in, gdn_conv_w, gdn_a_log, gdn_dt_bias, gdn_o_norm,
              gdn_w_out, gdn_post_norm, kv_norm, kv_w, kv_forget_bias, kv_k_norm,
              fox_pre_norm, fox_w_in, fox_q_norm, fox_w_out, fox_post_norm):
    h = x
    k_sh = v_sh = c_sh = None
    for layer in range(DEPTH_2):
        if layer < N_A_LAYERS:
            i = layer
            y = gdn_mixer(rms_norm(h, gdn_pre_norm[i]), gdn_w_in[i], gdn_conv_w[i],
                          gdn_a_log[i], gdn_dt_bias[i], gdn_o_norm[i], gdn_w_out[i])
            h = h + rms_norm(y, gdn_post_norm[i])
        else:
            if layer == N_A_LAYERS:
                k_sh, v_sh, c_sh = shared_kv(h, kv_norm, kv_w, kv_forget_bias, kv_k_norm)
            i = layer - N_A_LAYERS
            y = fox_mixer(rms_norm(h, fox_pre_norm[i]), k_sh, v_sh, c_sh,
                          fox_w_in[i], fox_q_norm[i], fox_w_out[i])
            h = h + rms_norm(y, fox_post_norm[i])
    return h


def setup_inputs(seed=0):
    out = dict(first_inputs(seed))
    for name, value in second_inputs(seed + 1).items():
        if name != "x":
            out[name + "_2"] = value
    return out


def reference(
    x, mem, positions, mix_norm_g, w_in, ret_gn_g, pool_w, pool_scale, w_out, xa_norm_g,
    mem_norm_g, xa_wq, xa_wkv, xa_wo, ffn_norm_g, ffn_w_up, ffn_conv_w, ffn_conv_b, ffn_w_down,
    final_norm_g, gdn_pre_norm_2, gdn_w_in_2, gdn_conv_w_2, gdn_a_log_2, gdn_dt_bias_2,
    gdn_o_norm_2, gdn_w_out_2, gdn_post_norm_2, kv_norm_2, kv_w_2, kv_forget_bias_2,
    kv_k_norm_2, fox_pre_norm_2, fox_w_in_2, fox_q_norm_2, fox_w_out_2, fox_post_norm_2,
):
    x = first_block(
        x, mem, positions, mix_norm_g, w_in, ret_gn_g, pool_w, pool_scale, w_out, xa_norm_g,
        mem_norm_g, xa_wq, xa_wkv, xa_wo, ffn_norm_g, ffn_w_up, ffn_conv_w, ffn_conv_b,
        ffn_w_down, final_norm_g,
    )
    return second_block(
        x, gdn_pre_norm_2, gdn_w_in_2, gdn_conv_w_2, gdn_a_log_2, gdn_dt_bias_2, gdn_o_norm_2,
        gdn_w_out_2, gdn_post_norm_2, kv_norm_2, kv_w_2, kv_forget_bias_2, kv_k_norm_2,
        fox_pre_norm_2, fox_w_in_2, fox_q_norm_2, fox_w_out_2, fox_post_norm_2,
    )


_drawn_inputs = setup_inputs


def setup_inputs(seed=0):
    import zlib

    import numpy as np

    out = dict(_drawn_inputs(seed))
    spreads = {}
    factors = {'ret_gn_g': 5.262,
     'xa_norm_g': 8.0,
     'mem_norm_g': 8.0,
     'ffn_norm_g': 3.037,
     'ffn_conv_b': 6.038,
     'kv_k_norm_2': 3.038,
     'fox_q_norm_2': 4.098}
    for name, (base, spread) in spreads.items():
        noise = np.random.default_rng([zlib.crc32(name.encode()), seed]).standard_normal(out[name].shape)
        drawn = base * np.exp(spread * noise) if base else spread * noise
        out[name] = __import__('jax').numpy.asarray(drawn.astype(out[name].dtype))
    for name, factor in factors.items():
        out[name] = (out[name] * factor).astype(out[name].dtype)
    return out
```

```python
import math
from contextlib import ExitStack

import numpy as np

import concourse.bass as bass
from concourse import mybir

F32 = mybir.dt.float32
F32R = mybir.dt.float32r
I32 = mybir.dt.int32
ALU = mybir.AluOpType
ACT = mybir.ActivationFunctionType
AX_X = mybir.AxisListType.X

P = 128
S = 1024
D = 1024
KT = D // P
HALF = 512
NB = S // P
EPS = 1e-6
N_MEM = 256
RET_HEADS, RET_DH = 4, 128
XA_HEADS, XA_DH = 4, 256
POOL_WINDOWS = (2, 4, 8, 16)
PAD = 16
D_FF = 2816
PAIRS = D_FF // P
FF_STEPS = PAIRS // 2
GDN_HEADS, GDN_DK = 8, 128
FOX_HEADS, FOX_D = 8, 128
CONV_K = 4
LEVELS = (2, 4, 8, 16, 32, 64)
MASKED = 1e30

T_RET = 0
T_WOUT = T_RET + 4 * RET_HEADS + len(POOL_WINDOWS)
T_MEM = T_WOUT + KT
T_XQ = T_MEM + 2 * KT
T_XO = T_XQ + KT
T_FF = T_XO + KT
T_GDN = T_FF + 2 * PAIRS + 2 * FF_STEPS
T_GO = T_GDN + 4 * GDN_HEADS
T_FOX = T_GO + KT
T_FO = T_FOX + 4 * FOX_HEADS
T_END = T_FO + KT
EV_RET, EV_MEM = 0, T_WOUT
EV_XQ = EV_MEM + 2 * KT
EV_FF = EV_XQ + KT
EV_GDN = EV_FF + 2 * PAIRS
EV_GO = EV_GDN + 4 * GDN_HEADS
EV_FOX = EV_GO + KT
EV_FO = EV_FOX + 4 * FOX_HEADS

VEC_NAMES = (("mix_g", KT), ("mem_g", KT), ("xa_g", KT), ("ffn_g", KT), ("final_g", KT), ("gdn_g", KT),
             ("gdn_post_g", KT), ("kv_g", KT), ("fox_g", KT), ("fox_post_g", KT), ("gn_g", RET_HEADS),
             ("pool_scale", 4), ("o_g", 1), ("kn_g", 1), ("qn_g", 1), ("ff_b", 2 * PAIRS),
             ("ff_w", 3 * 2 * PAIRS), ("gdn_w", CONV_K * 3 * GDN_HEADS))
VEC_AT, _n = {}, 0
for _name, _width in VEC_NAMES:
    VEC_AT[_name] = _n
    _n += _width
VEC_COLS = _n
CONST_NAMES = (("ident", P), ("triu", P), ("ones", P), ("causal", P), ("future", P),
               ("pair", P), ("pair_t", P), ("levels", P * len(LEVELS)), ("dmat", P * RET_HEADS),
               ("xi", P * RET_HEADS), ("zeta", RET_HEADS), ("inv_freq", 1), ("pool_rcnt", PAD * 4))
CONST_AT, _n = {}, 0
for _name, _width in CONST_NAMES:
    CONST_AT[_name] = _n
    _n += _width
CONST_COLS = _n
N_AB = 2 * GDN_HEADS
N_SMALL = N_AB + FOX_HEADS
LOG_GAMMA = np.log1p(-np.exp2(-5.0 - np.arange(RET_HEADS)))
RET_DECAY = [float(v) for v in np.exp(LOG_GAMMA * P).astype(np.float32)]
TWO_PI_HI, TWO_PI_MID = 6.28125, 1.9340515136718750e-3
TWO_PI_LO = 2 * math.pi - TWO_PI_HI - TWO_PI_MID
ROUND_MAGIC = 1.5 * 2.0 ** 23


def shape_constants():
    i = np.arange(P)
    row, col = i[:, None], i[None, :]
    c = {"ident": row == col, "triu": row <= col, "ones": np.ones((P, P)), "causal": row <= col,
         "future": MASKED * (col > row)}
    pair = (row // 2 == col // 2) & (row % 2 == 1) & (col % 2 == 0)
    c["pair"], c["pair_t"] = pair, pair.T
    c["levels"] = np.concatenate([(row // (2 * b) == col // (2 * b)) & (row // b % 2 == 1) & (col // b % 2 == 0)
                                  for b in LEVELS], 1)
    c["dmat"] = np.concatenate([np.where(col >= row, np.exp(lg * np.maximum(col - row, 0)), 0.0)
                                for lg in LOG_GAMMA], 1)
    c["xi"] = np.concatenate([np.exp(lg * (col + 1.0)) * np.ones((P, 1)) for lg in LOG_GAMMA], 1)
    c["zeta"] = np.exp(LOG_GAMMA[None, :] * (P - 1 - row))
    c["inv_freq"] = np.exp(-math.log(10000.0) * (row % 64) * 2 / 128)
    c["pool_rcnt"] = np.concatenate([1.0 / np.minimum(np.arange(PAD) + 1, w)[None, :] * np.ones((P, 1))
                                     for w in POOL_WINDOWS], 1)
    return np.concatenate([np.asarray(c[n], np.float32) for n, _ in CONST_NAMES], 1)


def build(nc, w_stream, x_t, mem_t, positions, vecs, rows, small_w, pool_w, consts, x_spill, out):
    ctx = ExitStack()
    with ctx:
        def sb(name, shape, dt=F32):
            return ctx.enter_context(nc.sbuf_tensor(name, shape, dt))

        def sem(name):
            return ctx.enter_context(nc.semaphore(name))

        raw = [sb(f"w_raw{i}", [P, KT, P]) for i in range(2)]
        whi = [sb(f"w_hi{i}", [P, KT, P], F32R) for i in range(2)]
        wlo = [sb(f"w_lo{i}", [P, KT, P], F32R) for i in range(2)]
        const = sb("const", [P, CONST_COLS])
        vec = sb("vec", [P, VEC_COLS])
        row = sb("row", [P, N_SMALL])
        poolw = sb("poolw", [P, 4, P])
        small_raw = sb("small_raw", [P, KT, N_SMALL])
        small_hi = sb("small_hi", [P, KT, N_SMALL], F32R)
        small_lo = sb("small_lo", [P, KT, N_SMALL], F32R)
        tiny = sb("tiny", [P, 16, 64])
        stat = sb("stat", [P, 32])
        state = sb("state", [P, P])
        rhs_r = sb("rhs_r", [P, P])
        v_new = sb("v_new", [P, P])
        eps = sb("eps", [P, 1])

        hhi = sb("h_hi", [P, KT, S], F32R)
        hlo = sb("h_lo", [P, KT, S], F32R)
        xres = sb("xres", [P, KT, S])
        H = sb("head", [P, 4, S])
        N = sb("norm", [P, 4, S])
        with nc.sbuf_tensor("yt", [P, KT, S], F32) as yt:
            pass
        with nc.sbuf_tensor("memx", [P, KT, N_MEM], F32) as memx, \
                nc.sbuf_tensor("mem_hi", [P, KT, N_MEM], F32R) as mem_hi, \
                nc.sbuf_tensor("mem_lo", [P, KT, N_MEM], F32R) as mem_lo:
            pass
        with nc.sbuf_tensor("act_hi", [P, 4, S], F32R) as act_hi, \
                nc.sbuf_tensor("act_lo", [P, 4, S], F32R) as act_lo:
            pass
        X = xres[:, :, :].rearrange("p k s -> p (k s)")
        Nf = N[:, :, :].rearrange("p k s -> p (k s)")

        def X4(i):
            return X[:, i * S:(i + 1) * S]

        GP0, GP1 = X[:, 0:S + 3], X[:, S + 3:2 * (S + 3)]
        G0 = 2 * (S + 3)
        AT, MT, TI, TT, XB = [X[:, G0 + i * S:G0 + (i + 1) * S] for i in range(5)]

        FP = S + 2

        gp = [ctx.enter_context(nc.psum_tensor(f"gemm{i}", [P, S], F32)) for i in range(2)]
        ps = [ctx.enter_context(nc.psum_tensor(f"small{i}", [P, S], F32)) for i in range(2)]
        pa, pb = ps[0][:, :], ps[1][:, :]

        def cn(name, i=0, width=P):
            at = CONST_AT[name] + i * width
            return const[:, at:at + width]

        def vc(name, i):
            return vec[:, VEC_AT[name] + i:VEC_AT[name] + i + 1]

        def chunks(ap):
            return ap.rearrange("p (n c) -> p n c", c=P)

        def ck(ap, n):
            return ap[:, n * P:(n + 1) * P]

        def over(ap, n):
            return ap.rearrange("p (a c) -> p a c", a=1).broadcast_to([P, n, P])

        ident, ones, triu = cn("ident"), cn("ones"), cn("triu")

        w_loaded = [sem(f"w_loaded{i}") for i in range(2)]
        const_loaded = sem("const_loaded")
        x_loaded = [sem(f"x_loaded{k}") for k in range(KT)]
        mem_loaded, pos_loaded = sem("mem_loaded"), sem("pos_loaded")
        spilled, stored = sem("spilled"), sem("stored")
        w_gained, w_hi_done, w_split = sem("w_gained"), sem("w_hi_done"), sem("w_split")
        small_step, small_split = sem("small_step"), sem("small_split")
        eps_set = sem("eps_set")
        pe_slot = sem("pe_slot")
        ev_act, ev_dve = sem("ev_act"), sem("ev_dve")
        sq_ready, sq_added = sem("sq_ready"), sem("sq_added")
        norm_mm, norm_root, norm_scaled = sem("norm_mm"), sem("norm_root"), sem("norm_scaled")
        h_hi_done, h_lo_done = sem("h_hi_done"), sem("h_lo_done")
        act_step, dve_step = sem("act_step"), sem("dve_step")
        angles, rope_tab = sem("angles"), sem("rope_tab")
        roped = sem("roped")
        ret_turned, ret_kz, ret_v = sem("ret_turned"), sem("ret_kz"), sem("ret_v")
        ret_scores, ret_probs = sem("ret_scores"), sem("ret_probs")
        ret_kv, ret_states, ret_out = sem("ret_kv"), sem("ret_states"), sem("ret_out")
        y_squared, y_sums, y_root, y_done = sem("y_squared"), sem("y_sums"), sem("y_root"), sem("y_done")
        pads_zero, pool_in, pool_mm, pool_y = sem("pads_zero"), sem("pool_in"), sem("pool_mm"), sem("pool_y")
        mem_turned, mem_v = sem("mem_turned"), sem("mem_v")
        xa_scores, xa_max, xa_exp, xa_probs = sem("xa_scores"), sem("xa_max"), sem("xa_exp"), sem("xa_probs")
        xa_turned, xa_pt, xa_out, xa_y = sem("xa_turned"), sem("xa_pt"), sem("xa_out"), sem("xa_y")
        ff_taps, ff_conv, ff_gate, ff_prod = sem("ff_taps"), sem("ff_conv"), sem("ff_gate"), sem("ff_prod")
        act_hi_done, act_lo_done = sem("act_hi_done"), sem("act_lo_done")
        down_mm, down_ev = sem("down_mm"), sem("down_ev")
        ab_mm, ab_out, ab_e, ab_ready = sem("ab_mm"), sem("ab_out"), sem("ab_e"), sem("ab_ready")
        gc_mm, gc_out, gc_diff, gc_ready = sem("gc_mm"), sem("gc_out"), sem("gc_diff"), sem("gc_ready")
        gd_conv, gd_silu, gd_sq, gd_ss, gd_root = (sem("gd_conv"), sem("gd_silu"), sem("gd_sq"), sem("gd_ss"),
                                                   sem("gd_root"))
        gd_qk = sem("gd_qk")
        gd_gr, gd_diff, gd_exp, gd_br, gd_mt1 = sem("gd_gr"), sem("gd_diff"), sem("gd_exp"), sem("gd_br"), sem("gd_mt1")
        gd_kk, gd_mt, gd_attn_mm, gd_attn = sem("gd_kk"), sem("gd_mt"), sem("gd_attn_mm"), sem("gd_attn")
        gd_kturn, gd_kdec, gd_vturn, gd_vb = sem("gd_kturn"), sem("gd_kdec"), sem("gd_vturn"), sem("gd_vb")
        gd_mturn, gd_t0 = sem("gd_mturn"), sem("gd_t0")
        inv_x_mm, inv_x, inv_y_mm, inv_t = sem("inv_x_mm"), sem("inv_x"), sem("inv_y_mm"), sem("inv_t")
        ch_ks, ch_r, ch_vn_mm, ch_vn, ch_s_mm, ch_s = (sem("ch_ks"), sem("ch_r"), sem("ch_vn_mm"), sem("ch_vn"),
                                                       sem("ch_s_mm"), sem("ch_s"))
        f_mm, f_out, f_e, f_ready = sem("f_mm"), sem("f_out"), sem("f_e"), sem("f_ready")
        fx_sq, fx_ss, fx_root, fx_qk = sem("fx_sq"), sem("fx_ss"), sem("fx_root"), sem("fx_qk")
        fx_vturn, fx_v, fx_c_mm, fx_c = sem("fx_vturn"), sem("fx_v"), sem("fx_c_mm"), sem("fx_c")
        fx_s_mm, fx_s, fx_exp, fx_p = sem("fx_s_mm"), sem("fx_s"), sem("fx_exp"), sem("fx_p")
        fx_turn, fx_pt, fx_o = sem("fx_turn"), sem("fx_pt"), sem("fx_o")
        out_ready = sem("out_ready")
        RET, GDN, FOX = RET_HEADS, GDN_HEADS, FOX_HEADS
        NMIX, NMEM, NXA, NFF, NFIN, NGDN, NGP, NFOX, NFP = range(9)
        HMIX, HRET, HMEM, HXA, HXO, HFF, HGDN, HGO, HFOX, HFO = range(10)
        Y_GDN, Y_FOX = RET, RET + GDN

        block = ctx.enter_context(nc.Block())

        @block.sync
        def _(sp):
            for t in range(2):
                sp.dma_start(raw[t][:, :, :], w_stream[t]).then_inc(w_loaded[t], 16)
                if t == 0:
                    for k in range(KT):
                        sp.dma_start(xres[:, k, :], x_t[k]).then_inc(x_loaded[k], 16)
            with sp.Fori(1, T_END // 2) as i:
                for t in range(2):
                    sp.wait_ge(w_split, 2 * i + t - 1)
                    sp.dma_start(raw[t][:, :, :], w_stream[2 * i + t]).then_inc(w_loaded[t], 16)

        @block.gpsimd
        def _(pool):
            for dst, src in ((const[:, :], consts), (vec[:, :], vecs), (row[:, :], rows.broadcast_to([P, N_SMALL])),
                             (small_raw[:, :, :], small_w), (poolw[:, :, :], pool_w)):
                pool.dma_start(dst, src).then_inc(const_loaded, 16)
            pool.dma_start(H[:, 3, :].bitcast(I32), positions.broadcast_to([P, S])).then_inc(pos_loaded, 16)
            nc.gpsimd.memset(eps[:, :], EPS).then_inc(eps_set, 1)

            pool.wait_ge(const_loaded, 80)
            fcols = small_raw[:, :, N_AB:N_SMALL]
            gain = vec[:, VEC_AT["kv_g"]:VEC_AT["kv_g"] + KT].rearrange("p (k a) -> p k a", a=1)
            nc.gpsimd.tensor_tensor(fcols, fcols, gain.broadcast_to([P, KT, FOX]), ALU.mult).then_inc(small_step, 1)
            pool.wait_ge(small_step, 1)
            nc.gpsimd.tensor_copy(small_hi[:, :, :], small_raw[:, :, :]).then_inc(small_step, 1)
            pool.wait_ge(small_step, 2)
            nc.gpsimd.tensor_tensor(small_lo[:, :, :], small_raw[:, :, :], small_hi[:, :, :].bitcast(F32),
                                    ALU.subtract).then_inc(small_split, 1)

            unit = ones[:, 0:1].rearrange("p (a b) -> p a b", a=1).broadcast_to([P, KT, P])

            def split_slot(t, s, turn):
                pool.wait_ge(w_loaded[s], 16 * turn)
                nc.gpsimd.tensor_tensor(whi[s][:, :, :], raw[s][:, :, :], unit, ALU.mult).then_inc(w_hi_done, 1)
                pool.wait_ge(w_hi_done, t + 1)
                nc.gpsimd.tensor_tensor(wlo[s][:, :, :], raw[s][:, :, :], whi[s][:, :, :].bitcast(F32),
                                        ALU.subtract).then_inc(w_split, 1)

            for s in range(2):
                split_slot(s, s, 1)
            with pool.Fori(1, T_FOX // 2) as i:
                for s in range(2):
                    pool.wait_ge(pe_slot, 2 * i + s - 1)
                    split_slot(2 * i + s, s, i + 1)
            with pool.Fori(0, FOX) as i:
                for j in range(4):
                    t, s, name = T_FOX + j, j % 2, ("kv_g", "kv_g", "fox_g", "fox_g")[j]
                    gain = vec[:, VEC_AT[name]:VEC_AT[name] + KT].rearrange("p (k a) -> p k a", a=1)
                    pool.wait_ge(w_loaded[s], 32 * i + 16 * (t // 2 + 1))
                    nc.gpsimd.tensor_tensor(raw[s][:, :, :], raw[s][:, :, :], gain.broadcast_to([P, KT, P]),
                                            ALU.mult).then_inc(w_gained, 1)
                    pool.wait_ge(w_gained, 4 * i + (j + 1))
                    pool.wait_ge(pe_slot, 4 * i + (t - 1))
                    nc.gpsimd.tensor_tensor(whi[s][:, :, :], raw[s][:, :, :], unit, ALU.mult).then_inc(w_hi_done, 1)
                    pool.wait_ge(w_hi_done, 4 * i + (t + 1))
                    nc.gpsimd.tensor_tensor(wlo[s][:, :, :], raw[s][:, :, :], whi[s][:, :, :].bitcast(F32),
                                            ALU.subtract).then_inc(w_split, 1)
            with pool.Fori(T_FO // 2, T_END // 2) as i:
                for s in range(2):
                    pool.wait_ge(pe_slot, 2 * i + s - 1)
                    split_slot(2 * i + s, s, i + 1)

        @block.tensor
        def _(pe):
            mm = nc.tensor.matmul

            def dot3(dst, w_hi, w_lo, a_hi, a_lo, first, last):
                mm(dst, w_hi, a_hi, start=first, stop=False)
                mm(dst, w_hi, a_lo, start=False, stop=False)
                return mm(dst, w_lo, a_hi, start=False, stop=last)

            def gemm_tile(t, b, a_hi, a_lo, width, fresh=None):
                pe.wait_ge(w_split, t + 1)
                for k in range(KT):
                    if fresh is not None:
                        pe.wait_ge(h_lo_done, KT * fresh + k + 1)
                    for c in range(0, width, HALF):
                        w = min(HALF, width)
                        last = dot3(gp[b][:, c:c + w], whi[b][:, k, :], wlo[b][:, k, :],
                                    a_hi[:, k, c:c + w], a_lo[:, k, c:c + w], k == 0, k == KT - 1)
                last.then_inc(pe_slot, 1)

            def norm_sum(j, width=S):
                pe.wait_ge(sq_added, KT * (j + 1))
                src = N[:, 2, :] if j != NMEM else H[:, 1, 0:N_MEM]
                for c in range(2):
                    w = width // 2
                    last = mm(pa[:, c * w:c * w + w], ones, src[:, c * w:c * w + w], start=True, stop=True)
                last.then_inc(norm_mm, 1)

            def sums(dst, src, done):
                for c in range(2):
                    last = mm(dst[:, c * HALF:(c + 1) * HALF], ones, src[:, c * HALF:(c + 1) * HALF],
                              start=True, stop=True)
                last.then_inc(done, 1)

            def turn8(dst, src, done):
                for n in range(NB):
                    last = nc.tensor.transpose(ck(dst, n), ck(src, n), ident)
                last.then_inc(done, 1)

            pe.wait_ge(const_loaded, 80)
            norm_sum(NMIX)
            for h in range(RET):
                for j in range(4):
                    t = T_RET + 4 * h + j
                    if t >= 2:
                        pe.wait_ge(ev_act, t - 1)
                    gemm_tile(t, t % 2, hhi, hlo, S, HMIX if t == 0 else None)
                pe.wait_ge(roped, 2 * h + 2)
                if h == 0:
                    pe.wait_ge(norm_root, 1)
                else:
                    pe.wait_ge(y_root, h)
                turn8(pa, H[:, 1, :], ret_turned)
                pe.wait_ge(ev_act, 4 * h + 3)
                turn8(pb, H[:, 2, :], ret_turned)
                pe.wait_ge(ret_kz, h + 1)
                for n in range(NB):
                    last = mm(ck(pa, n), ck(H[:, 1, :], n), ck(H[:, 0, :], n), start=True, stop=True)
                last.then_inc(ret_scores, 1)
                pe.wait_ge(ret_v, h + 1)
                for n in range(NB - 1):
                    last = mm(ck(pb, n), ck(X4(5), n), ck(X4(0), n), start=True, stop=True)
                last.then_inc(ret_kv, 1)
                pe.wait_ge(ret_probs, h + 1)
                pe.wait_ge(ret_states, h + 1)
                for n in range(NB):
                    last = mm(ck(pa, n), ck(X4(0), n), ck(X4(1), n), start=True, stop=(n == 0))
                    if n:
                        last = mm(ck(pa, n), ck(X4(2), n), ck(X4(4), n), start=False, stop=True)
                last.then_inc(ret_out, 1)
                pe.wait_ge(y_squared, h + 1)
                sums(pb, X4(3), y_sums)
            for g in range(4):
                t = T_RET + 4 * RET + g
                pe.wait_ge(ev_act, t - 1)
                gemm_tile(t, t % 2, hhi, hlo, S)
                pe.wait_ge(pool_in, g + 1)
                if g:
                    pe.wait_ge(pool_y, g)
                for c in range(2):
                    last = mm(pa[:, c * HALF:(c + 1) * HALF], poolw[:, g, :],
                              X[:, 3 * (PAD + S) + c * HALF:3 * (PAD + S) + (c + 1) * HALF], start=True, stop=True)
                last.then_inc(pool_mm, 1)
            pe.wait_ge(ev_act, T_WOUT)
            for m in range(KT):
                t = T_WOUT + m
                if m >= 2:
                    pe.wait_ge(ev_dve, m - 1)
                gemm_tile(t, t % 2, hhi, hlo, S, HRET if m == 0 else None)
                if m == 0:
                    norm_sum(NMEM, N_MEM)
            pe.wait_ge(ev_dve, KT)
            pe.wait_ge(norm_root, 2)
            norm_sum(NXA)
            pe.wait_ge(h_lo_done, KT * (HMEM + 1))
            for m in range(2 * KT):
                t = T_MEM + m
                if m >= 2:
                    pe.wait_ge(ev_act, EV_MEM + m - 1)
                gemm_tile(t, t % 2, mem_hi, mem_lo, N_MEM)
            pe.wait_ge(ev_act, EV_MEM + 2 * KT)
            for b in range(2):
                for k in range(KT):
                    last = nc.tensor.transpose(ck(ps[b][:, :], k),
                                               H[:, 2:4, :].rearrange("p a (k m) -> p (a k) m", m=N_MEM)[:, k, b * P:(b + 1) * P],
                                               ident)
                last.then_inc(mem_turned, 1)
            for h in range(XA_HEADS):
                for j in range(2):
                    t = T_XQ + 2 * h + j
                    pe.wait_ge(ev_act, EV_XQ + 2 * h + j - 1)
                    gemm_tile(t, t % 2, hhi, hlo, S, HXA if h == j == 0 else None)
                pe.wait_ge(mem_v, 2)
                pe.wait_ge(ev_act, EV_XQ + 2 * h + 2)
                for f in range(2):
                    u = 2 * h + f
                    if u:
                        pe.wait_ge(xa_y, u)
                    for q in range(4):
                        for j in range(2):
                            last = mm(pa[:, q * N_MEM:(q + 1) * N_MEM], ck(H[:, j, :], 4 * f + q),
                                      Nf[:, (2 * h + j) * N_MEM:(2 * h + j + 1) * N_MEM], start=(j == 0), stop=(j == 1))
                    last.then_inc(xa_scores, 1)
                    pe.wait_ge(xa_probs, u + 1)
                    for b in range(2):
                        for q in range(4):
                            last = nc.tensor.transpose(pb[:, b * HALF + q * P:b * HALF + (q + 1) * P],
                                                       H[:, 2, q * N_MEM + b * P:q * N_MEM + (b + 1) * P], ident)
                    last.then_inc(xa_turned, 1)
                    pe.wait_ge(xa_pt, u + 1)
                    for d in range(2):
                        for b in range(2):
                            at = 2 * S + b * D + h * XA_DH + d * P
                            last = mm(pa[:, d * HALF:(d + 1) * HALF], Nf[:, at:at + P], H[:, 3, b * HALF:(b + 1) * HALF],
                                      start=(b == 0), stop=(b == 1))
                    last.then_inc(xa_out, 1)
            pe.wait_ge(ev_act, EV_XQ + KT)
            for m in range(KT):
                t = T_XO + m
                if m >= 2:
                    pe.wait_ge(ev_dve, KT + m - 1)
                gemm_tile(t, t % 2, hhi, hlo, S, HXO if m == 0 else None)
            pe.wait_ge(xa_y, 8)
            norm_sum(NFF)
            def up_at(i):
                for q in range(4):
                    pe.wait_ge(ev_act, 4 * i + (EV_FF + q - 1))
                    gemm_tile(6 * i + (T_FF - 2 + q), q % 2, hhi, hlo, S)

            def down_at(i, b, t0):
                for a in range(2):
                    t = t0 + a
                    pe.wait_ge(w_split, t + 1)
                    for q in range(4):
                        m = 4 * a + q
                        if a == q == 0:
                            pe.wait_ge(act_lo_done, 2 * i + 2)
                        if not (isinstance(i, int) and 8 * i + m < 2):
                            pe.wait_ge(down_ev, 8 * i + (m - 1))
                        for k in range(2):
                            for c in range(2):
                                last = dot3(ps[m % 2][:, c * HALF:(c + 1) * HALF], whi[a][:, 2 * q + k, :], wlo[a][:, 2 * q + k, :],
                                            act_hi[:, 2 * b + k, c * HALF:(c + 1) * HALF],
                                            act_lo[:, 2 * b + k, c * HALF:(c + 1) * HALF], k == 0, k == 1)
                        last.then_inc(pe_slot if q == 3 else down_mm, 1)

            pe.wait_ge(ev_dve, 2 * KT)
            for q in range(4):
                if q >= 2:
                    pe.wait_ge(ev_act, EV_FF + q - 1)
                gemm_tile(T_FF + q, q % 2, hhi, hlo, S, HFF if q == 0 else None)
            pe.wait_ge(norm_root, NFF + 1)
            up_at(1)
            down_at(0, 0, T_FF + 8)
            up_at(2)
            down_at(1, 1, T_FF + 14)
            with pe.Fori(1, FF_STEPS // 2) as r:
                for b in range(2):
                    up_at(2 * r + b + 1)
                    down_at(2 * r + b, b, 12 * r + (6 * b + T_FF + 8))
            down_at(FF_STEPS - 1, (FF_STEPS - 1) % 2, T_GDN - 2)
            pe.wait_ge(down_ev, 8 * FF_STEPS)
            norm_sum(NFIN)
            pe.wait_ge(norm_root, NFIN + 1)
            norm_sum(NGDN)
            pe.wait_ge(norm_root, NGDN + 1)

            def narrow(c0, c1, fresh, done):
                pe.wait_ge(small_split, 1)
                pe.wait_ge(h_lo_done, KT * (fresh + 1))
                w = c1 - c0
                for n in range(NB):
                    for k in range(KT):
                        last = dot3(pa[:, n * w:(n + 1) * w], hhi[:, k, n * P:(n + 1) * P], hlo[:, k, n * P:(n + 1) * P],
                                    small_hi[:, k, c0:c1], small_lo[:, k, c0:c1], k == 0, k == KT - 1)
                last.then_inc(done, 1)

            narrow(0, N_AB, HGDN, ab_mm)
            pe.wait_ge(ab_ready, 1)
            mm(pb[:, 0:64], triu, tiny[:, 5, :], start=True, stop=True)
            mm(pb[:, 64:128], ones, tiny[:, 5, :], start=True, stop=True).then_inc(gc_mm, 1)

            for h in range(GDN):
                for j in range(4):
                    t = T_GDN + 4 * h + j
                    pe.wait_ge(ev_act, EV_GDN + 4 * h + j - 1)
                    gemm_tile(t, t % 2, hhi, hlo, S)
                if h == 0:
                    pe.wait_ge(gc_ready, 1)
                else:
                    pe.wait_ge(y_done, Y_GDN + h)
                pe.wait_ge(gd_sq, 2 * h + 1)
                sums(pa, N[:, 0, :], gd_ss)
                pe.wait_ge(gd_sq, 2 * h + 2)
                sums(pb, N[:, 1, :], gd_ss)
                pe.wait_ge(gd_root, 2 * h + 1)
                for n in range(NB):
                    col = n * GDN + h
                    last = mm(ck(pa, n), tiny[:, 5, col:col + 1].broadcast_to([P, P]), triu, start=True, stop=True)
                last.then_inc(gd_gr, 1)
                pe.wait_ge(gd_root, 2 * h + 2)
                for n in range(NB):
                    col = n * GDN + h
                    last = mm(ck(pb, n), tiny[:, 6, col:col + 1].broadcast_to([P, P]), ident, start=True, stop=True)
                last.then_inc(gd_br, 1)
                pe.wait_ge(gd_qk, 2 * h + 2)
                pe.wait_ge(gd_exp, 2 * h + 2)
                for n in range(NB):
                    last = mm(ck(pa, n), ck(H[:, 1, :], n), ck(H[:, 1, :], n), start=True, stop=True)
                last.then_inc(gd_kk, 1)
                pe.wait_ge(gd_mt1, h + 1)
                for n in range(NB):
                    last = mm(ck(pb, n), ck(H[:, 1, :], n), ck(H[:, 0, :], n), start=True, stop=True)
                last.then_inc(gd_attn_mm, 1)
                pe.wait_ge(gd_mt, h + 1)
                turn8(pa, H[:, 1, :], gd_kturn)
                pe.wait_ge(gd_silu, 3 * h + 3)
                pe.wait_ge(gd_attn, h + 1)
                turn8(pb, H[:, 2, :], gd_vturn)
                pe.wait_ge(gd_kdec, h + 1)
                turn8(pa, MT, gd_mturn)
                pe.wait_ge(gd_vb, h + 1)
                def prod(dst, half, left, right, done):
                    for n in range(4 * half, 4 * half + 4):
                        last = mm(dst[:, (n % 4) * P:(n % 4 + 1) * P], ck(left, n), ck(right, n), start=True, stop=True)
                    last.then_inc(done, 1)

                for l in range(len(LEVELS)):
                    for f in range(2):
                        if l == 0:
                            pe.wait_ge(gd_t0, h + 1)
                        else:
                            pe.wait_ge(inv_t, 4 * len(LEVELS) * h + 4 * (l - 1) + 2 * f + 2)
                        prod(ps[f][:, 0:HALF], f, MT, TI, inv_x_mm)
                    for f in range(2):
                        pe.wait_ge(inv_x, 2 * len(LEVELS) * h + 2 * l + f + 1)
                        prod(ps[f][:, 0:HALF], f, TT, XB, inv_y_mm)
                        prod(ps[f][:, HALF:S], f, XB, TT, inv_y_mm)
                pe.wait_ge(inv_t, 4 * len(LEVELS) * (h + 1))
                for n in range(NB):
                    u = NB * h + n
                    if n:
                        pe.wait_ge(ch_s, u)
                        mm(pa[:, 0:P], ck(H[:, 1, :], n), state[:, :], start=True, stop=True).then_inc(ch_ks, 1)
                    pe.wait_ge(ch_r, u + 1)
                    mm(pa[:, HALF:HALF + P], ck(TT, n), rhs_r[:, :], start=True, stop=True).then_inc(ch_vn_mm, 1)
                    if n:
                        mm(ck(pb, n), state[:, :], ck(N[:, 1, :], n), start=True, stop=False)
                    pe.wait_ge(ch_vn, u + 1)
                    mm(ck(pb, n), v_new[:, :], ck(AT, n), start=(n == 0), stop=True)
                    mm(pa[:, P:2 * P], ck(N[:, 2, :], n), v_new[:, :], start=True, stop=True).then_inc(ch_s_mm, 1)
                pe.wait_ge(y_squared, Y_GDN + h + 1)
                pe.wait_ge(ch_s, NB * (h + 1))
                sums(pa, N[:, 0, :], y_sums)
            pe.wait_ge(ev_act, EV_GO)
            for m in range(KT):
                t = T_GO + m
                if m >= 2:
                    pe.wait_ge(ev_act, EV_GO + m - 1)
                gemm_tile(t, t % 2, hhi, hlo, S, HGO if m == 0 else None)
            pe.wait_ge(y_root, Y_GDN + GDN)
            norm_sum(NGP)
            pe.wait_ge(norm_root, NGP + 1)
            norm_sum(NFOX)
            pe.wait_ge(norm_root, NFOX + 1)

            narrow(N_AB, N_SMALL, HFOX, f_mm)
            pe.wait_ge(f_ready, 1)
            for h in range(FOX):
                for j in range(4):
                    t = T_FOX + 4 * h + j
                    pe.wait_ge(ev_act, EV_FOX + 4 * h + j - 1)
                    if h and j == 0:
                        pe.wait_ge(y_done, Y_FOX + h)
                        pe.wait_ge(fx_pt, NB * h)
                    gemm_tile(t, t % 2, hhi, hlo, S)
                pe.wait_ge(ev_act, EV_FOX + 4 * h + 4)
                pe.wait_ge(fx_sq, 2 * h + 1)
                sums(pa, N[:, 0, :], fx_ss)
                pe.wait_ge(fx_sq, 2 * h + 2)
                sums(pb, N[:, 1, :], fx_ss)
                pe.wait_ge(fx_root, 2 * h + 1)
                turn8(pa, H[:, 1, :], fx_vturn)
                pe.wait_ge(fx_root, 2 * h + 2)
                for n in range(NB):
                    col = n * FOX + h
                    last = mm(ck(pb, n), tiny[:, 11, col:col + 1].broadcast_to([P, P]), triu, start=True, stop=True)
                last.then_inc(fx_c_mm, 1)
                pe.wait_ge(fx_qk, 2 * h + 2)
                pe.wait_ge(fx_c, h + 1)
                pe.wait_ge(fx_v, h + 1)

                def scores(q):
                    u = NB * h + q
                    if q >= 2:
                        pe.wait_ge(fx_s, u - 1)
                    for c in range(0, (q + 1) * P, HALF):
                        w = min(HALF, (q + 1) * P - c)
                        last = mm(ps[q % 2][:, c:c + w], ck(H[:, 2, :], q), H[:, 0, c:c + w], start=True, stop=True)
                    last.then_inc(fx_s_mm, 1)

                scores(0)
                for q in range(NB):
                    u = NB * h + q
                    if q + 1 < NB:
                        scores(q + 1)
                    pe.wait_ge(fx_p, u + 1)
                    if q:
                        pe.wait_ge(fx_pt, u)
                    for b in range(q + 1):
                        last = nc.tensor.transpose(ck(gp[0][:, :], b), X4(3 + q % 2)[:, b * P:(b + 1) * P], ident)
                    last.then_inc(fx_turn, 1)
                    pe.wait_ge(fx_pt, u + 1)
                    for b in range(q + 1):
                        last = mm(ck(gp[1][:, :], q), ck(X4(0), b), ck(X4(5), b), start=(b == 0), stop=(b == q))
                    last.then_inc(fx_o, 1)
            pe.wait_ge(y_done, Y_FOX + FOX)
            for m in range(KT):
                t = T_FO + m
                if m >= 2:
                    pe.wait_ge(ev_act, EV_FO + m - 1)
                gemm_tile(t, t % 2, hhi, hlo, S, HFO if m == 0 else None)
            norm_sum(NFP)

        @block.scalar
        def _(act):
            A = nc.scalar.activation
            steps = [0]

            def done(ins):
                steps[0] += 1
                ins.then_inc(act_step, 1)

            def settle():
                act.wait_ge(act_step, steps[0])

            def square(j, k, src):
                n = KT * j + k
                if n >= 2:
                    act.wait_ge(sq_added, n - 1)
                dst = N[:, k % 2, :] if j != NMEM else H[:, 0, (k % 2) * N_MEM:(k % 2 + 1) * N_MEM]
                A(dst, src, ACT.Square).then_inc(sq_ready, 1)

            def root(j, width=S):
                act.wait_ge(norm_mm, j + 1)
                dst = N[:, 3, :] if j != NMEM else H[:, 1, N_MEM:2 * N_MEM]
                A(dst, pa[:, 0:width], ACT.Sqrt, bias=eps[:, 0:1], scale=1.0 / D).then_inc(norm_root, 1)

            def hi_parts(p, srcs, dst, waits=None, free=None):
                for k in range(KT):
                    if k == 0 and free is not None:
                        act.wait_ge(pe_slot, free)
                    if waits is not None:
                        act.wait_ge(waits[0], waits[1] + k)
                    A(dst[:, k, :], srcs(k), ACT.Copy).then_inc(h_hi_done, 1)

            def evac(t, ev, dst, b, func=ACT.Copy, width=S):
                act.wait_ge(pe_slot, t + 1)
                A(dst, gp[b][:, 0:width], func).then_inc(ev_act, 1)

            def nt(k):
                return N[:, k % 2, :]

            act.wait_ge(eps_set, 1)
            act.wait_ge(const_loaded, 80)
            for k in range(KT):
                act.wait_ge(x_loaded[k], 16)
                square(NMIX, k, xres[:, k, :])
            root(NMIX)
            hi_parts(HMIX, nt, hhi, (norm_scaled, 1))
            act.wait_ge(angles, 1)
            A(X4(6)[0:64, :], X4(6)[0:64, :], ACT.Sin, scale=-1.0)
            A(X4(6)[64:P, :], X4(6)[64:P, :], ACT.Sin)
            A(X4(7), X4(7), ACT.Sin).then_inc(rope_tab, 1)
            for h in range(RET):
                for j in range(4):
                    t = T_RET + 4 * h + j
                    if j == 0 and h:
                        act.wait_ge(y_done, h)
                    if j < 2:
                        act.wait_ge(pe_slot, t + 1)
                        A(H[:, j, :], gp[t % 2][:, :], ACT.Copy)
                        A(X4(j)[0:64, :], gp[t % 2][64:P, :], ACT.Copy)
                        A(X4(j)[64:P, :], gp[t % 2][0:64, :], ACT.Copy).then_inc(ev_act, 1)
                    else:
                        evac(t, t, H[:, j, :], t % 2, ACT.Copy if j == 2 else ACT.Silu)
                act.wait_ge(ret_turned, 2 * h + 1)
                A(X4(5), pa, ACT.Copy, scale=cn("zeta", h, 1)).then_inc(ret_kz, 1)
                act.wait_ge(ret_out, h + 1)
                done(A(X4(5), pa, ACT.Copy))
                settle()
                A(X4(3), X4(5), ACT.Square).then_inc(y_squared, 1)
                act.wait_ge(y_sums, h + 1)
                A(N[:, 2, :], pb, ACT.Sqrt, bias=eps[:, 0:1], scale=1.0 / RET_DH).then_inc(y_root, 1)
            for g in range(4):
                t = T_RET + 4 * RET + g
                act.wait_ge(pads_zero, 1)
                if g:
                    act.wait_ge(pool_in, g)
                evac(t, t, X[:, PAD:PAD + S], t % 2)
                act.wait_ge(pool_mm, g + 1)
                A(yt[:, 4 + g, :], pa, ACT.Copy, scale=vc("pool_scale", g)).then_inc(pool_y, 1)
            act.wait_ge(y_done, RET)
            act.wait_ge(pool_y, 4)
            hi_parts(HRET, lambda k: yt[:, k, :], hhi, None, T_WOUT)
            act.wait_ge(h_lo_done, KT * (HRET + 1))
            act.dma_start(memx[:, :, :], mem_t).then_inc(mem_loaded, 16)
            for k in range(KT):
                act.dma_start(xres[:, k, :], x_t[k]).then_inc(x_loaded[k], 16)
            act.wait_ge(mem_loaded, 16)
            for k in range(KT):
                square(NMEM, k, memx[:, k, :])
            root(NMEM, N_MEM)
            hi_parts(HMEM, lambda k: H[:, 0, (k % 2) * N_MEM:(k % 2 + 1) * N_MEM], mem_hi, (norm_scaled, KT + 1))
            for m in range(KT):
                act.wait_ge(ev_dve, m + 1)
                square(NXA, m, xres[:, m, :])
            root(NXA)
            hi_parts(HXA, nt, hhi, (norm_scaled, 2 * KT + 1), T_MEM)
            act.wait_ge(h_lo_done, KT * (HXA + 1))
            for m in range(2 * KT):
                dst = Nf[:, m * N_MEM:(m + 1) * N_MEM] if m < KT else \
                    H[:, 2:4, :].rearrange("p a (k m) -> p (a k) m", m=N_MEM)[:, m - KT, :]
                evac(T_MEM + m, 0, dst, m % 2, ACT.Copy, N_MEM)
            for b in range(2):
                act.wait_ge(mem_turned, b + 1)
                A(N[:, 2 + b, :], ps[b][:, :], ACT.Copy).then_inc(mem_v, 1)
            for h in range(XA_HEADS):
                for j in range(2):
                    if h:
                        act.wait_ge(xa_scores, 2 * h)
                    evac(T_XQ + 2 * h + j, 0, H[:, j, :], j)
                for f in range(2):
                    u = 2 * h + f
                    act.wait_ge(xa_max, u + 1)
                    if u:
                        act.wait_ge(xa_turned, u)
                    else:
                        act.wait_ge(mem_turned, 2)
                    for q in range(4):
                        last = A(H[:, 2, q * N_MEM:(q + 1) * N_MEM], pa[:, q * N_MEM:(q + 1) * N_MEM], ACT.Exp,
                                 bias=stat[:, 4 + q:5 + q], scale=XA_DH ** -0.5, accum_out=stat[:, 8 + q:9 + q])
                    last.then_inc(xa_exp, 1)
                    act.wait_ge(xa_turned, u + 1)
                    A(H[:, 3, :], pb, ACT.Copy).then_inc(xa_pt, 1)
                    act.wait_ge(xa_out, u + 1)
                    for d in range(2):
                        last = A(yt[:, 2 * h + d, f * HALF:(f + 1) * HALF], pa[:, d * HALF:(d + 1) * HALF], ACT.Copy)
                    last.then_inc(xa_y, 1)
            act.wait_ge(xa_y, 8)
            hi_parts(HXO, lambda k: yt[:, k, :], hhi, None, T_XO)
            for m in range(KT):
                act.wait_ge(ev_dve, KT + m + 1)
                square(NFF, m, xres[:, m, :])
            root(NFF)
            hi_parts(HFF, nt, hhi, (norm_scaled, 3 * KT + 1), T_FF)
            act.wait_ge(h_lo_done, KT * (HFF + 1))
            act.wait_ge(pads_zero, 2)

            def up(i, b, t0, first):
                for j in range(2):
                    for v in range(2):
                        q = 2 * j + v
                        act.wait_ge(pe_slot, t0 + (q + 1))
                        if not (first and j == 0):
                            act.wait_ge(ff_conv, 4 * i + (q - 1))
                        A(Nf[:, v * FP + 2:v * FP + 2 + S], gp[v][:, :], ACT.Copy).then_inc(ev_act, 1)
                    act.wait_ge(ff_conv, 4 * i + (2 * j + 1))
                    A(H[:, 2 * j, :], H[:, 2 * j, :], ACT.Silu).then_inc(ff_gate, 1)
                    if j == 0 and not (isinstance(i, int) and i < 2):
                        act.wait_ge(pe_slot, 6 * i + (T_FF - 2))
                    act.wait_ge(ff_prod, 2 * i + (j + 1))
                    A(act_hi[:, 2 * b + j, :], H[:, 2 * j, :], ACT.Copy).then_inc(act_hi_done, 1)

            up(0, 0, T_FF, True)
            up(1, 1, T_FF + 4, False)
            with act.Fori(1, FF_STEPS // 2) as r:
                for b in range(2):
                    up(2 * r + b, b, 12 * r + (6 * b + T_FF - 2), False)
            up(FF_STEPS - 1, 0, T_FF + 6 * (FF_STEPS - 1) - 2, False)
            for m in range(KT):
                act.wait_ge(down_ev, 8 * (FF_STEPS - 1) + m + 1)
                square(NFIN, m, xres[:, m, :])
            root(NFIN)
            for k in range(KT):
                act.wait_ge(norm_scaled, 4 * KT + k + 1)
                square(NGDN, k, xres[:, k, :])
            root(NGDN)
            hi_parts(HGDN, nt, hhi, (norm_scaled, 5 * KT + 1), T_GDN)
            act.wait_ge(h_lo_done, KT * (HGDN + 1))
            for k in range(KT):
                act.dma_start(x_spill[k], xres[:, k, :]).then_inc(spilled, 16)
            act.wait_ge(ab_mm, 1)
            A(tiny[:, 0:2, :], pa[:, 0:NB * N_AB].rearrange("p (n c) -> p n c", c=64), ACT.Copy).then_inc(ab_out, 1)
            act.wait_ge(ab_e, 1)
            done(A(tiny[:, 3, :], tiny[:, 3, :], ACT.Exp, scale=-1.0))
            done(A(tiny[:, 6, :], tiny[:, 6, :], ACT.Exp, scale=-1.0))
            done(A(row[:, 0:GDN], row[:, 0:GDN], ACT.Exp))
            settle()
            A(tiny[:, 3, :], tiny[:, 3, :], ACT.Ln, bias=1.0).then_inc(ab_e, 1)
            act.wait_ge(gc_mm, 1)
            A(tiny[:, 7, :], pb[:, 0:64], ACT.Copy)
            A(tiny[:, 8, :], pb[:, 64:128], ACT.Copy).then_inc(gc_out, 1)
            act.wait_ge(gc_diff, 1)
            A(tiny[:, 9, :], tiny[:, 9, :], ACT.Exp)
            A(tiny[:, 8, :], tiny[:, 8, :], ACT.Exp)
            A(tiny[:, 10, :], tiny[:, 7, :], ACT.Exp).then_inc(gc_out, 1)
            for h in range(GDN):
                if h == 0:
                    act.wait_ge(pads_zero, 3)
                else:
                    act.wait_ge(y_done, Y_GDN + h)
                for j in range(3):
                    n = 3 * h + j
                    t = T_GDN + 4 * h + j
                    if n >= 2:
                        act.wait_ge(gd_conv, n - 1)
                    evac(t, 0, (GP0, GP1)[n % 2][:, 3:3 + S], t % 2)
                    if j:
                        act.wait_ge(gd_conv, n)
                        A(H[:, j - 1, :], H[:, j - 1, :], ACT.Silu).then_inc(gd_silu, 1)
                t = T_GDN + 4 * h + 3
                act.wait_ge(gd_conv, 3 * h + 3)
                A(H[:, 2, :], H[:, 2, :], ACT.Silu).then_inc(gd_silu, 1)
                evac(t, 0, H[:, 3, :], t % 2, ACT.Silu)
                act.wait_ge(gd_silu, 3 * h + 2)
                for j in range(2):
                    A(N[:, j, :], H[:, j, :], ACT.Square).then_inc(gd_sq, 1)
                for j in range(2):
                    act.wait_ge(gd_ss, 2 * h + j + 1)
                    A(N[:, 2 + j, :], ps[j][:, :], ACT.Sqrt, bias=eps[:, 0:1]).then_inc(gd_root, 1)
                act.wait_ge(gd_diff, h + 1)
                A(TI, TI, ACT.Exp).then_inc(gd_exp, 1)
                A(N[:, 1, :], pa, ACT.Exp).then_inc(gd_exp, 1)
                act.wait_ge(gd_qk, 2 * h + 2)
                act.wait_ge(gd_kturn, h + 1)
                for n in range(NB):
                    last = A(ck(N[:, 2, :], n), ck(pa, n), ACT.Copy, scale=tiny[:, 9, n * GDN + h:n * GDN + h + 1])
                last.then_inc(gd_kdec, 1)
                act.wait_ge(gd_vturn, h + 1)
                for n in range(NB):
                    last = A(ck(N[:, 3, :], n), ck(pb, n), ACT.Copy, scale=tiny[:, 6, n * GDN + h:n * GDN + h + 1])
                last.then_inc(gd_vb, 1)
                for n in range(NB):
                    u = NB * h + n
                    act.wait_ge(ch_vn_mm, u + 1)
                    if u:
                        act.wait_ge(ch_s_mm, u)
                    A(v_new[:, :], pa[:, HALF:HALF + P], ACT.Copy).then_inc(ch_vn, 1)
                act.wait_ge(ch_s_mm, NB * (h + 1))
                done(A(XB, pb, ACT.Copy))
                settle()
                A(N[:, 0, :], XB, ACT.Square).then_inc(y_squared, 1)
                act.wait_ge(y_sums, RET + h + 1)
                A(TI, pa, ACT.Sqrt, bias=eps[:, 0:1], scale=1.0 / GDN_DK).then_inc(y_root, 1)
            act.wait_ge(y_done, Y_GDN + GDN)
            hi_parts(HGO, lambda k: yt[:, k, :], hhi, None, T_GO)
            act.wait_ge(h_lo_done, KT * (HGO + 1))
            act.wait_ge(spilled, 16 * KT)
            for k in range(KT):
                act.dma_start(xres[:, k, :], x_spill[k]).then_inc(x_loaded[k], 16)
            for m in range(KT):
                evac(T_GO + m, 0, yt[:, m, :], m % 2)
                act.wait_ge(ev_act, EV_GO + m + 1)
                square(NGP, m, yt[:, m, :])
            root(NGP)
            for k in range(KT):
                act.wait_ge(ev_dve, 2 * KT + k + 1)
                square(NFOX, k, xres[:, k, :])
            root(NFOX)
            hi_parts(HFOX, nt, hhi, (norm_scaled, 7 * KT + 1), T_FOX)
            act.wait_ge(h_lo_done, KT * (HFOX + 1))
            for k in range(KT):
                act.dma_start(x_spill[k], xres[:, k, :]).then_inc(spilled, 16)
            act.wait_ge(f_mm, 1)
            A(tiny[:, 0, :], pa[:, 0:64], ACT.Copy).then_inc(f_out, 1)
            act.wait_ge(f_e, 1)
            done(A(tiny[:, 3, :], tiny[:, 3, :], ACT.Exp, scale=-1.0))
            settle()
            A(tiny[:, 3, :], tiny[:, 3, :], ACT.Ln, bias=1.0).then_inc(f_e, 1)
            for h in range(FOX):
                if h:
                    act.wait_ge(y_done, Y_FOX + h)
                for j in range(4):
                    t = T_FOX + 4 * h + j
                    evac(t, 0, H[:, j, :], t % 2, ACT.Silu if j == 3 else ACT.Copy)
                act.wait_ge(ev_act, EV_FOX + 4 * h + 3)
                for j in range(2):
                    A(N[:, j, :], H[:, 2 * j, :], ACT.Square).then_inc(fx_sq, 1)
                for j in range(2):
                    act.wait_ge(fx_ss, 2 * h + j + 1)
                    A(N[:, 2 + j, :], ps[j][:, :], ACT.Sqrt, bias=eps[:, 0:1], scale=1.0 / FOX_D).then_inc(fx_root, 1)
                act.wait_ge(fx_vturn, h + 1)
                if h == 0:
                    act.wait_ge(spilled, 2 * 16 * KT)
                A(X4(0), pa, ACT.Copy).then_inc(fx_v, 1)
                for q in range(NB):
                    u = NB * h + q
                    w = (q + 1) * P
                    act.wait_ge(fx_s, u + 1)
                    A(X4(3 + q % 2)[:, 0:w], X4(3 + q % 2)[:, 0:w], ACT.Exp, bias=stat[:, 14 + 4 * (q % 2):15 + 4 * (q % 2)],
                      accum_out=stat[:, 15 + 4 * (q % 2):16 + 4 * (q % 2)]).then_inc(fx_exp, 1)
                    act.wait_ge(fx_turn, u + 1)
                    if u:
                        act.wait_ge(fx_o, u)
                    A(X4(5)[:, 0:w], gp[0][:, 0:w], ACT.Copy).then_inc(fx_pt, 1)
            act.wait_ge(y_done, Y_FOX + FOX)
            hi_parts(HFO, lambda k: yt[:, k, :], hhi, None, T_FO)
            act.wait_ge(h_lo_done, KT * (HFO + 1))
            act.wait_ge(spilled, 2 * 16 * KT)
            for k in range(KT):
                act.dma_start(xres[:, k, :], x_spill[k]).then_inc(x_loaded[k], 16)
            for m in range(KT):
                evac(T_FO + m, 0, yt[:, m, :], m % 2)
                act.wait_ge(ev_act, EV_FO + m + 1)
                square(NFP, m, yt[:, m, :])
            root(NFP)
            for k in range(KT):
                act.wait_ge(out_ready, k + 1)
                act.dma_start(out[k], xres[:, k, :]).then_inc(stored, 16)
            act.wait_ge(stored, 16 * KT)

        @block.vector
        def _(dve):
            V = nc.vector
            steps = [0]

            def done(ins):
                steps[0] += 1
                ins.then_inc(dve_step, 1)

            def settle():
                dve.wait_ge(dve_step, steps[0])

            def add_square(j, k):
                n = KT * j + k
                wide = j != NMEM
                ssq = N[:, 2, :] if wide else H[:, 1, 0:N_MEM]
                src = N[:, k % 2, :] if wide else H[:, 0, (k % 2) * N_MEM:(k % 2 + 1) * N_MEM]
                dve.wait_ge(sq_ready, n + 1)
                if k == 0:
                    if j:
                        dve.wait_ge(norm_mm, j)
                    V.tensor_copy(ssq, src).then_inc(sq_added, 1)
                else:
                    dve.wait_ge(sq_added, n)
                    V.tensor_tensor(ssq, ssq, src, ALU.add).then_inc(sq_added, 1)

            def rstd(j):
                dve.wait_ge(norm_root, j + 1)
                r = N[:, 3, :] if j != NMEM else H[:, 1, N_MEM:2 * N_MEM]
                done(V.reciprocal(r, r))
                settle()

            def lo_part(p, k, src, dst_hi, dst_lo):
                dve.wait_ge(h_hi_done, KT * p + k + 1)
                V.tensor_tensor(dst_lo[:, k, :], src, dst_hi[:, k, :].bitcast(F32), ALU.subtract).then_inc(h_lo_done, 1)

            def norm_to_h(j, p, c, src, gain, dst_hi, dst_lo):
                rstd(j)
                wide = j != NMEM
                r = N[:, 3, :] if wide else H[:, 1, N_MEM:2 * N_MEM]

                def t(k):
                    return N[:, k % 2, :] if wide else H[:, 0, (k % 2) * N_MEM:(k % 2 + 1) * N_MEM]

                for k in range(KT):
                    if k >= 2:
                        dve.wait_ge(h_lo_done, KT * p + k - 1)
                    if gain is None:
                        V.tensor_tensor(t(k), src(k), r, ALU.mult).then_inc(norm_scaled, 1)
                    else:
                        V.scalar_tensor_tensor(t(k), src(k), vc(gain, k), r, ALU.mult, ALU.mult).then_inc(norm_scaled, 1)
                    if k:
                        lo_part(p, k - 1, t(k - 1), dst_hi, dst_lo)
                lo_part(p, KT - 1, t(KT - 1), dst_hi, dst_lo)

            def xt(k):
                return xres[:, k, :]

            dve.wait_ge(const_loaded, 80)
            for k in range(KT):
                add_square(NMIX, k)
            norm_to_h(NMIX, HMIX, 0, xt, "mix_g", hhi, hlo)
            dve.wait_ge(pos_loaded, 16)
            done(V.tensor_copy(X4(5), H[:, 3, :].bitcast(I32)))
            settle()
            done(V.tensor_scalar(X4(5), X4(5), cn("inv_freq", 0, 1), None, ALU.mult))
            settle()
            for dst, shift in ((X4(6), 0.0), (X4(7), 0.25)):
                done(V.tensor_scalar(X4(4), X4(5), 1.0 / (2 * math.pi), shift, ALU.mult, ALU.add))
                settle()
                done(V.tensor_scalar(X4(4), X4(4), ROUND_MAGIC, ROUND_MAGIC, ALU.add, ALU.subtract))
                settle()
                done(V.scalar_tensor_tensor(dst, X4(4), -TWO_PI_HI, X4(5), ALU.mult, ALU.add))
                settle()
                for part in (TWO_PI_MID, TWO_PI_LO):
                    done(V.scalar_tensor_tensor(dst, X4(4), -part, dst, ALU.mult, ALU.add))
                    settle()
                done(V.tensor_scalar(dst, dst, shift * 2 * math.pi, math.pi, ALU.add, ALU.min))
                settle()
                if shift:
                    V.tensor_scalar(dst, dst, -math.pi, None, ALU.max).then_inc(angles, 1)
                else:
                    done(V.tensor_scalar(dst, dst, -math.pi, None, ALU.max))
                    settle()
            dve.wait_ge(rope_tab, 1)
            for h in range(RET):
                for j in range(2):
                    scale = 1.0 if j == 0 else RET_DH ** -0.5
                    dve.wait_ge(ev_act, 4 * h + j + 1)
                    if h and j == 0:
                        dve.wait_ge(ret_out, h)
                    done(V.scalar_tensor_tensor(X4(2), H[:, j, :], scale, X4(7), ALU.mult, ALU.mult))
                    done(V.scalar_tensor_tensor(X4(3), X4(j), scale, X4(6), ALU.mult, ALU.mult))
                    settle()
                    V.tensor_tensor(H[:, j, :], X4(2), X4(3), ALU.add).then_inc(roped, 1)
                    dve.wait_ge(roped, 2 * h + j + 1)
                    if j == 0:
                        done(V.tensor_tensor(chunks(X4(4)), chunks(H[:, 0, :]), over(cn("xi", h), NB), ALU.mult))
                dve.wait_ge(ret_turned, 2 * h + 2)
                V.tensor_copy(X4(0), pb).then_inc(ret_v, 1)
                dve.wait_ge(ret_scores, h + 1)
                V.tensor_tensor(chunks(X4(1)), chunks(pa), over(cn("dmat", h), NB), ALU.mult).then_inc(ret_probs, 1)
                dve.wait_ge(ret_kv, h + 1)
                for n in range(NB - 1):
                    if n == 0:
                        done(V.tensor_copy(ck(X4(2), 1), ck(pb, 0)))
                    else:
                        settle()
                        last = V.scalar_tensor_tensor(ck(X4(2), n + 1), ck(X4(2), n), RET_DECAY[h], ck(pb, n), ALU.mult, ALU.add)
                        if n < NB - 2:
                            done(last)
                last.then_inc(ret_states, 1)
                dve.wait_ge(y_root, h + 1)
                done(V.reciprocal(N[:, 2, :], N[:, 2, :]))
                settle()
                done(V.scalar_tensor_tensor(X4(5), X4(5), vc("gn_g", h), N[:, 2, :], ALU.mult, ALU.mult))
                dve.wait_ge(ev_act, 4 * h + 4)
                settle()
                V.tensor_tensor(yt[:, h, :], X4(5), H[:, 3, :], ALU.mult).then_inc(y_done, 1)
            W = PAD + S
            U, B, C, DD = X[:, 0:W], X[:, W:2 * W], X[:, 2 * W:3 * W], X[:, 3 * W:3 * W + S]
            dve.wait_ge(y_done, RET)
            for i in range(2):
                V.memset((U, B)[i][:, 0:PAD], 0.0)
            V.memset(C[:, 0:PAD], 0.0).then_inc(pads_zero, 1)
            dve.wait_ge(pads_zero, 1)
            for g, win in enumerate(POOL_WINDOWS):
                dve.wait_ge(ev_act, 4 * RET + g + 1)
                if g:
                    dve.wait_ge(pool_mm, g)
                src, dst = U, B
                step = 1
                while step < win:
                    done(V.tensor_tensor(dst[:, PAD:], src[:, PAD:], src[:, PAD - step:W - step], ALU.add))
                    settle()
                    src, dst = dst, (C if dst is B else B)
                    step *= 2
                done(V.scalar_tensor_tensor(DD[:, PAD:], src[:, 2 * PAD:], 1.0 / win, U[:, 2 * PAD:], ALU.mult, ALU.subtract))
                done(V.tensor_tensor(DD[:, 0:PAD], src[:, PAD:2 * PAD], cn("pool_rcnt", g, PAD), ALU.mult))
                settle()
                V.tensor_tensor(DD[:, 0:PAD], DD[:, 0:PAD], U[:, PAD:2 * PAD], ALU.subtract).then_inc(pool_in, 1)
            for k in range(KT):
                lo_part(HRET, k, yt[:, k, :], hhi, hlo)
            for k in range(KT):
                add_square(NMEM, k)
            norm_to_h(NMEM, HMEM, KT, lambda k: memx[:, k, :], "mem_g", mem_hi, mem_lo)

            def residual(t0, ev0, j):
                for m in range(KT):
                    dve.wait_ge(pe_slot, t0 + m + 1)
                    if ev0 == 0:
                        dve.wait_ge(x_loaded[m], 32)
                    V.tensor_tensor(xres[:, m, :], gp[m % 2][:, :], xres[:, m, :], ALU.add).then_inc(ev_dve, 1)
                    if m:
                        add_square(j, m - 1)
                add_square(j, KT - 1)

            residual(T_WOUT, 0, NXA)
            norm_to_h(NXA, HXA, 2 * KT, xt, "xa_g", hhi, hlo)
            for u in range(2 * XA_HEADS):
                dve.wait_ge(xa_scores, u + 1)
                done(V.tensor_reduce(stat[:, 0:4], pa.rearrange("p (q m) -> p q m", m=N_MEM), AX_X, ALU.max))
                settle()
                V.tensor_scalar(stat[:, 4:8], stat[:, 0:4], -(XA_DH ** -0.5), None, ALU.mult).then_inc(xa_max, 1)
                dve.wait_ge(xa_exp, u + 1)
                done(V.reciprocal(stat[:, 8:12], stat[:, 8:12]))
                settle()
                p3 = H[:, 2, :].rearrange("p (q m) -> p q m", m=N_MEM)
                r3 = stat[:, 8:12].rearrange("p (q a) -> p q a", a=1).broadcast_to([P, 4, N_MEM])
                V.tensor_tensor(p3, p3, r3, ALU.mult).then_inc(xa_probs, 1)
            for k in range(KT):
                lo_part(HXO, k, yt[:, k, :], hhi, hlo)
            residual(T_XO, KT, NFF)
            norm_to_h(NFF, HFF, 3 * KT, xt, "ffn_g", hhi, hlo)
            dve.wait_ge(h_lo_done, KT * (HFF + 1))
            V.memset(Nf[:, 0:2], 0.0)
            V.memset(Nf[:, FP:FP + 2], 0.0).then_inc(pads_zero, 1)

            def conv(i, j, v, cols):
                q = 2 * j + v
                a = Nf[:, v * FP:(v + 1) * FP]
                c = H[:, q, :]
                at = lambda name, n: vec[:, cols(name, n)]
                dve.wait_ge(ev_act, 4 * i + (EV_FF + q + 1))
                if not (isinstance(i, int) and i == 0):
                    dve.wait_ge(act_lo_done, 2 * i + (j - 1))
                V.tensor_scalar(c, a[:, 2:2 + S], at("ff_w", 2 * 2 * PAIRS + q), at("ff_b", q), ALU.mult, ALU.add).then_inc(ff_taps, 1)
                dve.wait_ge(ff_taps, 8 * i + (2 * q + 1))
                V.scalar_tensor_tensor(c, a[:, 1:1 + S], at("ff_w", 2 * PAIRS + q), c, ALU.mult, ALU.add).then_inc(ff_taps, 1)
                dve.wait_ge(ff_taps, 8 * i + (2 * q + 2))
                V.scalar_tensor_tensor(c, a[:, 0:S], at("ff_w", q), c, ALU.mult, ALU.add).then_inc(ff_conv, 1)

            def product(i, j):
                dve.wait_ge(ff_gate, 2 * i + (j + 1))
                dve.wait_ge(ff_conv, 4 * i + (2 * j + 2))
                V.tensor_tensor(H[:, 2 * j, :], H[:, 2 * j, :], H[:, 2 * j + 1, :], ALU.mult).then_inc(ff_prod, 1)

            def act_low(i, b, j):
                dve.wait_ge(act_hi_done, 2 * i + (j + 1))
                V.tensor_tensor(act_lo[:, 2 * b + j, :], H[:, 2 * j, :], act_hi[:, 2 * b + j, :].bitcast(F32),
                                ALU.subtract).then_inc(act_lo_done, 1)

            def down_add(i, t0, m):
                a, q = m // 4, m % 4
                if q == 3:
                    dve.wait_ge(pe_slot, t0 + (a + 1))
                else:
                    dve.wait_ge(down_mm, 6 * i + (3 * a + q + 1))
                V.tensor_tensor(xres[:, m, :], ps[m % 2][:, :], xres[:, m, :], ALU.add).then_inc(down_ev, 1)

            def cols_of(i):
                def cols(name, n):
                    at = 4 * i + (VEC_AT[name] + n)
                    return slice(at, at + 1) if isinstance(at, int) else bass.ds(at, 1)
                return cols

            def ff_step(i, b, t_down):
                cols = cols_of(i)
                conv(i, 0, 0, cols)
                conv(i, 0, 1, cols)
                product(i, 0)
                conv(i, 1, 0, cols)
                act_low(i, b, 0)
                conv(i, 1, 1, cols)
                for m in range(2):
                    down_add(i - 1, t_down, m)
                product(i, 1)
                down_add(i - 1, t_down, 2)
                down_add(i - 1, t_down, 3)
                act_low(i, b, 1)
                for m in range(4, KT):
                    down_add(i - 1, t_down, m)

            cols = cols_of(0)
            for j in range(2):
                conv(0, j, 0, cols)
                conv(0, j, 1, cols)
                product(0, j)
                act_low(0, 0, j)
            ff_step(1, 1, T_FF + 8)
            with dve.Fori(1, FF_STEPS // 2) as r:
                for b in range(2):
                    ff_step(2 * r + b, b, 12 * r + (6 * b + T_FF + 2))
            ff_step(FF_STEPS - 1, 0, T_FF + 6 * (FF_STEPS - 1) + 2)
            for m in range(KT):
                down_add(FF_STEPS - 1, T_GDN - 2, m)
                if m:
                    add_square(NFIN, m - 1)
            add_square(NFIN, KT - 1)
            rstd(NFIN)
            for k in range(KT):
                V.scalar_tensor_tensor(xres[:, k, :], xres[:, k, :], vc("final_g", k), N[:, 3, :], ALU.mult,
                                       ALU.mult).then_inc(norm_scaled, 1)
                if k:
                    add_square(NGDN, k - 1)
            add_square(NGDN, KT - 1)
            norm_to_h(NGDN, HGDN, 5 * KT, xt, "gdn_g", hhi, hlo)

            def t3(i):
                return tiny[:, i, :].rearrange("p (n h) -> p n h", h=8)

            ab = tiny[:, 0:2, :].rearrange("p a c -> p (a c)").rearrange("p (n c) -> p n c", c=N_AB)
            dve.wait_ge(ab_out, 1)

            def bias_row(at):
                return row[:, at:at + 8].rearrange("p (a h) -> p a h", a=1).broadcast_to([P, NB, 8])

            done(V.tensor_tensor(t3(2), ab[:, :, 0:GDN], bias_row(GDN), ALU.add))
            done(V.tensor_copy(t3(6), ab[:, :, GDN:N_AB]))
            settle()
            V.scalar_tensor_tensor(tiny[:, 3, :], tiny[:, 2, :], -1.0, tiny[:, 2, :], ALU.mult, ALU.max).then_inc(ab_e, 1)
            dve.wait_ge(ab_e, 2)
            done(V.scalar_tensor_tensor(tiny[:, 4, :], tiny[:, 2, :], 0.0, tiny[:, 3, :], ALU.max, ALU.add))
            done(V.tensor_scalar(tiny[:, 6, :], tiny[:, 6, :], 1.0, None, ALU.add))
            settle()
            done(V.reciprocal(tiny[:, 6, :], tiny[:, 6, :]))
            settle()
            V.scalar_tensor_tensor(t3(5), t3(4), -1.0, bias_row(0), ALU.mult, ALU.mult).then_inc(ab_ready, 1)
            dve.wait_ge(gc_out, 1)
            V.tensor_tensor(tiny[:, 9, :], tiny[:, 8, :], tiny[:, 7, :], ALU.subtract).then_inc(gc_diff, 1)
            dve.wait_ge(gc_out, 2)
            V.scalar_tensor_tensor(tiny[:, 10, :], tiny[:, 10, :], -1.0, tiny[:, 6, :], ALU.mult, ALU.mult).then_inc(gc_ready, 1)
            dve.wait_ge(gc_ready, 1)
            dve.wait_ge(spilled, 16 * KT)
            V.memset(GP0[:, 0:3], 0.0)
            V.memset(GP1[:, 0:3], 0.0).then_inc(pads_zero, 1)
            NL = len(LEVELS)
            for h in range(GDN):
                for j in range(3):
                    n = 3 * h + j
                    pad, c = (GP0, GP1)[n % 2], H[:, j, :]
                    dve.wait_ge(ev_act, EV_GDN + 4 * h + j + 1)

                    def tap(i):
                        return vc("gdn_w", (i * 3 + j) * GDN + h)

                    done(V.tensor_scalar(c, pad[:, 3:3 + S], tap(3), None, ALU.mult))
                    for i in (2, 1, 0):
                        settle()
                        last = V.scalar_tensor_tensor(c, pad[:, i:i + S], tap(i), c, ALU.mult, ALU.add)
                        if i:
                            done(last)
                    last.then_inc(gd_conv, 1)
                for j in range(2):
                    dve.wait_ge(gd_root, 2 * h + j + 1)
                    done(V.reciprocal(N[:, 2 + j, :], N[:, 2 + j, :]))
                    settle()
                    V.scalar_tensor_tensor(H[:, j, :], H[:, j, :], GDN_DK ** -0.5 if j == 0 else 1.0, N[:, 2 + j, :], ALU.mult,
                                           ALU.mult).then_inc(gd_qk, 1)
                dve.wait_ge(gd_gr, h + 1)
                for n in range(NB):
                    col = n * GDN + h
                    last = V.tensor_scalar(ck(TI, n), ck(pa, n), tiny[:, 7, col:col + 1], 0.0, ALU.subtract, ALU.min)
                last.then_inc(gd_diff, 1)
                dve.wait_ge(gd_exp, 2 * h + 1)
                done(V.tensor_tensor(chunks(AT), chunks(TI), over(cn("causal"), NB), ALU.mult))
                dve.wait_ge(gd_br, h + 1)
                V.tensor_tensor(MT, TI, pb, ALU.mult).then_inc(gd_mt1, 1)
                dve.wait_ge(gd_kk, h + 1)
                dve.wait_ge(gd_mt1, h + 1)
                V.tensor_tensor(MT, pa, MT, ALU.mult).then_inc(gd_mt, 1)
                dve.wait_ge(gd_attn_mm, h + 1)
                settle()
                V.tensor_tensor(AT, pb, AT, ALU.mult).then_inc(gd_attn, 1)
                dve.wait_ge(gd_exp, 2 * h + 2)
                dve.wait_ge(gd_qk, 2 * h + 1)
                done(V.tensor_tensor(N[:, 1, :], N[:, 1, :], H[:, 0, :], ALU.mult))
                dve.wait_ge(gd_mt, h + 1)
                done(V.tensor_tensor(chunks(TT), chunks(MT), over(cn("pair_t"), NB), ALU.mult))
                dve.wait_ge(gd_mturn, h + 1)
                done(V.tensor_tensor(chunks(TI), chunks(pa), over(cn("pair"), NB), ALU.mult))
                settle()
                done(V.scalar_tensor_tensor(chunks(TT), chunks(TT), -1.0, over(ident, NB), ALU.mult, ALU.add))
                V.scalar_tensor_tensor(chunks(TI), chunks(TI), -1.0, over(ident, NB), ALU.mult, ALU.add).then_inc(gd_t0, 1)
                settle()
                dve.wait_ge(gd_t0, h + 1)
                for l in range(NL):
                    for f in range(2):
                        cols = slice(f * HALF, (f + 1) * HALF)
                        dve.wait_ge(inv_x_mm, 2 * NL * h + 2 * l + f + 1)
                        V.tensor_tensor(chunks(XB[:, cols]), chunks(ps[f][:, 0:HALF]), over(cn("levels", l), 4),
                                        ALU.mult).then_inc(inv_x, 1)
                    for f in range(2):
                        cols = slice(f * HALF, (f + 1) * HALF)
                        dve.wait_ge(inv_y_mm, 4 * NL * h + 4 * l + 2 * f + 2)
                        V.tensor_tensor(TI[:, cols], TI[:, cols], ps[f][:, 0:HALF], ALU.subtract).then_inc(inv_t, 1)
                        V.tensor_tensor(TT[:, cols], TT[:, cols], ps[f][:, HALF:S], ALU.subtract).then_inc(inv_t, 1)
                        dve.wait_ge(inv_t, 4 * NL * h + 4 * l + 2 * f + 2)
                dve.wait_ge(gd_vb, h + 1)
                for n in range(NB):
                    u = NB * h + n
                    col = n * GDN + h
                    if u:
                        dve.wait_ge(ch_vn_mm, u)
                    if n == 0:
                        V.tensor_copy(rhs_r[:, :], ck(N[:, 3, :], 0)).then_inc(ch_r, 1)
                    else:
                        dve.wait_ge(ch_ks, (NB - 1) * h + n)
                        V.scalar_tensor_tensor(rhs_r[:, :], pa[:, 0:P], tiny[:, 10, col:col + 1], ck(N[:, 3, :], n), ALU.mult,
                                               ALU.add).then_inc(ch_r, 1)
                    dve.wait_ge(ch_s_mm, u + 1)
                    if n == 0:
                        V.tensor_copy(state[:, :], pa[:, P:2 * P]).then_inc(ch_s, 1)
                    else:
                        dve.wait_ge(ch_s, u)
                        V.scalar_tensor_tensor(state[:, :], state[:, :], tiny[:, 8, col:col + 1], pa[:, P:2 * P], ALU.mult,
                                               ALU.add).then_inc(ch_s, 1)
                dve.wait_ge(y_root, RET + h + 1)
                done(V.reciprocal(TI, TI))
                settle()
                done(V.scalar_tensor_tensor(XB, XB, vc("o_g", 0), TI, ALU.mult, ALU.mult))
                dve.wait_ge(ev_act, EV_GDN + 4 * h + 4)
                settle()
                V.tensor_tensor(yt[:, h, :], XB, H[:, 3, :], ALU.mult).then_inc(y_done, 1)
            for k in range(KT):
                lo_part(HGO, k, yt[:, k, :], hhi, hlo)
            for m in range(KT):
                add_square(NGP, m)

            def post(j, gain, signal, reload):
                rstd(j)
                for k in range(KT):
                    dve.wait_ge(x_loaded[k], reload)
                    V.scalar_tensor_tensor(yt[:, k, :], yt[:, k, :], vc(gain, k), N[:, 3, :], ALU.mult, ALU.mult).then_inc(norm_scaled, 1)
                    dve.wait_ge(norm_scaled, KT * j + k + 1)
                    V.tensor_tensor(xres[:, k, :], xres[:, k, :], yt[:, k, :], ALU.add).then_inc(signal, 1)
                    if j == NGP and k:
                        add_square(NFOX, k - 1)

            post(NGP, "gdn_post_g", ev_dve, 48)
            add_square(NFOX, KT - 1)
            norm_to_h(NFOX, HFOX, 7 * KT, xt, None, hhi, hlo)
            dve.wait_ge(f_out, 1)
            done(V.tensor_tensor(t3(2), t3(0), bias_row(N_AB), ALU.add))
            settle()
            V.scalar_tensor_tensor(tiny[:, 3, :], tiny[:, 2, :], -1.0, tiny[:, 2, :], ALU.mult, ALU.max).then_inc(f_e, 1)
            dve.wait_ge(f_e, 2)
            V.scalar_tensor_tensor(tiny[:, 11, :], tiny[:, 2, :], 0.0, tiny[:, 3, :], ALU.min, ALU.subtract).then_inc(f_ready, 1)
            dve.wait_ge(spilled, 2 * 16 * KT)
            done(V.tensor_scalar(stat[:, 24:25], vc("qn_g", 0), FOX_D ** -0.5, None, ALU.mult))
            settle()
            for h in range(FOX):
                for j in range(2):
                    dve.wait_ge(fx_root, 2 * h + j + 1)
                    done(V.reciprocal(N[:, 2 + j, :], N[:, 2 + j, :]))
                    settle()
                    gain = vc("kn_g", 0) if j == 0 else stat[:, 24:25]
                    V.scalar_tensor_tensor(H[:, 2 * j, :], H[:, 2 * j, :], gain, N[:, 2 + j, :], ALU.mult, ALU.mult).then_inc(fx_qk, 1)
                dve.wait_ge(fx_c_mm, h + 1)
                done(V.tensor_copy(ck(X4(1), 0), ck(pb, 0)))
                for n in range(1, NB):
                    settle()
                    done(V.tensor_scalar(ck(X4(1), n), ck(pb, n), X4(1)[:, n * P - 1:n * P], None, ALU.add))
                settle()
                V.tensor_tensor(chunks(X4(2)), chunks(X4(1)), over(cn("future"), NB), ALU.add).then_inc(fx_c, 1)
                dve.wait_ge(fx_c, h + 1)

                def rescale(q):
                    u = NB * h + q
                    w = (q + 1) * P
                    z = 4 * (q % 2)
                    dve.wait_ge(fx_exp, u + 1)
                    done(V.reciprocal(stat[:, 15 + z:16 + z], stat[:, 15 + z:16 + z]))
                    settle()
                    p = X4(3 + q % 2)[:, 0:w]
                    V.tensor_scalar(p, p, stat[:, 15 + z:16 + z], None, ALU.mult).then_inc(fx_p, 1)

                for q in range(NB):
                    u = NB * h + q
                    z = 4 * (q % 2)
                    sc = X4(3 + q % 2)
                    dve.wait_ge(fx_s_mm, u + 1)
                    if u >= 2:
                        dve.wait_ge(fx_turn, u - 1)
                    last = q * P
                    done(V.tensor_tensor_reduce(out=sc[:, last:last + P], in0=ps[q % 2][:, last:last + P], in1=ck(X4(2), q), scale=1.0,
                                                scalar=-MASKED, op0=ALU.subtract, op1=ALU.max, accum_out=stat[:, 12 + z:13 + z]))
                    settle()
                    if q:
                        done(V.tensor_tensor_reduce(out=sc[:, 0:last], in0=ps[q % 2][:, 0:last], in1=X4(1)[:, 0:last], scale=1.0,
                                                    scalar=stat[:, 12 + z:13 + z], op0=ALU.subtract, op1=ALU.max,
                                                    accum_out=stat[:, 13 + z:14 + z]))
                        settle()
                    m = 13 + z if q else 12 + z
                    V.tensor_scalar(stat[:, 14 + z:15 + z], stat[:, m:m + 1], -1.0, None, ALU.mult).then_inc(fx_s, 1)
                    if q:
                        rescale(q - 1)
                rescale(NB - 1)
                dve.wait_ge(fx_o, NB * (h + 1))
                dve.wait_ge(ev_act, EV_FOX + 4 * h + 4)
                V.tensor_tensor(yt[:, h, :], gp[1][:, :], H[:, 3, :], ALU.mult).then_inc(y_done, 1)
            for k in range(KT):
                lo_part(HFO, k, yt[:, k, :], hhi, hlo)
            for m in range(KT):
                add_square(NFP, m)
            post(NFP, "fox_post_g", out_ready, 64)


def kernel(**inputs):
    from concourse import bacc
    from concourse.bass_utils import run_bass_kernel_spmd

    a = {name: np.asarray(value) for name, value in inputs.items()}

    def tiles(w):
        return w.reshape(w.shape[0] // P, P, -1, P).transpose(2, 1, 0, 3)

    def cols(v):
        return v.reshape(-1, P).T

    w_in, gdn_in = tiles(a["w_in"][0]), tiles(a["gdn_w_in_2"][0][:, :4 * D])
    kv, fox_in = tiles(a["kv_w_2"][:, :2 * D]), tiles(a["fox_w_in_2"][0])
    ff_up = tiles(a["ffn_w_up"][0]).reshape(2, PAIRS, P, KT, P).transpose(1, 0, 2, 3, 4).reshape(2 * PAIRS, P, KT, P)
    ff_down = a["ffn_w_down"][0].reshape(FF_STEPS, 2, P, 2, 4, P).transpose(0, 3, 2, 4, 1, 5).reshape(FF_STEPS, 2, P, KT, P)
    steps = [ff_up[0:4]]
    for i in range(FF_STEPS):
        steps += [ff_up[4 * (i + 1):4 * (i + 2)], ff_down[i]]
    stream = [w_in[[4 * j + h for h in range(RET_HEADS) for j in range(4)]], w_in[16:20], tiles(a["w_out"][0]),
              tiles(a["xa_wkv"][0]), tiles(a["xa_wq"][0]), tiles(a["xa_wo"][0]), *steps,
              gdn_in[[8 * j + h for h in range(GDN_HEADS) for j in range(4)]], tiles(a["gdn_w_out_2"][0])]
    for h in range(FOX_HEADS):
        stream += [kv[[h, 8 + h]], fox_in[[h, 8 + h]]]
    stream.append(tiles(a["fox_w_out_2"][0]))
    ff_order = [v * PAIRS + p for p in range(PAIRS) for v in range(2)]
    vecs = {"mix_g": a["mix_norm_g"], "mem_g": a["mem_norm_g"], "xa_g": a["xa_norm_g"], "ffn_g": a["ffn_norm_g"],
            "final_g": a["final_norm_g"], "gdn_g": a["gdn_pre_norm_2"], "gdn_post_g": a["gdn_post_norm_2"],
            "kv_g": a["kv_norm_2"], "fox_g": a["fox_pre_norm_2"], "fox_post_g": a["fox_post_norm_2"],
            "gn_g": a["ret_gn_g"], "pool_scale": a["pool_scale"], "o_g": a["gdn_o_norm_2"], "kn_g": a["kv_k_norm_2"],
            "qn_g": a["fox_q_norm_2"], "gdn_w": a["gdn_conv_w_2"],
            "ff_b": a["ffn_conv_b"][0].reshape(-1, P)[ff_order],
            "ff_w": a["ffn_conv_w"][0].reshape(3, -1, P)[:, ff_order]}
    arrays = {
        "w_stream": np.concatenate(stream),
        "x_t": a["x"][0].T.reshape(KT, P, S),
        "mem_t": a["mem"][0].T.reshape(KT, P, N_MEM).transpose(1, 0, 2),
        "positions": a["positions"].reshape(1, S),
        "vecs": np.concatenate([cols(vecs[name]) for name, _ in VEC_NAMES], 1),
        "rows": np.concatenate([a["gdn_a_log_2"][0], a["gdn_dt_bias_2"][0], a["kv_forget_bias_2"]]).reshape(1, N_SMALL),
        "small_w": np.concatenate([a["gdn_w_in_2"][0][:, 4 * D:], a["kv_w_2"][:, 2 * D:]], 1)
        .reshape(KT, P, N_SMALL).transpose(1, 0, 2),
        "pool_w": a["pool_w"][0].transpose(1, 0, 2),
        "consts": shape_constants(),
    }
    arrays = {name: np.ascontiguousarray(v) for name, v in arrays.items()}
    nc = bacc.Bacc("TRN2", target_bir_lowering=False, num_devices=1)
    args = [nc.dram_tensor(name, v.shape, mybir.dt.from_np(v.dtype), kind="ExternalInput").ap() for name, v in arrays.items()]
    x_spill = nc.dram_tensor("x_spill", (KT, P, S), F32, kind="Internal").ap()
    out = nc.dram_tensor("out_t", (KT, P, S), F32, kind="ExternalOutput").ap()
    build(nc, *args, x_spill, out)
    got = run_bass_kernel_spmd(nc, [arrays], core_ids=[0]).results[0]["out_t"]
    return got.reshape(D, S).T.reshape(1, S, D)
```

```python
import math
from contextlib import ExitStack

import numpy as np

import concourse.bass as bass
from concourse import mybir

F32 = mybir.dt.float32
F32R = mybir.dt.float32r
I32 = mybir.dt.int32
ALU = mybir.AluOpType
ACT = mybir.ActivationFunctionType
AX_X = mybir.AxisListType.X

P = 128
S = 1024
D = 1024
KT = D // P
HALF = 512
NB = S // P
EPS = 1e-6
N_MEM = 256
RET_HEADS, RET_DH = 4, 128
XA_HEADS, XA_DH = 4, 256
POOL_WINDOWS = (2, 4, 8, 16)
PAD = 16
D_FF = 2816
PAIRS = D_FF // P
FF_STEPS = PAIRS // 2
GDN_HEADS, GDN_DK = 8, 128
FOX_HEADS, FOX_D = 8, 128
CONV_K = 4
LEVELS = (2, 4, 8, 16, 32, 64)
MASKED = 1e30

T_RET = 0
T_WOUT = T_RET + 4 * RET_HEADS + len(POOL_WINDOWS)
T_MEM = T_WOUT + KT
T_XQ = T_MEM + 2 * KT
T_XO = T_XQ + KT
T_FF = T_XO + KT
T_GDN = T_FF + 2 * PAIRS + 2 * FF_STEPS
T_GO = T_GDN + 4 * GDN_HEADS
T_FOX = T_GO + KT
T_FO = T_FOX + 4 * FOX_HEADS
T_END = T_FO + KT
EV_RET, EV_MEM = 0, T_WOUT
EV_XQ = EV_MEM + 2 * KT
EV_FF = EV_XQ + KT
EV_GDN = EV_FF + 2 * PAIRS
EV_GO = EV_GDN + 4 * GDN_HEADS
EV_FOX = EV_GO + KT
EV_FO = EV_FOX + 4 * FOX_HEADS

VEC_NAMES = (("mix_g", KT), ("mem_g", KT), ("xa_g", KT), ("ffn_g", KT), ("final_g", KT), ("gdn_g", KT),
             ("gdn_post_g", KT), ("kv_g", KT), ("fox_g", KT), ("fox_post_g", KT), ("gn_g", RET_HEADS),
             ("pool_scale", 4), ("o_g", 1), ("kn_g", 1), ("qn_g", 1), ("ff_b", 2 * PAIRS),
             ("ff_w", 3 * 2 * PAIRS), ("gdn_w", CONV_K * 3 * GDN_HEADS))
VEC_AT, _n = {}, 0
for _name, _width in VEC_NAMES:
    VEC_AT[_name] = _n
    _n += _width
VEC_COLS = _n
CONST_NAMES = (("ident", P), ("triu", P), ("ones", P), ("causal", P), ("future", P),
               ("pair_t", P), ("levels", P // 2 * len(LEVELS)), ("dmat", P * RET_HEADS),
               ("xi", P * RET_HEADS), ("zeta", RET_HEADS), ("inv_freq", 1), ("pool_rcnt", PAD * 4))
CONST_AT, _n = {}, 0
for _name, _width in CONST_NAMES:
    CONST_AT[_name] = _n
    _n += _width
CONST_COLS = _n
N_AB = 2 * GDN_HEADS
N_SMALL = N_AB + FOX_HEADS
LOG_GAMMA = np.log1p(-np.exp2(-5.0 - np.arange(RET_HEADS)))
RET_DECAY = [float(v) for v in np.exp(LOG_GAMMA * P).astype(np.float32)]
TWO_PI_HI, TWO_PI_MID = 6.28125, 1.9340515136718750e-3
TWO_PI_LO = 2 * math.pi - TWO_PI_HI - TWO_PI_MID
ROUND_MAGIC = 1.5 * 2.0 ** 23


def shape_constants():
    i = np.arange(P)
    row, col = i[:, None], i[None, :]
    c = {"ident": row == col, "triu": row <= col, "ones": np.ones((P, P)), "causal": row <= col,
         "future": MASKED * (col > row)}
    pair = (row // 2 == col // 2) & (row % 2 == 1) & (col % 2 == 0)
    c["pair_t"] = -1.0 * pair.T
    c["levels"] = np.concatenate([((row // (2 * b) == col // (2 * b)) & (row // b % 2 == 1))[:, i // b % 2 == 0]
                                  for b in LEVELS], 1)
    c["dmat"] = np.concatenate([np.where(col >= row, np.exp(lg * np.maximum(col - row, 0)), 0.0)
                                for lg in LOG_GAMMA], 1)
    c["xi"] = np.concatenate([np.exp(lg * (col + 1.0)) * np.ones((P, 1)) for lg in LOG_GAMMA], 1)
    c["zeta"] = np.exp(LOG_GAMMA[None, :] * (P - 1 - row))
    c["inv_freq"] = np.exp(-math.log(10000.0) * (row % 64) * 2 / 128)
    c["pool_rcnt"] = np.concatenate([1.0 / np.minimum(np.arange(PAD) + 1, w)[None, :] * np.ones((P, 1))
                                     for w in POOL_WINDOWS], 1)
    return np.concatenate([np.asarray(c[n], np.float32) for n, _ in CONST_NAMES], 1)


def build(nc, w_stream, x_t, mem_t, positions, vecs, rows, small_w, pool_w, consts, x_spill, out):
    ctx = ExitStack()
    with ctx:
        def sb(name, shape, dt=F32):
            return ctx.enter_context(nc.sbuf_tensor(name, shape, dt))

        def sem(name):
            return ctx.enter_context(nc.semaphore(name))

        raw = [sb(f"w_raw{i}", [P, KT, P]) for i in range(2)]
        whi = [sb(f"w_hi{i}", [P, KT, P], F32R) for i in range(2)]
        wlo = [sb(f"w_lo{i}", [P, KT, P], F32R) for i in range(2)]
        const = sb("const", [P, CONST_COLS])
        vec = sb("vec", [P, VEC_COLS])
        row = sb("row", [P, N_SMALL])
        poolw = sb("poolw", [P, 4, P])
        small_raw = sb("small_raw", [P, KT, N_SMALL])
        small_hi = sb("small_hi", [P, KT, N_SMALL], F32R)
        small_lo = sb("small_lo", [P, KT, N_SMALL], F32R)
        tiny = sb("tiny", [P, 16, 64])
        stat = sb("stat", [P, 32])
        rn = sb("head_rstd", [P, 32])
        state = sb("state", [P, P])
        rhs_r = sb("rhs_r", [P, P])
        v_new = sb("v_new", [P, P])
        eps = sb("eps", [P, 1])

        hhi = sb("h_hi", [P, KT, S], F32R)
        hlo = sb("h_lo", [P, KT, S], F32R)
        xres = sb("xres", [P, KT, S])
        H = sb("head", [P, 4, S])
        N = sb("norm", [P, 4, S])
        with nc.sbuf_tensor("yt", [P, KT, S], F32) as yt:
            pass
        with nc.sbuf_tensor("memx", [P, KT, N_MEM], F32) as memx, \
                nc.sbuf_tensor("mem_hi", [P, KT, N_MEM], F32R) as mem_hi, \
                nc.sbuf_tensor("mem_lo", [P, KT, N_MEM], F32R) as mem_lo:
            pass
        with nc.sbuf_tensor("act_hi", [P, 4, S], F32R) as act_hi, \
                nc.sbuf_tensor("act_lo", [P, 4, S], F32R) as act_lo:
            pass
        X = xres[:, :, :].rearrange("p k s -> p (k s)")
        Nf = N[:, :, :].rearrange("p k s -> p (k s)")

        def X4(i):
            return X[:, i * S:(i + 1) * S]

        GP0, GP1 = X[:, 0:S + 3], X[:, S + 3:2 * (S + 3)]
        G0 = 2 * (S + 3)
        AT, MT, TI, TT, V_RAW = [X[:, G0 + i * S:G0 + (i + 1) * S] for i in range(5)]
        XB = X[:, G0 + 5 * S:G0 + 5 * S + HALF]

        FP = S + 2

        gp = [ctx.enter_context(nc.psum_tensor(f"gemm{i}", [P, S], F32)) for i in range(2)]
        ps = [ctx.enter_context(nc.psum_tensor(f"small{i}", [P, S], F32)) for i in range(2)]
        pa, pb = ps[0][:, :], ps[1][:, :]

        def cn(name, i=0, width=P):
            at = CONST_AT[name] + i * width
            return const[:, at:at + width]

        def vc(name, i):
            return vec[:, VEC_AT[name] + i:VEC_AT[name] + i + 1]

        def chunks(ap):
            return ap.rearrange("p (n c) -> p n c", c=P)

        def ck(ap, n):
            return ap[:, n * P:(n + 1) * P]

        def over(ap, n):
            return ap.rearrange("p (a c) -> p a c", a=1).broadcast_to([P, n, P])

        ident, ones, triu = cn("ident"), cn("ones"), cn("triu")

        w_loaded = [sem(f"w_loaded{i}") for i in range(2)]
        const_loaded = sem("const_loaded")
        x_loaded = [sem(f"x_loaded{k}") for k in range(KT)]
        mem_loaded, pos_loaded = sem("mem_loaded"), sem("pos_loaded")
        spilled, stored = sem("spilled"), sem("stored")
        w_gained, w_hi_done, w_split = sem("w_gained"), sem("w_hi_done"), sem("w_split")
        small_step, small_split = sem("small_step"), sem("small_split")
        eps_set = sem("eps_set")
        pe_slot = sem("pe_slot")
        ev_act, ev_dve = sem("ev_act"), sem("ev_dve")
        sq_ready, sq_added = sem("sq_ready"), sem("sq_added")
        norm_mm, norm_root, norm_scaled = sem("norm_mm"), sem("norm_root"), sem("norm_scaled")
        h_hi_done, h_lo_done = sem("h_hi_done"), sem("h_lo_done")
        act_step, dve_step = sem("act_step"), sem("dve_step")
        angles, rope_tab = sem("angles"), sem("rope_tab")
        roped = sem("roped")
        ret_turned, ret_kz, ret_v = sem("ret_turned"), sem("ret_kz"), sem("ret_v")
        ret_scores, ret_probs = sem("ret_scores"), sem("ret_probs")
        ret_kv, ret_states, ret_out = sem("ret_kv"), sem("ret_states"), sem("ret_out")
        y_squared, y_sums, y_root, y_done = sem("y_squared"), sem("y_sums"), sem("y_root"), sem("y_done")
        pads_zero, pool_in, pool_mm, pool_y = sem("pads_zero"), sem("pool_in"), sem("pool_mm"), sem("pool_y")
        mem_turned, mem_v = sem("mem_turned"), sem("mem_v")
        xa_scores, xa_max, xa_exp, xa_probs = sem("xa_scores"), sem("xa_max"), sem("xa_exp"), sem("xa_probs")
        xa_turned, xa_pt, xa_out, xa_y = sem("xa_turned"), sem("xa_pt"), sem("xa_out"), sem("xa_y")
        ff_taps, ff_conv, ff_gate, ff_prod = sem("ff_taps"), sem("ff_conv"), sem("ff_gate"), sem("ff_prod")
        act_hi_done, act_lo_done = sem("act_hi_done"), sem("act_lo_done")
        down_mm, down_ev = sem("down_mm"), sem("down_ev")
        ab_mm, ab_out, ab_e, ab_ready = sem("ab_mm"), sem("ab_out"), sem("ab_e"), sem("ab_ready")
        gc_mm, gc_out, gc_diff, gc_ready = sem("gc_mm"), sem("gc_out"), sem("gc_diff"), sem("gc_ready")
        gd_conv, gd_silu, gd_sq, gd_ss, gd_root = (sem("gd_conv"), sem("gd_silu"), sem("gd_sq"), sem("gd_ss"),
                                                   sem("gd_root"))
        gd_qk = sem("gd_qk")
        gd_gr, gd_diff, gd_exp, gd_br, gd_mt1 = sem("gd_gr"), sem("gd_diff"), sem("gd_exp"), sem("gd_br"), sem("gd_mt1")
        gd_kk, gd_mt, gd_attn_mm, gd_attn = sem("gd_kk"), sem("gd_mt"), sem("gd_attn_mm"), sem("gd_attn")
        gd_kturn, gd_kdec, gd_vturn, gd_vb = sem("gd_kturn"), sem("gd_kdec"), sem("gd_vturn"), sem("gd_vb")
        gd_t0, gd_tturn, gd_ti = sem("gd_t0"), sem("gd_tturn"), sem("gd_ti")
        gd_rstd, gd_wide, gd_o = sem("gd_rstd"), sem("gd_wide"), sem("gd_o")
        go_ss, go_root, go_rstd, go_wide = sem("go_ss"), sem("go_root"), sem("go_rstd"), sem("go_wide")
        inv_turn, inv_tt = sem("inv_turn"), sem("inv_tt")
        inv_x_mm, inv_x, inv_y_mm, inv_t = sem("inv_x_mm"), sem("inv_x"), sem("inv_y_mm"), sem("inv_t")
        ch_ks, ch_r, ch_vn_mm, ch_vn, ch_s_mm, ch_s = (sem("ch_ks"), sem("ch_r"), sem("ch_vn_mm"), sem("ch_vn"),
                                                       sem("ch_s_mm"), sem("ch_s"))
        f_mm, f_out, f_e, f_ready = sem("f_mm"), sem("f_out"), sem("f_e"), sem("f_ready")
        fx_sq, fx_ss, fx_root, fx_qk = sem("fx_sq"), sem("fx_ss"), sem("fx_root"), sem("fx_qk")
        fx_vturn, fx_v, fx_c_mm, fx_c = sem("fx_vturn"), sem("fx_v"), sem("fx_c_mm"), sem("fx_c")
        fx_s_mm, fx_s, fx_exp, fx_p = sem("fx_s_mm"), sem("fx_s"), sem("fx_exp"), sem("fx_p")
        fx_turn, fx_pt, fx_o, fx_y = sem("fx_turn"), sem("fx_pt"), sem("fx_o"), sem("fx_y")
        fx_rstd, fx_wide = sem("fx_rstd"), sem("fx_wide")
        out_ready = sem("out_ready")
        RET, GDN, FOX = RET_HEADS, GDN_HEADS, FOX_HEADS
        NMIX, NMEM, NXA, NFF, NFIN, NGDN, NGP, NFOX, NFP = range(9)
        HMIX, HRET, HMEM, HXA, HXO, HFF, HGDN, HGO, HFOX, HFO = range(10)
        Y_GDN = RET

        def gdn_dst(h, j):
            return (yt[:, h, :], H[:, h % 2, :], V_RAW)[j]

        def fox_round(g, q, r):
            return 12 * g + (q if q < 4 else 2 * q - 4) + r

        block = ctx.enter_context(nc.Block())

        @block.sync
        def _(sp):
            for t in range(2):
                sp.dma_start(raw[t][:, :, :], w_stream[t]).then_inc(w_loaded[t], 16)
                if t == 0:
                    for k in range(KT):
                        sp.dma_start(xres[:, k, :], x_t[k]).then_inc(x_loaded[k], 16)
            with sp.Fori(1, T_END // 2) as i:
                for t in range(2):
                    sp.wait_ge(w_split, 2 * i + t - 1)
                    sp.dma_start(raw[t][:, :, :], w_stream[2 * i + t]).then_inc(w_loaded[t], 16)

        @block.gpsimd
        def _(pool):
            for dst, src in ((const[:, :], consts), (vec[:, :], vecs), (row[:, :], rows.broadcast_to([P, N_SMALL])),
                             (small_raw[:, :, :], small_w), (poolw[:, :, :], pool_w)):
                pool.dma_start(dst, src).then_inc(const_loaded, 16)
            pool.dma_start(H[:, 3, :].bitcast(I32), positions.broadcast_to([P, S])).then_inc(pos_loaded, 16)
            nc.gpsimd.memset(eps[:, :], EPS).then_inc(eps_set, 1)

            pool.wait_ge(const_loaded, 80)
            fcols = small_raw[:, :, N_AB:N_SMALL]
            gain = vec[:, VEC_AT["kv_g"]:VEC_AT["kv_g"] + KT].rearrange("p (k a) -> p k a", a=1)
            nc.gpsimd.tensor_tensor(fcols, fcols, gain.broadcast_to([P, KT, FOX]), ALU.mult).then_inc(small_step, 1)
            pool.wait_ge(small_step, 1)
            nc.gpsimd.tensor_copy(small_hi[:, :, :], small_raw[:, :, :]).then_inc(small_step, 1)
            pool.wait_ge(small_step, 2)
            nc.gpsimd.tensor_tensor(small_lo[:, :, :], small_raw[:, :, :], small_hi[:, :, :].bitcast(F32),
                                    ALU.subtract).then_inc(small_split, 1)

            unit = ones[:, 0:1].rearrange("p (a b) -> p a b", a=1).broadcast_to([P, KT, P])

            def split_slot(t, s, turn):
                pool.wait_ge(w_loaded[s], 16 * turn)
                nc.gpsimd.tensor_tensor(whi[s][:, :, :], raw[s][:, :, :], unit, ALU.mult).then_inc(w_hi_done, 1)
                pool.wait_ge(w_hi_done, t + 1)
                nc.gpsimd.tensor_tensor(wlo[s][:, :, :], raw[s][:, :, :], whi[s][:, :, :].bitcast(F32),
                                        ALU.subtract).then_inc(w_split, 1)

            for s in range(2):
                split_slot(s, s, 1)
            with pool.Fori(1, T_FOX // 2) as i:
                for s in range(2):
                    pool.wait_ge(pe_slot, 2 * i + s - 1)
                    split_slot(2 * i + s, s, i + 1)
            with pool.Fori(0, FOX) as i:
                for j in range(4):
                    t, s, name = T_FOX + j, j % 2, ("kv_g", "fox_g", "kv_g", "fox_g")[j]
                    gain = vec[:, VEC_AT[name]:VEC_AT[name] + KT].rearrange("p (k a) -> p k a", a=1)
                    pool.wait_ge(w_loaded[s], 32 * i + 16 * (t // 2 + 1))
                    nc.gpsimd.tensor_tensor(raw[s][:, :, :], raw[s][:, :, :], gain.broadcast_to([P, KT, P]),
                                            ALU.mult).then_inc(w_gained, 1)
                    pool.wait_ge(w_gained, 4 * i + (j + 1))
                    pool.wait_ge(pe_slot, 4 * i + (t - 1))
                    nc.gpsimd.tensor_tensor(whi[s][:, :, :], raw[s][:, :, :], unit, ALU.mult).then_inc(w_hi_done, 1)
                    pool.wait_ge(w_hi_done, 4 * i + (t + 1))
                    nc.gpsimd.tensor_tensor(wlo[s][:, :, :], raw[s][:, :, :], whi[s][:, :, :].bitcast(F32),
                                            ALU.subtract).then_inc(w_split, 1)
            with pool.Fori(T_FO // 2, T_END // 2) as i:
                for s in range(2):
                    pool.wait_ge(pe_slot, 2 * i + s - 1)
                    split_slot(2 * i + s, s, i + 1)

        @block.tensor
        def _(pe):
            mm = nc.tensor.matmul

            def dot3(dst, w_hi, w_lo, a_hi, a_lo, first, last):
                mm(dst, w_hi, a_hi, start=first, stop=False)
                mm(dst, w_hi, a_lo, start=False, stop=False)
                return mm(dst, w_lo, a_hi, start=False, stop=last)

            def gemm_tile(t, b, a_hi, a_lo, width, fresh=None, among=None, s0=0):
                pe.wait_ge(w_split, t + 1)
                for k in range(KT):
                    if fresh is not None:
                        pe.wait_ge(h_lo_done, KT * fresh + k + 1)
                    for c in range(0, width, HALF):
                        w = min(HALF, width)
                        last = dot3(gp[b][:, c:c + w], whi[b][:, k, :], wlo[b][:, k, :],
                                    a_hi[:, k, c:c + w], a_lo[:, k, c:c + w], k == 0, k == KT - 1)
                        if k == KT - 1 and c + w == width:
                            last.then_inc(pe_slot, 1)
                        if among is not None:
                            among(s0 + 2 * k + c // HALF)

            def token_sums(dst, src):
                for n in range(NB):
                    last = mm(dst[:, n:n + 1], ck(src, n), ones[:, 0:1], start=True, stop=True)
                return last

            def spread(dst, cols):
                for n in range(NB):
                    last = mm(ck(dst, n), cols[:, n:n + 1].broadcast_to([P, P]), ident, start=True, stop=True)
                return last

            def norm_sum(j, width=S):
                pe.wait_ge(sq_added, KT * (j + 1))
                src = N[:, 2, :] if j != NMEM else H[:, 1, 0:N_MEM]
                for c in range(2):
                    w = width // 2
                    last = mm(pa[:, c * w:c * w + w], ones, src[:, c * w:c * w + w], start=True, stop=True)
                last.then_inc(norm_mm, 1)

            def sums(dst, src, done):
                for c in range(2):
                    last = mm(dst[:, c * HALF:(c + 1) * HALF], ones, src[:, c * HALF:(c + 1) * HALF],
                              start=True, stop=True)
                last.then_inc(done, 1)

            def turn8(dst, src, done):
                for n in range(NB):
                    last = nc.tensor.transpose(ck(dst, n), ck(src, n), ident)
                last.then_inc(done, 1)

            pe.wait_ge(const_loaded, 80)
            norm_sum(NMIX)
            for h in range(RET):
                for j in range(4):
                    t = T_RET + 4 * h + j
                    if t >= 2:
                        pe.wait_ge(ev_act, t - 1)
                    gemm_tile(t, t % 2, hhi, hlo, S, HMIX if t == 0 else None)
                pe.wait_ge(roped, 2 * h + 2)
                if h == 0:
                    pe.wait_ge(norm_root, 1)
                else:
                    pe.wait_ge(y_root, h)
                turn8(pa, H[:, 1, :], ret_turned)
                pe.wait_ge(ev_act, 4 * h + 3)
                turn8(pb, H[:, 2, :], ret_turned)
                pe.wait_ge(ret_kz, h + 1)
                for n in range(NB):
                    last = mm(ck(pa, n), ck(H[:, 1, :], n), ck(H[:, 0, :], n), start=True, stop=True)
                last.then_inc(ret_scores, 1)
                pe.wait_ge(ret_v, h + 1)
                for n in range(NB - 1):
                    last = mm(ck(pb, n), ck(X4(5), n), ck(X4(0), n), start=True, stop=True)
                last.then_inc(ret_kv, 1)
                pe.wait_ge(ret_probs, h + 1)
                pe.wait_ge(ret_states, h + 1)
                for n in range(NB):
                    last = mm(ck(pa, n), ck(X4(0), n), ck(X4(1), n), start=True, stop=(n == 0))
                    if n:
                        last = mm(ck(pa, n), ck(X4(2), n), ck(X4(4), n), start=False, stop=True)
                last.then_inc(ret_out, 1)
                pe.wait_ge(y_squared, h + 1)
                sums(pb, X4(3), y_sums)
            for g in range(4):
                t = T_RET + 4 * RET + g
                pe.wait_ge(ev_act, t - 1)
                gemm_tile(t, t % 2, hhi, hlo, S)
                pe.wait_ge(pool_in, g + 1)
                if g:
                    pe.wait_ge(pool_y, g)
                for c in range(2):
                    last = mm(pa[:, c * HALF:(c + 1) * HALF], poolw[:, g, :],
                              X[:, 3 * (PAD + S) + c * HALF:3 * (PAD + S) + (c + 1) * HALF], start=True, stop=True)
                last.then_inc(pool_mm, 1)
            pe.wait_ge(ev_act, T_WOUT)
            for m in range(KT):
                t = T_WOUT + m
                if m >= 2:
                    pe.wait_ge(ev_dve, m - 1)
                gemm_tile(t, t % 2, hhi, hlo, S, HRET if m == 0 else None)
                if m == 0:
                    norm_sum(NMEM, N_MEM)
            pe.wait_ge(ev_dve, KT)
            pe.wait_ge(norm_root, 2)
            norm_sum(NXA)
            pe.wait_ge(h_lo_done, KT * (HMEM + 1))
            for m in range(2 * KT):
                t = T_MEM + m
                if m >= 2:
                    pe.wait_ge(ev_act, EV_MEM + m - 1)
                gemm_tile(t, t % 2, mem_hi, mem_lo, N_MEM)
            pe.wait_ge(ev_act, EV_MEM + 2 * KT)
            for b in range(2):
                for k in range(KT):
                    last = nc.tensor.transpose(ck(ps[b][:, :], k),
                                               H[:, 2:4, :].rearrange("p a (k m) -> p (a k) m", m=N_MEM)[:, k, b * P:(b + 1) * P],
                                               ident)
                last.then_inc(mem_turned, 1)
            for h in range(XA_HEADS):
                for j in range(2):
                    t = T_XQ + 2 * h + j
                    pe.wait_ge(ev_act, EV_XQ + 2 * h + j - 1)
                    gemm_tile(t, t % 2, hhi, hlo, S, HXA if h == j == 0 else None)
                pe.wait_ge(mem_v, 2)
                pe.wait_ge(ev_act, EV_XQ + 2 * h + 2)
                for f in range(2):
                    u = 2 * h + f
                    if u:
                        pe.wait_ge(xa_y, u)
                    for q in range(4):
                        for j in range(2):
                            last = mm(pa[:, q * N_MEM:(q + 1) * N_MEM], ck(H[:, j, :], 4 * f + q),
                                      Nf[:, (2 * h + j) * N_MEM:(2 * h + j + 1) * N_MEM], start=(j == 0), stop=(j == 1))
                    last.then_inc(xa_scores, 1)
                    pe.wait_ge(xa_probs, u + 1)
                    for b in range(2):
                        for q in range(4):
                            last = nc.tensor.transpose(pb[:, b * HALF + q * P:b * HALF + (q + 1) * P],
                                                       H[:, 2, q * N_MEM + b * P:q * N_MEM + (b + 1) * P], ident)
                    last.then_inc(xa_turned, 1)
                    pe.wait_ge(xa_pt, u + 1)
                    for d in range(2):
                        for b in range(2):
                            at = 2 * S + b * D + h * XA_DH + d * P
                            last = mm(pa[:, d * HALF:(d + 1) * HALF], Nf[:, at:at + P], H[:, 3, b * HALF:(b + 1) * HALF],
                                      start=(b == 0), stop=(b == 1))
                    last.then_inc(xa_out, 1)
            pe.wait_ge(ev_act, EV_XQ + KT)
            for m in range(KT):
                t = T_XO + m
                if m >= 2:
                    pe.wait_ge(ev_dve, KT + m - 1)
                gemm_tile(t, t % 2, hhi, hlo, S, HXO if m == 0 else None)
            pe.wait_ge(xa_y, 8)
            norm_sum(NFF)
            def up_at(i):
                for q in range(4):
                    pe.wait_ge(ev_act, 4 * i + (EV_FF + q - 1))
                    gemm_tile(6 * i + (T_FF - 2 + q), q % 2, hhi, hlo, S)

            def down_at(i, b, t0):
                for a in range(2):
                    t = t0 + a
                    pe.wait_ge(w_split, t + 1)
                    for q in range(4):
                        m = 4 * a + q
                        if a == q == 0:
                            pe.wait_ge(act_lo_done, 2 * i + 2)
                        if not (isinstance(i, int) and 8 * i + m < 2):
                            pe.wait_ge(down_ev, 8 * i + (m - 1))
                        for k in range(2):
                            for c in range(2):
                                last = dot3(ps[m % 2][:, c * HALF:(c + 1) * HALF], whi[a][:, 2 * q + k, :], wlo[a][:, 2 * q + k, :],
                                            act_hi[:, 2 * b + k, c * HALF:(c + 1) * HALF],
                                            act_lo[:, 2 * b + k, c * HALF:(c + 1) * HALF], k == 0, k == 1)
                        last.then_inc(pe_slot if q == 3 else down_mm, 1)

            pe.wait_ge(ev_dve, 2 * KT)
            for q in range(4):
                if q >= 2:
                    pe.wait_ge(ev_act, EV_FF + q - 1)
                gemm_tile(T_FF + q, q % 2, hhi, hlo, S, HFF if q == 0 else None)
            pe.wait_ge(norm_root, NFF + 1)
            up_at(1)
            down_at(0, 0, T_FF + 8)
            up_at(2)
            down_at(1, 1, T_FF + 14)
            with pe.Fori(1, FF_STEPS // 2) as r:
                for b in range(2):
                    up_at(2 * r + b + 1)
                    down_at(2 * r + b, b, 12 * r + (6 * b + T_FF + 8))
            down_at(FF_STEPS - 1, (FF_STEPS - 1) % 2, T_GDN - 2)
            pe.wait_ge(down_ev, 8 * FF_STEPS)
            norm_sum(NFIN)
            pe.wait_ge(norm_root, NFIN + 1)
            norm_sum(NGDN)
            pe.wait_ge(norm_root, NGDN + 1)

            def narrow(c0, c1, fresh, done):
                pe.wait_ge(small_split, 1)
                pe.wait_ge(h_lo_done, KT * (fresh + 1))
                w = c1 - c0
                for n in range(NB):
                    for k in range(KT):
                        last = dot3(pa[:, n * w:(n + 1) * w], hhi[:, k, n * P:(n + 1) * P], hlo[:, k, n * P:(n + 1) * P],
                                    small_hi[:, k, c0:c1], small_lo[:, k, c0:c1], k == 0, k == KT - 1)
                last.then_inc(done, 1)

            narrow(0, N_AB, HGDN, ab_mm)
            pe.wait_ge(ab_ready, 1)
            mm(pb[:, 0:64], triu, tiny[:, 5, :], start=True, stop=True)
            mm(pb[:, 64:128], ones, tiny[:, 5, :], start=True, stop=True).then_inc(gc_mm, 1)

            NL = len(LEVELS)

            def even(ap, b):
                return ap.rearrange("p (a two b) -> p a two b", two=2, b=b)[:, :, 0, :]

            def gdn_chunk(g, n, step):
                u, k = NB * g + n, H[:, g % 2, :]
                if step == 0 and n:
                    pe.wait_ge(ch_s, u)
                    mm(pa[:, 0:P], ck(k, n), state[:, :], start=True, stop=True).then_inc(ch_ks, 1)
                if step == 1:
                    pe.wait_ge(ch_r, u + 1)
                    mm(pa[:, HALF:HALF + P], ck(TT, n), rhs_r[:, :], start=True, stop=True).then_inc(ch_vn_mm, 1)
                    if n:
                        mm(ck(pb, n), state[:, :], ck(N[:, 1, :], n), start=True, stop=False)
                if step == 2:
                    pe.wait_ge(ch_vn, u + 1)
                    mm(ck(pb, n), v_new[:, :], ck(AT, n), start=(n == 0), stop=True)
                    mm(pa[:, P:2 * P], ck(N[:, 2, :], n), v_new[:, :], start=True, stop=True).then_inc(ch_s_mm, 1)

            def gdn_rule(g, s):
                q, k = yt[:, g, :], H[:, g % 2, :]
                if s == 0:
                    pe.wait_ge(gd_qk, 2 * g + 2)
                    for n in range(NB):
                        col = n * GDN + g
                        last = mm(ck(pa, n), tiny[:, 5, col:col + 1].broadcast_to([P, P]), triu, start=True, stop=True)
                    last.then_inc(gd_gr, 1)
                    for n in range(NB):
                        col = n * GDN + g
                        last = mm(ck(pb, n), tiny[:, 6, col:col + 1].broadcast_to([P, P]), ident, start=True, stop=True)
                    last.then_inc(gd_br, 1)
                if s == 6:
                    pe.wait_ge(gd_exp, 2 * g + 2)
                    for n in range(NB):
                        last = mm(ck(pa, n), ck(k, n), ck(k, n), start=True, stop=True)
                    last.then_inc(gd_kk, 1)
                if s == 7:
                    pe.wait_ge(gd_mt1, g + 1)
                    for n in range(NB):
                        last = mm(ck(pb, n), ck(k, n), ck(q, n), start=True, stop=True)
                    last.then_inc(gd_attn_mm, 1)
                if s == 9:
                    pe.wait_ge(gd_mt, g + 1)
                    turn8(pa, k, gd_kturn)
                if s == 10:
                    pe.wait_ge(gd_silu, 3 * g + 3)
                    pe.wait_ge(gd_attn, g + 1)
                    turn8(pb, V_RAW, gd_vturn)
                if s == 12:
                    pe.wait_ge(gd_kdec, g + 1)
                    pe.wait_ge(gd_t0, g + 1)
                    turn8(pa, TT, gd_tturn)
                for l, b in enumerate(LEVELS):
                    if s == 17 + 3 * l:
                        if l:
                            pe.wait_ge(inv_t, NL * g + l)
                        else:
                            pe.wait_ge(gd_ti, g + 1)
                        for n in range(NB):
                            last = mm(pa[:, n * 64:n * 64 + 64], ck(MT, n), even(ck(TI, n), b), start=True, stop=True)
                        last.then_inc(inv_x_mm, 1)
                    if s == 18 + 3 * l:
                        pe.wait_ge(inv_x, NL * g + l + 1)
                        if l:
                            pe.wait_ge(inv_tt, NL * g + l)
                        for n in range(NB):
                            last = mm(pa[:, HALF + n * 64:HALF + n * 64 + 64], ck(TT, n), XB[:, n * 64:n * 64 + 64],
                                      start=True, stop=True)
                        last.then_inc(inv_y_mm, 1)
                    if s == 20 + 3 * l:
                        pe.wait_ge(inv_t, NL * g + l + 1)
                        if l:
                            pe.wait_ge(inv_tt, NL * g + l)
                        elif g:
                            pe.wait_ge(y_done, Y_GDN + g)
                        turn8(pb, TI, inv_turn)
                if s == 36:
                    pe.wait_ge(inv_tt, NL * (g + 1))
                if s >= 37 and (s - 37) // 3 < NB:
                    gdn_chunk(g, (s - 37) // 3, (s - 37) % 3)

            def gdn_among(w):
                g, h = w - 1, w

                def at(s):
                    if 0 <= g < GDN:
                        gdn_rule(g, s)
                    if g >= 1 and s == 13:
                        pe.wait_ge(y_squared, Y_GDN + g)
                        if g < GDN:
                            pe.wait_ge(gd_vb, g + 1)
                        token_sums(pb[:, 0:NB], N[:, 0, :]).then_inc(go_ss, 1)
                    if g >= 1 and s == 15:
                        pe.wait_ge(go_rstd, g)
                        spread(pb, rn[:, 2 * NB:3 * NB]).then_inc(go_wide, 1)
                    if h < GDN and s == 61:
                        pe.wait_ge(gd_sq, 2 * h + 2)
                        if h:
                            pe.wait_ge(ch_s, NB * h)
                        else:
                            pe.wait_ge(gc_ready, 1)
                        token_sums(pa[:, 0:NB], MT)
                        token_sums(pa[:, NB:2 * NB], TI).then_inc(gd_ss, 1)
                    if h < GDN and s == 62:
                        pe.wait_ge(gd_rstd, h + 1)
                        spread(pa, rn[:, 0:NB]).then_inc(gd_wide, 1)
                        if h:
                            pe.wait_ge(gd_o, h)
                        spread(pb, rn[:, NB:2 * NB]).then_inc(gd_wide, 1)

                return at

            for w in range(GDN + 2):
                among = gdn_among(w)
                if w < GDN:
                    for j in range(4):
                        t = T_GDN + 4 * w + j
                        pe.wait_ge(ev_act, EV_GDN + 4 * w + j - 1)
                        gemm_tile(t, t % 2, hhi, hlo, S, None, among, 16 * j)
                else:
                    for s in range(64):
                        among(s)
            pe.wait_ge(ev_act, EV_GO)
            for m in range(KT):
                t = T_GO + m
                if m >= 2:
                    pe.wait_ge(ev_act, EV_GO + m - 1)
                gemm_tile(t, t % 2, hhi, hlo, S, HGO if m == 0 else None)
            pe.wait_ge(ch_s, NB * GDN)
            norm_sum(NGP)
            pe.wait_ge(norm_root, NGP + 1)
            norm_sum(NFOX)
            pe.wait_ge(norm_root, NFOX + 1)

            narrow(N_AB, N_SMALL, HFOX, f_mm)
            pe.wait_ge(f_ready, 1)
            def fox_scores(g, q):
                if q:
                    pe.wait_ge(fx_s, NB * g + q)
                else:
                    pe.wait_ge(fx_qk, 2 * g + 2)
                for c in range(0, (q + 1) * P, HALF):
                    w = min(HALF, (q + 1) * P - c)
                    last = mm(pa[:, c:c + w], ck(yt[:, g, :], q), H[:, g % 2, c:c + w], start=True, stop=True)
                last.then_inc(fx_s_mm, 1)

            def fox_turn(g, q, r):
                if r == 0:
                    pe.wait_ge(fx_p, NB * g + q + 1)
                if fox_round(g, q, r):
                    pe.wait_ge(fx_pt, fox_round(g, q, r))
                for b in range(4 * r, min(q + 1, 4 * r + 4)):
                    last = nc.tensor.transpose(ck(pb, b - 4 * r), X4(3 + q % 2)[:, b * P:(b + 1) * P], ident)
                last.then_inc(fx_turn, 1)

            def fox_out(g, q):
                pe.wait_ge(fx_pt, fox_round(g, q, q // 4) + 1)
                if q == 0:
                    pe.wait_ge(fx_v, g + 1)
                if q % 4 == 0 and (g or q):
                    pe.wait_ge(fx_y, 2 * g + q // 4)
                for b in range(q + 1):
                    last = mm(ck(pb, 4 + q % 4), ck(X4(0), b), ck(X4(5), b), start=(b == 0), stop=(b == q))
                last.then_inc(fx_o, 1)

            def fox_among(w):
                g, h = w - 1, w

                def at(s):
                    for q in range(NB):
                        if g >= 0 and q and s == 6 * q - 4:
                            fox_scores(g, q)
                        if g >= 0 and s == 6 * q + 1:
                            fox_turn(g, q, 0)
                        if g >= 0 and q >= 4 and s == 6 * q + 2:
                            fox_turn(g, q, 1)
                        if g >= 0 and s == 6 * q + 4:
                            fox_out(g, q)
                    if h == FOX:
                        return
                    if s == 48:
                        pe.wait_ge(fx_sq, 2 * h + 2)
                        if h:
                            pe.wait_ge(fx_s, NB * h)
                        token_sums(pa[:, 0:NB], N[:, 0, :])
                        token_sums(pa[:, NB:2 * NB], N[:, 1, :]).then_inc(fx_ss, 1)
                    if s == 49:
                        if h:
                            pe.wait_ge(fx_pt, fox_round(h, 0, 0))
                            pe.wait_ge(fx_y, 2 * h)
                        for n in range(NB):
                            col = n * FOX + h
                            last = mm(ck(pb, n), tiny[:, 11, col:col + 1].broadcast_to([P, P]), triu, start=True, stop=True)
                        last.then_inc(fx_c_mm, 1)
                    if s == 51:
                        pe.wait_ge(fx_rstd, h + 1)
                        spread(pa, rn[:, 0:NB]).then_inc(fx_wide, 1)
                    if s == 53:
                        pe.wait_ge(ev_act, EV_FOX + 4 * h + 3)
                        pe.wait_ge(fx_c, h + 1)
                        turn8(pb, X4(6), fx_vturn)
                    if s == 56:
                        pe.wait_ge(fx_qk, 2 * h + 1)
                        spread(pa, rn[:, NB:2 * NB]).then_inc(fx_wide, 1)
                    if s == 60:
                        fox_scores(h, 0)

                return at

            for w in range(FOX + 1):
                among = fox_among(w)
                if w < FOX:
                    for j in range(4):
                        t = T_FOX + 4 * w + j
                        pe.wait_ge(ev_act, EV_FOX + 4 * w + j - 1)
                        gemm_tile(t, t % 2, hhi, hlo, S, None, among, 16 * j)
                else:
                    for s in range(64):
                        among(s)
            for m in range(KT):
                t = T_FO + m
                if m >= 2:
                    pe.wait_ge(ev_act, EV_FO + m - 1)
                gemm_tile(t, t % 2, hhi, hlo, S, HFO if m == 0 else None)
            norm_sum(NFP)

        @block.scalar
        def _(act):
            A = nc.scalar.activation
            steps = [0]

            def done(ins):
                steps[0] += 1
                ins.then_inc(act_step, 1)

            def settle():
                act.wait_ge(act_step, steps[0])

            def square(j, k, src):
                n = KT * j + k
                if n >= 2:
                    act.wait_ge(sq_added, n - 1)
                dst = N[:, k % 2, :] if j != NMEM else H[:, 0, (k % 2) * N_MEM:(k % 2 + 1) * N_MEM]
                A(dst, src, ACT.Square).then_inc(sq_ready, 1)

            def root(j, width=S):
                act.wait_ge(norm_mm, j + 1)
                dst = N[:, 3, :] if j != NMEM else H[:, 1, N_MEM:2 * N_MEM]
                A(dst, pa[:, 0:width], ACT.Sqrt, bias=eps[:, 0:1], scale=1.0 / D).then_inc(norm_root, 1)

            def hi_parts(p, srcs, dst, waits=None, free=None):
                for k in range(KT):
                    if k == 0 and free is not None:
                        act.wait_ge(pe_slot, free)
                    if waits is not None:
                        act.wait_ge(waits[0], waits[1] + k)
                    A(dst[:, k, :], srcs(k), ACT.Copy).then_inc(h_hi_done, 1)

            def evac(t, ev, dst, b, func=ACT.Copy, width=S):
                act.wait_ge(pe_slot, t + 1)
                A(dst, gp[b][:, 0:width], func).then_inc(ev_act, 1)

            def nt(k):
                return N[:, k % 2, :]

            act.wait_ge(eps_set, 1)
            act.wait_ge(const_loaded, 80)
            for k in range(KT):
                act.wait_ge(x_loaded[k], 16)
                square(NMIX, k, xres[:, k, :])
            root(NMIX)
            hi_parts(HMIX, nt, hhi, (norm_scaled, 1))
            act.wait_ge(angles, 1)
            A(X4(6)[0:64, :], X4(6)[0:64, :], ACT.Sin, scale=-1.0)
            A(X4(6)[64:P, :], X4(6)[64:P, :], ACT.Sin)
            A(X4(7), X4(7), ACT.Sin).then_inc(rope_tab, 1)
            for h in range(RET):
                for j in range(4):
                    t = T_RET + 4 * h + j
                    if j == 0 and h:
                        act.wait_ge(y_done, h)
                    if j < 2:
                        act.wait_ge(pe_slot, t + 1)
                        A(H[:, j, :], gp[t % 2][:, :], ACT.Copy)
                        A(X4(j)[0:64, :], gp[t % 2][64:P, :], ACT.Copy)
                        A(X4(j)[64:P, :], gp[t % 2][0:64, :], ACT.Copy).then_inc(ev_act, 1)
                    else:
                        evac(t, t, H[:, j, :], t % 2, ACT.Copy if j == 2 else ACT.Silu)
                act.wait_ge(ret_turned, 2 * h + 1)
                A(X4(5), pa, ACT.Copy, scale=cn("zeta", h, 1)).then_inc(ret_kz, 1)
                act.wait_ge(ret_out, h + 1)
                done(A(X4(5), pa, ACT.Copy))
                settle()
                A(X4(3), X4(5), ACT.Square).then_inc(y_squared, 1)
                act.wait_ge(y_sums, h + 1)
                A(N[:, 2, :], pb, ACT.Sqrt, bias=eps[:, 0:1], scale=1.0 / RET_DH).then_inc(y_root, 1)
            for g in range(4):
                t = T_RET + 4 * RET + g
                act.wait_ge(pads_zero, 1)
                if g:
                    act.wait_ge(pool_in, g)
                evac(t, t, X[:, PAD:PAD + S], t % 2)
                act.wait_ge(pool_mm, g + 1)
                A(yt[:, 4 + g, :], pa, ACT.Copy, scale=vc("pool_scale", g)).then_inc(pool_y, 1)
            act.wait_ge(y_done, RET)
            act.wait_ge(pool_y, 4)
            hi_parts(HRET, lambda k: yt[:, k, :], hhi, None, T_WOUT)
            act.wait_ge(h_lo_done, KT * (HRET + 1))
            act.dma_start(memx[:, :, :], mem_t).then_inc(mem_loaded, 16)
            for k in range(KT):
                act.dma_start(xres[:, k, :], x_t[k]).then_inc(x_loaded[k], 16)
            act.wait_ge(mem_loaded, 16)
            for k in range(KT):
                square(NMEM, k, memx[:, k, :])
            root(NMEM, N_MEM)
            hi_parts(HMEM, lambda k: H[:, 0, (k % 2) * N_MEM:(k % 2 + 1) * N_MEM], mem_hi, (norm_scaled, KT + 1))
            for m in range(KT):
                act.wait_ge(ev_dve, m + 1)
                square(NXA, m, xres[:, m, :])
            root(NXA)
            hi_parts(HXA, nt, hhi, (norm_scaled, 2 * KT + 1), T_MEM)
            act.wait_ge(h_lo_done, KT * (HXA + 1))
            for m in range(2 * KT):
                dst = Nf[:, m * N_MEM:(m + 1) * N_MEM] if m < KT else \
                    H[:, 2:4, :].rearrange("p a (k m) -> p (a k) m", m=N_MEM)[:, m - KT, :]
                evac(T_MEM + m, 0, dst, m % 2, ACT.Copy, N_MEM)
            for b in range(2):
                act.wait_ge(mem_turned, b + 1)
                A(N[:, 2 + b, :], ps[b][:, :], ACT.Copy).then_inc(mem_v, 1)
            for h in range(XA_HEADS):
                for j in range(2):
                    if h:
                        act.wait_ge(xa_scores, 2 * h)
                    evac(T_XQ + 2 * h + j, 0, H[:, j, :], j)
                for f in range(2):
                    u = 2 * h + f
                    act.wait_ge(xa_max, u + 1)
                    if u:
                        act.wait_ge(xa_turned, u)
                    else:
                        act.wait_ge(mem_turned, 2)
                    for q in range(4):
                        last = A(H[:, 2, q * N_MEM:(q + 1) * N_MEM], pa[:, q * N_MEM:(q + 1) * N_MEM], ACT.Exp,
                                 bias=stat[:, 4 + q:5 + q], scale=XA_DH ** -0.5, accum_out=stat[:, 8 + q:9 + q])
                    last.then_inc(xa_exp, 1)
                    act.wait_ge(xa_turned, u + 1)
                    A(H[:, 3, :], pb, ACT.Copy).then_inc(xa_pt, 1)
                    act.wait_ge(xa_out, u + 1)
                    for d in range(2):
                        last = A(yt[:, 2 * h + d, f * HALF:(f + 1) * HALF], pa[:, d * HALF:(d + 1) * HALF], ACT.Copy)
                    last.then_inc(xa_y, 1)
            act.wait_ge(xa_y, 8)
            hi_parts(HXO, lambda k: yt[:, k, :], hhi, None, T_XO)
            for m in range(KT):
                act.wait_ge(ev_dve, KT + m + 1)
                square(NFF, m, xres[:, m, :])
            root(NFF)
            hi_parts(HFF, nt, hhi, (norm_scaled, 3 * KT + 1), T_FF)
            act.wait_ge(h_lo_done, KT * (HFF + 1))
            act.wait_ge(pads_zero, 2)

            def up(i, b, t0, first):
                for j in range(2):
                    for v in range(2):
                        q = 2 * j + v
                        act.wait_ge(pe_slot, t0 + (q + 1))
                        if not (first and j == 0):
                            act.wait_ge(ff_conv, 4 * i + (q - 1))
                        A(Nf[:, v * FP + 2:v * FP + 2 + S], gp[v][:, :], ACT.Copy).then_inc(ev_act, 1)
                    act.wait_ge(ff_conv, 4 * i + (2 * j + 1))
                    A(H[:, 2 * j, :], H[:, 2 * j, :], ACT.Silu).then_inc(ff_gate, 1)
                    if j == 0 and not (isinstance(i, int) and i < 2):
                        act.wait_ge(pe_slot, 6 * i + (T_FF - 2))
                    act.wait_ge(ff_prod, 2 * i + (j + 1))
                    A(act_hi[:, 2 * b + j, :], H[:, 2 * j, :], ACT.Copy).then_inc(act_hi_done, 1)

            up(0, 0, T_FF, True)
            up(1, 1, T_FF + 4, False)
            with act.Fori(1, FF_STEPS // 2) as r:
                for b in range(2):
                    up(2 * r + b, b, 12 * r + (6 * b + T_FF - 2), False)
            up(FF_STEPS - 1, 0, T_FF + 6 * (FF_STEPS - 1) - 2, False)
            for m in range(KT):
                act.wait_ge(down_ev, 8 * (FF_STEPS - 1) + m + 1)
                square(NFIN, m, xres[:, m, :])
            root(NFIN)
            for k in range(KT):
                act.wait_ge(norm_scaled, 4 * KT + k + 1)
                square(NGDN, k, xres[:, k, :])
            root(NGDN)
            hi_parts(HGDN, nt, hhi, (norm_scaled, 5 * KT + 1), T_GDN)
            act.wait_ge(h_lo_done, KT * (HGDN + 1))
            for k in range(KT):
                act.dma_start(x_spill[k], xres[:, k, :]).then_inc(spilled, 16)
            act.wait_ge(ab_mm, 1)
            A(tiny[:, 0:2, :], pa[:, 0:NB * N_AB].rearrange("p (n c) -> p n c", c=64), ACT.Copy).then_inc(ab_out, 1)
            act.wait_ge(ab_e, 1)
            done(A(tiny[:, 3, :], tiny[:, 3, :], ACT.Exp, scale=-1.0))
            done(A(tiny[:, 6, :], tiny[:, 6, :], ACT.Exp, scale=-1.0))
            done(A(row[:, 0:GDN], row[:, 0:GDN], ACT.Exp))
            settle()
            A(tiny[:, 3, :], tiny[:, 3, :], ACT.Ln, bias=1.0).then_inc(ab_e, 1)
            act.wait_ge(gc_mm, 1)
            A(tiny[:, 7, :], pb[:, 0:64], ACT.Copy)
            A(tiny[:, 8, :], pb[:, 64:128], ACT.Copy).then_inc(gc_out, 1)
            act.wait_ge(gc_diff, 1)
            A(tiny[:, 9, :], tiny[:, 9, :], ACT.Exp)
            A(tiny[:, 8, :], tiny[:, 8, :], ACT.Exp)
            A(tiny[:, 10, :], tiny[:, 7, :], ACT.Exp).then_inc(gc_out, 1)
            NL = len(LEVELS)

            def gdn_tile(h, j):
                t, n = T_GDN + 4 * h + j, 3 * h + j
                if j == 3:
                    if h >= 2:
                        act.wait_ge(y_done, Y_GDN + h - 1)
                    evac(t, 0, H[:, 2 + h % 2, :], t % 2, ACT.Silu)
                    return
                act.wait_ge(pe_slot, t + 1)
                if n >= 2:
                    act.wait_ge(gd_conv, n - 1)
                else:
                    act.wait_ge(pads_zero, 3)
                if j == 1 and h >= 2:
                    act.wait_ge(ch_s_mm, NB * (h - 1))
                if j == 2 and h:
                    act.wait_ge(gd_vturn, h)
                A((GP0, GP1)[n % 2][:, 3:3 + S], gp[t % 2][:, :], ACT.Copy)
                A(gdn_dst(h, j), gp[t % 2][:, :], ACT.Copy, scale=vc("gdn_w", (3 * 3 + j) * GDN + h)).then_inc(ev_act, 1)

            def gdn_silu(h, j):
                act.wait_ge(gd_conv, 3 * h + j + 1)
                A(gdn_dst(h, j), gdn_dst(h, j), ACT.Silu).then_inc(gd_silu, 1)

            for w in range(GDN + 2):
                g, h = w - 1, w
                for s in range(65):
                    if h < GDN and s in (16, 32, 48, 64):
                        gdn_tile(h, s // 16 - 1)
                    if g >= 1 and s == 13:
                        act.wait_ge(go_ss, g)
                        A(rn[:, 2 * NB:3 * NB], pb[:, 0:NB], ACT.Sqrt, bias=eps[:, 0:1], scale=1.0 / GDN_DK).then_inc(go_root, 1)
                    if 0 <= g < GDN:
                        if s == 0:
                            act.wait_ge(gd_diff, g + 1)
                            A(TI, TI, ACT.Exp).then_inc(gd_exp, 1)
                            A(N[:, 1, :], pa, ACT.Exp).then_inc(gd_exp, 1)
                        if s == 9:
                            act.wait_ge(gd_kturn, g + 1)
                            for n in range(NB):
                                col = n * GDN + g
                                last = A(ck(N[:, 2, :], n), ck(pa, n), ACT.Copy, scale=tiny[:, 9, col:col + 1])
                            last.then_inc(gd_kdec, 1)
                        if s == 10:
                            act.wait_ge(gd_vturn, g + 1)
                            for n in range(NB):
                                col = n * GDN + g
                                last = A(ck(N[:, 3, :], n), ck(pb, n), ACT.Copy, scale=tiny[:, 6, col:col + 1])
                            last.then_inc(gd_vb, 1)
                        if s == 12:
                            act.wait_ge(gd_tturn, g + 1)
                            A(TI, pa, ACT.Copy).then_inc(gd_ti, 1)
                        if s >= 20 and (s - 20) % 3 == 0 and (s - 20) // 3 < NL:
                            l = (s - 20) // 3
                            act.wait_ge(inv_turn, NL * g + l + 1)
                            act.wait_ge(inv_y_mm, NL * g + l + 1)
                            A(TT, pb, ACT.Copy).then_inc(inv_tt, 1)
                        if s >= 38 and (s - 38) % 3 == 0 and (s - 38) // 3 < NB:
                            u = NB * g + (s - 38) // 3
                            act.wait_ge(ch_vn_mm, u + 1)
                            if u:
                                act.wait_ge(ch_s_mm, u)
                            A(v_new[:, :], pa[:, HALF:HALF + P], ACT.Copy).then_inc(ch_vn, 1)
                        if s == 61:
                            act.wait_ge(ch_s_mm, NB * (g + 1))
                            A(yt[:, g, :], pb, ACT.Copy).then_inc(gd_o, 1)
                    if h < GDN:
                        if s == 27:
                            gdn_silu(h, 0)
                        if s == 38:
                            gdn_silu(h, 1)
                        if s == 41:
                            act.wait_ge(gd_silu, 3 * h + 2)
                            if h:
                                act.wait_ge(inv_turn, NL * h)
                            for j in range(2):
                                A((MT, TI)[j], gdn_dst(h, j), ACT.Square).then_inc(gd_sq, 1)
                        if s == 56:
                            gdn_silu(h, 2)
                        if s == 61:
                            act.wait_ge(gd_ss, h + 1)
                            if h:
                                act.wait_ge(gd_wide, 2 * h)
                            A(rn[:, 0:2 * NB], pa[:, 0:2 * NB], ACT.Sqrt, bias=eps[:, 0:1]).then_inc(gd_root, 1)
                    if 0 <= g < GDN and s == 62:
                        act.wait_ge(gd_o, g + 1)
                        if g:
                            act.wait_ge(go_ss, g)
                        A(N[:, 0, :], yt[:, g, :], ACT.Square).then_inc(y_squared, 1)
            act.wait_ge(y_done, Y_GDN + GDN)
            hi_parts(HGO, lambda k: yt[:, k, :], hhi, None, T_GO)
            act.wait_ge(h_lo_done, KT * (HGO + 1))
            act.wait_ge(spilled, 16 * KT)
            for k in range(KT):
                act.dma_start(xres[:, k, :], x_spill[k]).then_inc(x_loaded[k], 16)
            for m in range(KT):
                evac(T_GO + m, 0, yt[:, m, :], m % 2)
                act.wait_ge(ev_act, EV_GO + m + 1)
                square(NGP, m, yt[:, m, :])
            root(NGP)
            for k in range(KT):
                act.wait_ge(ev_dve, 2 * KT + k + 1)
                square(NFOX, k, xres[:, k, :])
            root(NFOX)
            hi_parts(HFOX, nt, hhi, (norm_scaled, 7 * KT + 1), T_FOX)
            act.wait_ge(h_lo_done, KT * (HFOX + 1))
            for k in range(KT):
                act.dma_start(x_spill[k], xres[:, k, :]).then_inc(spilled, 16)
            act.wait_ge(f_mm, 1)
            A(tiny[:, 0, :], pa[:, 0:64], ACT.Copy).then_inc(f_out, 1)
            act.wait_ge(f_e, 1)
            done(A(tiny[:, 3, :], tiny[:, 3, :], ACT.Exp, scale=-1.0))
            settle()
            A(tiny[:, 3, :], tiny[:, 3, :], ACT.Ln, bias=1.0).then_inc(f_e, 1)
            for w in range(FOX + 1):
                g, h = w - 1, w
                for s in range(65):
                    if h < FOX and s in (16, 32, 48, 64):
                        j = s // 16 - 1
                        t = T_FOX + 4 * h + j
                        if j == 0:
                            if h >= 2:
                                act.wait_ge(fx_s_mm, NB * (h - 1))
                            evac(t, 0, H[:, h % 2, :], t % 2)
                        elif j == 1:
                            evac(t, 0, yt[:, h, :], t % 2)
                        elif j == 2:
                            if h:
                                act.wait_ge(fx_vturn, h)
                            else:
                                act.wait_ge(spilled, 2 * 16 * KT)
                            evac(t, 0, X4(6), t % 2)
                        else:
                            if h >= 2:
                                act.wait_ge(fx_y, 2 * (h - 1))
                            evac(t, 0, H[:, 2 + h % 2, :], t % 2, ACT.Silu)
                        if j < 2:
                            act.wait_ge(ev_act, EV_FOX + 4 * h + j + 1)
                            if h:
                                act.wait_ge(fx_ss, h)
                            A(N[:, j, :], (H[:, h % 2, :], yt[:, h, :])[j], ACT.Square).then_inc(fx_sq, 1)
                    if h < FOX and s == 48:
                        act.wait_ge(fx_ss, h + 1)
                        if h:
                            act.wait_ge(fx_wide, 2 * h)
                        A(rn[:, 0:2 * NB], pa[:, 0:2 * NB], ACT.Sqrt, bias=eps[:, 0:1], scale=1.0 / FOX_D).then_inc(fx_root, 1)
                    if h < FOX and s == 53:
                        act.wait_ge(fx_vturn, h + 1)
                        if h:
                            act.wait_ge(fx_o, NB * h)
                        A(X4(0), pb, ACT.Copy).then_inc(fx_v, 1)
                    for q in range(NB):
                        z = 4 * (q % 2)
                        if g >= 0 and s == max(6 * q - 3, 0):
                            sc = X4(3 + q % 2)[:, 0:(q + 1) * P]
                            act.wait_ge(fx_s, NB * g + q + 1)
                            A(sc, sc, ACT.Exp, bias=stat[:, 14 + z:15 + z], accum_out=stat[:, 15 + z:16 + z]).then_inc(fx_exp, 1)
                        for r in range(q // 4 + 1):
                            if g >= 0 and s == 6 * q + 1 + r:
                                act.wait_ge(fx_turn, fox_round(g, q, r) + 1)
                                if r == 0 and g + q:
                                    act.wait_ge(fx_o, NB * g + q)
                                n = min(q + 1 - 4 * r, 4) * P
                                A(X4(5)[:, r * HALF:r * HALF + n], pb[:, 0:n], ACT.Copy).then_inc(fx_pt, 1)
            act.wait_ge(fx_y, 2 * FOX)
            hi_parts(HFO, lambda k: yt[:, k, :], hhi, None, T_FO)
            act.wait_ge(h_lo_done, KT * (HFO + 1))
            act.wait_ge(spilled, 2 * 16 * KT)
            for k in range(KT):
                act.dma_start(xres[:, k, :], x_spill[k]).then_inc(x_loaded[k], 16)
            for m in range(KT):
                evac(T_FO + m, 0, yt[:, m, :], m % 2)
                act.wait_ge(ev_act, EV_FO + m + 1)
                square(NFP, m, yt[:, m, :])
            root(NFP)
            for k in range(KT):
                act.wait_ge(out_ready, k + 1)
                act.dma_start(out[k], xres[:, k, :]).then_inc(stored, 16)
            act.wait_ge(stored, 16 * KT)

        @block.vector
        def _(dve):
            V = nc.vector
            steps = [0]

            def done(ins):
                steps[0] += 1
                ins.then_inc(dve_step, 1)

            def settle():
                dve.wait_ge(dve_step, steps[0])

            def add_square(j, k):
                n = KT * j + k
                wide = j != NMEM
                ssq = N[:, 2, :] if wide else H[:, 1, 0:N_MEM]
                src = N[:, k % 2, :] if wide else H[:, 0, (k % 2) * N_MEM:(k % 2 + 1) * N_MEM]
                dve.wait_ge(sq_ready, n + 1)
                if k == 0:
                    if j:
                        dve.wait_ge(norm_mm, j)
                    V.tensor_copy(ssq, src).then_inc(sq_added, 1)
                else:
                    dve.wait_ge(sq_added, n)
                    V.tensor_tensor(ssq, ssq, src, ALU.add).then_inc(sq_added, 1)

            def rstd(j):
                dve.wait_ge(norm_root, j + 1)
                r = N[:, 3, :] if j != NMEM else H[:, 1, N_MEM:2 * N_MEM]
                done(V.reciprocal(r, r))
                settle()

            def lo_part(p, k, src, dst_hi, dst_lo):
                dve.wait_ge(h_hi_done, KT * p + k + 1)
                V.tensor_tensor(dst_lo[:, k, :], src, dst_hi[:, k, :].bitcast(F32), ALU.subtract).then_inc(h_lo_done, 1)

            def norm_to_h(j, p, c, src, gain, dst_hi, dst_lo):
                rstd(j)
                wide = j != NMEM
                r = N[:, 3, :] if wide else H[:, 1, N_MEM:2 * N_MEM]

                def t(k):
                    return N[:, k % 2, :] if wide else H[:, 0, (k % 2) * N_MEM:(k % 2 + 1) * N_MEM]

                for k in range(KT):
                    if k >= 2:
                        dve.wait_ge(h_lo_done, KT * p + k - 1)
                    if gain is None:
                        V.tensor_tensor(t(k), src(k), r, ALU.mult).then_inc(norm_scaled, 1)
                    else:
                        V.scalar_tensor_tensor(t(k), src(k), vc(gain, k), r, ALU.mult, ALU.mult).then_inc(norm_scaled, 1)
                    if k:
                        lo_part(p, k - 1, t(k - 1), dst_hi, dst_lo)
                lo_part(p, KT - 1, t(KT - 1), dst_hi, dst_lo)

            def xt(k):
                return xres[:, k, :]

            dve.wait_ge(const_loaded, 80)
            for k in range(KT):
                add_square(NMIX, k)
            norm_to_h(NMIX, HMIX, 0, xt, "mix_g", hhi, hlo)
            dve.wait_ge(pos_loaded, 16)
            done(V.tensor_copy(X4(5), H[:, 3, :].bitcast(I32)))
            settle()
            done(V.tensor_scalar(X4(5), X4(5), cn("inv_freq", 0, 1), None, ALU.mult))
            settle()
            for dst, shift in ((X4(6), 0.0), (X4(7), 0.25)):
                done(V.tensor_scalar(X4(4), X4(5), 1.0 / (2 * math.pi), shift, ALU.mult, ALU.add))
                settle()
                done(V.tensor_scalar(X4(4), X4(4), ROUND_MAGIC, ROUND_MAGIC, ALU.add, ALU.subtract))
                settle()
                done(V.scalar_tensor_tensor(dst, X4(4), -TWO_PI_HI, X4(5), ALU.mult, ALU.add))
                settle()
                for part in (TWO_PI_MID, TWO_PI_LO):
                    done(V.scalar_tensor_tensor(dst, X4(4), -part, dst, ALU.mult, ALU.add))
                    settle()
                done(V.tensor_scalar(dst, dst, shift * 2 * math.pi, math.pi, ALU.add, ALU.min))
                settle()
                if shift:
                    V.tensor_scalar(dst, dst, -math.pi, None, ALU.max).then_inc(angles, 1)
                else:
                    done(V.tensor_scalar(dst, dst, -math.pi, None, ALU.max))
                    settle()
            dve.wait_ge(rope_tab, 1)
            for h in range(RET):
                for j in range(2):
                    scale = 1.0 if j == 0 else RET_DH ** -0.5
                    dve.wait_ge(ev_act, 4 * h + j + 1)
                    if h and j == 0:
                        dve.wait_ge(ret_out, h)
                    done(V.scalar_tensor_tensor(X4(2), H[:, j, :], scale, X4(7), ALU.mult, ALU.mult))
                    done(V.scalar_tensor_tensor(X4(3), X4(j), scale, X4(6), ALU.mult, ALU.mult))
                    settle()
                    V.tensor_tensor(H[:, j, :], X4(2), X4(3), ALU.add).then_inc(roped, 1)
                    dve.wait_ge(roped, 2 * h + j + 1)
                    if j == 0:
                        done(V.tensor_tensor(chunks(X4(4)), chunks(H[:, 0, :]), over(cn("xi", h), NB), ALU.mult))
                dve.wait_ge(ret_turned, 2 * h + 2)
                V.tensor_copy(X4(0), pb).then_inc(ret_v, 1)
                dve.wait_ge(ret_scores, h + 1)
                V.tensor_tensor(chunks(X4(1)), chunks(pa), over(cn("dmat", h), NB), ALU.mult).then_inc(ret_probs, 1)
                dve.wait_ge(ret_kv, h + 1)
                for n in range(NB - 1):
                    if n == 0:
                        done(V.tensor_copy(ck(X4(2), 1), ck(pb, 0)))
                    else:
                        settle()
                        last = V.scalar_tensor_tensor(ck(X4(2), n + 1), ck(X4(2), n), RET_DECAY[h], ck(pb, n), ALU.mult, ALU.add)
                        if n < NB - 2:
                            done(last)
                last.then_inc(ret_states, 1)
                dve.wait_ge(y_root, h + 1)
                done(V.reciprocal(N[:, 2, :], N[:, 2, :]))
                settle()
                done(V.scalar_tensor_tensor(X4(5), X4(5), vc("gn_g", h), N[:, 2, :], ALU.mult, ALU.mult))
                dve.wait_ge(ev_act, 4 * h + 4)
                settle()
                V.tensor_tensor(yt[:, h, :], X4(5), H[:, 3, :], ALU.mult).then_inc(y_done, 1)
            W = PAD + S
            U, B, C, DD = X[:, 0:W], X[:, W:2 * W], X[:, 2 * W:3 * W], X[:, 3 * W:3 * W + S]
            dve.wait_ge(y_done, RET)
            for i in range(2):
                V.memset((U, B)[i][:, 0:PAD], 0.0)
            V.memset(C[:, 0:PAD], 0.0).then_inc(pads_zero, 1)
            dve.wait_ge(pads_zero, 1)
            for g, win in enumerate(POOL_WINDOWS):
                dve.wait_ge(ev_act, 4 * RET + g + 1)
                if g:
                    dve.wait_ge(pool_mm, g)
                src, dst = U, B
                step = 1
                while step < win:
                    done(V.tensor_tensor(dst[:, PAD:], src[:, PAD:], src[:, PAD - step:W - step], ALU.add))
                    settle()
                    src, dst = dst, (C if dst is B else B)
                    step *= 2
                done(V.scalar_tensor_tensor(DD[:, PAD:], src[:, 2 * PAD:], 1.0 / win, U[:, 2 * PAD:], ALU.mult, ALU.subtract))
                done(V.tensor_tensor(DD[:, 0:PAD], src[:, PAD:2 * PAD], cn("pool_rcnt", g, PAD), ALU.mult))
                settle()
                V.tensor_tensor(DD[:, 0:PAD], DD[:, 0:PAD], U[:, PAD:2 * PAD], ALU.subtract).then_inc(pool_in, 1)
            for k in range(KT):
                lo_part(HRET, k, yt[:, k, :], hhi, hlo)
            for k in range(KT):
                add_square(NMEM, k)
            norm_to_h(NMEM, HMEM, KT, lambda k: memx[:, k, :], "mem_g", mem_hi, mem_lo)

            def residual(t0, ev0, j):
                for m in range(KT):
                    dve.wait_ge(pe_slot, t0 + m + 1)
                    if ev0 == 0:
                        dve.wait_ge(x_loaded[m], 32)
                    V.tensor_tensor(xres[:, m, :], gp[m % 2][:, :], xres[:, m, :], ALU.add).then_inc(ev_dve, 1)
                    if m:
                        add_square(j, m - 1)
                add_square(j, KT - 1)

            residual(T_WOUT, 0, NXA)
            norm_to_h(NXA, HXA, 2 * KT, xt, "xa_g", hhi, hlo)
            for u in range(2 * XA_HEADS):
                dve.wait_ge(xa_scores, u + 1)
                done(V.tensor_reduce(stat[:, 0:4], pa.rearrange("p (q m) -> p q m", m=N_MEM), AX_X, ALU.max))
                settle()
                V.tensor_scalar(stat[:, 4:8], stat[:, 0:4], -(XA_DH ** -0.5), None, ALU.mult).then_inc(xa_max, 1)
                dve.wait_ge(xa_exp, u + 1)
                done(V.reciprocal(stat[:, 8:12], stat[:, 8:12]))
                settle()
                p3 = H[:, 2, :].rearrange("p (q m) -> p q m", m=N_MEM)
                r3 = stat[:, 8:12].rearrange("p (q a) -> p q a", a=1).broadcast_to([P, 4, N_MEM])
                V.tensor_tensor(p3, p3, r3, ALU.mult).then_inc(xa_probs, 1)
            for k in range(KT):
                lo_part(HXO, k, yt[:, k, :], hhi, hlo)
            residual(T_XO, KT, NFF)
            norm_to_h(NFF, HFF, 3 * KT, xt, "ffn_g", hhi, hlo)
            dve.wait_ge(h_lo_done, KT * (HFF + 1))
            V.memset(Nf[:, 0:2], 0.0)
            V.memset(Nf[:, FP:FP + 2], 0.0).then_inc(pads_zero, 1)

            def conv(i, j, v, cols):
                q = 2 * j + v
                a = Nf[:, v * FP:(v + 1) * FP]
                c = H[:, q, :]
                at = lambda name, n: vec[:, cols(name, n)]
                dve.wait_ge(ev_act, 4 * i + (EV_FF + q + 1))
                if not (isinstance(i, int) and i == 0):
                    dve.wait_ge(act_lo_done, 2 * i + (j - 1))
                V.tensor_scalar(c, a[:, 2:2 + S], at("ff_w", 2 * 2 * PAIRS + q), at("ff_b", q), ALU.mult, ALU.add).then_inc(ff_taps, 1)
                dve.wait_ge(ff_taps, 8 * i + (2 * q + 1))
                V.scalar_tensor_tensor(c, a[:, 1:1 + S], at("ff_w", 2 * PAIRS + q), c, ALU.mult, ALU.add).then_inc(ff_taps, 1)
                dve.wait_ge(ff_taps, 8 * i + (2 * q + 2))
                V.scalar_tensor_tensor(c, a[:, 0:S], at("ff_w", q), c, ALU.mult, ALU.add).then_inc(ff_conv, 1)

            def product(i, j):
                dve.wait_ge(ff_gate, 2 * i + (j + 1))
                dve.wait_ge(ff_conv, 4 * i + (2 * j + 2))
                V.tensor_tensor(H[:, 2 * j, :], H[:, 2 * j, :], H[:, 2 * j + 1, :], ALU.mult).then_inc(ff_prod, 1)

            def act_low(i, b, j):
                dve.wait_ge(act_hi_done, 2 * i + (j + 1))
                V.tensor_tensor(act_lo[:, 2 * b + j, :], H[:, 2 * j, :], act_hi[:, 2 * b + j, :].bitcast(F32),
                                ALU.subtract).then_inc(act_lo_done, 1)

            def down_add(i, t0, m):
                a, q = m // 4, m % 4
                if q == 3:
                    dve.wait_ge(pe_slot, t0 + (a + 1))
                else:
                    dve.wait_ge(down_mm, 6 * i + (3 * a + q + 1))
                V.tensor_tensor(xres[:, m, :], ps[m % 2][:, :], xres[:, m, :], ALU.add).then_inc(down_ev, 1)

            def cols_of(i):
                def cols(name, n):
                    at = 4 * i + (VEC_AT[name] + n)
                    return slice(at, at + 1) if isinstance(at, int) else bass.ds(at, 1)
                return cols

            def ff_step(i, b, t_down):
                cols = cols_of(i)
                conv(i, 0, 0, cols)
                conv(i, 0, 1, cols)
                product(i, 0)
                conv(i, 1, 0, cols)
                act_low(i, b, 0)
                conv(i, 1, 1, cols)
                for m in range(2):
                    down_add(i - 1, t_down, m)
                product(i, 1)
                down_add(i - 1, t_down, 2)
                down_add(i - 1, t_down, 3)
                act_low(i, b, 1)
                for m in range(4, KT):
                    down_add(i - 1, t_down, m)

            cols = cols_of(0)
            for j in range(2):
                conv(0, j, 0, cols)
                conv(0, j, 1, cols)
                product(0, j)
                act_low(0, 0, j)
            ff_step(1, 1, T_FF + 8)
            with dve.Fori(1, FF_STEPS // 2) as r:
                for b in range(2):
                    ff_step(2 * r + b, b, 12 * r + (6 * b + T_FF + 2))
            ff_step(FF_STEPS - 1, 0, T_FF + 6 * (FF_STEPS - 1) + 2)
            for m in range(KT):
                down_add(FF_STEPS - 1, T_GDN - 2, m)
                if m:
                    add_square(NFIN, m - 1)
            add_square(NFIN, KT - 1)
            rstd(NFIN)
            for k in range(KT):
                V.scalar_tensor_tensor(xres[:, k, :], xres[:, k, :], vc("final_g", k), N[:, 3, :], ALU.mult,
                                       ALU.mult).then_inc(norm_scaled, 1)
                if k:
                    add_square(NGDN, k - 1)
            add_square(NGDN, KT - 1)
            norm_to_h(NGDN, HGDN, 5 * KT, xt, "gdn_g", hhi, hlo)

            def t3(i):
                return tiny[:, i, :].rearrange("p (n h) -> p n h", h=8)

            ab = tiny[:, 0:2, :].rearrange("p a c -> p (a c)").rearrange("p (n c) -> p n c", c=N_AB)
            dve.wait_ge(ab_out, 1)

            def bias_row(at):
                return row[:, at:at + 8].rearrange("p (a h) -> p a h", a=1).broadcast_to([P, NB, 8])

            done(V.tensor_tensor(t3(2), ab[:, :, 0:GDN], bias_row(GDN), ALU.add))
            done(V.tensor_copy(t3(6), ab[:, :, GDN:N_AB]))
            settle()
            V.scalar_tensor_tensor(tiny[:, 3, :], tiny[:, 2, :], -1.0, tiny[:, 2, :], ALU.mult, ALU.max).then_inc(ab_e, 1)
            dve.wait_ge(ab_e, 2)
            done(V.scalar_tensor_tensor(tiny[:, 4, :], tiny[:, 2, :], 0.0, tiny[:, 3, :], ALU.max, ALU.add))
            done(V.tensor_scalar(tiny[:, 6, :], tiny[:, 6, :], 1.0, None, ALU.add))
            settle()
            done(V.reciprocal(tiny[:, 6, :], tiny[:, 6, :]))
            settle()
            V.scalar_tensor_tensor(t3(5), t3(4), -1.0, bias_row(0), ALU.mult, ALU.mult).then_inc(ab_ready, 1)
            dve.wait_ge(gc_out, 1)
            V.tensor_tensor(tiny[:, 9, :], tiny[:, 8, :], tiny[:, 7, :], ALU.subtract).then_inc(gc_diff, 1)
            dve.wait_ge(gc_out, 2)
            V.scalar_tensor_tensor(tiny[:, 10, :], tiny[:, 10, :], -1.0, tiny[:, 6, :], ALU.mult, ALU.mult).then_inc(gc_ready, 1)
            dve.wait_ge(gc_ready, 1)
            dve.wait_ge(spilled, 16 * KT)
            V.memset(GP0[:, 0:3], 0.0)
            V.memset(GP1[:, 0:3], 0.0).then_inc(pads_zero, 1)
            NL = len(LEVELS)

            def even(ap, b):
                return ap.rearrange("p (a two b) -> p a two b", two=2, b=b)[:, :, 0, :]

            def tap(h, j, i):
                n, c = 3 * h + j, gdn_dst(h, j)
                if i == 2:
                    dve.wait_ge(ev_act, EV_GDN + 4 * h + j + 1)
                settle()
                last = V.scalar_tensor_tensor(c, (GP0, GP1)[n % 2][:, i:i + S], vc("gdn_w", (i * 3 + j) * GDN + h), c,
                                              ALU.mult, ALU.add)
                if i:
                    done(last)
                else:
                    last.then_inc(gd_conv, 1)

            def gdn_rule(g, s):
                if s == 0:
                    dve.wait_ge(gd_gr, g + 1)
                    for n in range(NB):
                        col = n * GDN + g
                        last = V.tensor_scalar(ck(TI, n), ck(pa, n), tiny[:, 7, col:col + 1], 0.0, ALU.subtract, ALU.min)
                    last.then_inc(gd_diff, 1)
                    dve.wait_ge(gd_exp, 2 * g + 1)
                    dve.wait_ge(gd_br, g + 1)
                    V.tensor_tensor(MT, TI, pb, ALU.mult).then_inc(gd_mt1, 1)
                    done(V.tensor_tensor(chunks(AT), chunks(TI), over(cn("causal"), NB), ALU.mult))
                if s == 6:
                    dve.wait_ge(gd_kk, g + 1)
                    dve.wait_ge(gd_mt1, g + 1)
                    V.tensor_tensor(MT, pa, MT, ALU.mult).then_inc(gd_mt, 1)
                if s == 7:
                    dve.wait_ge(gd_attn_mm, g + 1)
                    settle()
                    V.tensor_tensor(AT, pb, AT, ALU.mult).then_inc(gd_attn, 1)
                if s == 8:
                    dve.wait_ge(gd_mt, g + 1)
                    done(V.tensor_tensor(chunks(TT), chunks(MT), over(cn("pair_t"), NB), ALU.mult))
                    settle()
                    V.tensor_tensor(chunks(TT), chunks(TT), over(ident, NB), ALU.add).then_inc(gd_t0, 1)
                if s == 9:
                    dve.wait_ge(gd_exp, 2 * g + 2)
                    done(V.tensor_tensor(N[:, 1, :], N[:, 1, :], yt[:, g, :], ALU.mult))
                for l, b in enumerate(LEVELS):
                    if s == 17 + 3 * l:
                        dve.wait_ge(inv_x_mm, NL * g + l + 1)
                        mask = cn("levels", l, P // 2).rearrange("p (a c) -> p a c", a=1).broadcast_to([P, NB, P // 2])
                        V.tensor_tensor(XB.rearrange("p (n c) -> p n c", c=P // 2),
                                        pa[:, 0:HALF].rearrange("p (n c) -> p n c", c=P // 2), mask, ALU.mult).then_inc(inv_x, 1)
                    if s == 18 + 3 * l:
                        dve.wait_ge(inv_y_mm, NL * g + l + 1)
                        if l:
                            dve.wait_ge(inv_turn, NL * g + l)
                        V.tensor_tensor(even(TI, b), even(TI, b), pa[:, HALF:S].rearrange("p (a b) -> p a b", b=b),
                                        ALU.subtract).then_inc(inv_t, 1)
                        dve.wait_ge(inv_t, NL * g + l + 1)
                if s >= 37 and (s - 37) // 3 < NB:
                    n = (s - 37) // 3
                    u, col = NB * g + n, n * GDN + g
                    if (s - 37) % 3 == 0:
                        if u:
                            dve.wait_ge(ch_vn_mm, u)
                        if n == 0:
                            dve.wait_ge(gd_vb, g + 1)
                            V.tensor_copy(rhs_r[:, :], ck(N[:, 3, :], 0)).then_inc(ch_r, 1)
                        else:
                            dve.wait_ge(ch_ks, (NB - 1) * g + n)
                            V.scalar_tensor_tensor(rhs_r[:, :], pa[:, 0:P], tiny[:, 10, col:col + 1], ck(N[:, 3, :], n), ALU.mult,
                                                   ALU.add).then_inc(ch_r, 1)
                    if (s - 37) % 3 == 2:
                        dve.wait_ge(ch_s_mm, u + 1)
                        if n == 0:
                            V.tensor_copy(state[:, :], pa[:, P:2 * P]).then_inc(ch_s, 1)
                        else:
                            dve.wait_ge(ch_s, u)
                            V.scalar_tensor_tensor(state[:, :], state[:, :], tiny[:, 8, col:col + 1], pa[:, P:2 * P], ALU.mult,
                                                   ALU.add).then_inc(ch_s, 1)

            for w in range(GDN + 2):
                g, h = w - 1, w
                for s in range(64):
                    if 0 <= g < GDN:
                        gdn_rule(g, s)
                    if g >= 1 and s == 13:
                        dve.wait_ge(go_root, g)
                        V.reciprocal(rn[:, 2 * NB:3 * NB], rn[:, 2 * NB:3 * NB]).then_inc(go_rstd, 1)
                    if g >= 1 and s == 15:
                        o = yt[:, g - 1, :]
                        dve.wait_ge(go_wide, g)
                        done(V.scalar_tensor_tensor(o, o, vc("o_g", 0), pb, ALU.mult, ALU.mult))
                        dve.wait_ge(ev_act, EV_GDN + 4 * g)
                        settle()
                        V.tensor_tensor(o, o, H[:, 2 + (g - 1) % 2, :], ALU.mult).then_inc(y_done, 1)
                    if h >= GDN:
                        continue
                    if s in (19, 22, 25):
                        tap(h, 0, (25 - s) // 3)
                    if s in (34, 36, 37):
                        tap(h, 1, 2 - (34, 36, 37).index(s))
                    if s in (49, 52, 55):
                        tap(h, 2, (55 - s) // 3)
                    if s == 61:
                        dve.wait_ge(gd_root, h + 1)
                        V.reciprocal(rn[:, 0:2 * NB], rn[:, 0:2 * NB]).then_inc(gd_rstd, 1)
                    if s == 62:
                        for j in range(2):
                            dve.wait_ge(gd_wide, 2 * h + j + 1)
                            V.scalar_tensor_tensor(gdn_dst(h, j), gdn_dst(h, j), GDN_DK ** -0.5 if j == 0 else 1.0,
                                                   ps[j][:, :], ALU.mult, ALU.mult).then_inc(gd_qk, 1)
            for k in range(KT):
                lo_part(HGO, k, yt[:, k, :], hhi, hlo)
            for m in range(KT):
                add_square(NGP, m)

            def post(j, gain, signal, reload):
                rstd(j)
                for k in range(KT):
                    dve.wait_ge(x_loaded[k], reload)
                    V.scalar_tensor_tensor(yt[:, k, :], yt[:, k, :], vc(gain, k), N[:, 3, :], ALU.mult, ALU.mult).then_inc(norm_scaled, 1)
                    dve.wait_ge(norm_scaled, KT * j + k + 1)
                    V.tensor_tensor(xres[:, k, :], xres[:, k, :], yt[:, k, :], ALU.add).then_inc(signal, 1)
                    if j == NGP and k:
                        add_square(NFOX, k - 1)

            post(NGP, "gdn_post_g", ev_dve, 48)
            add_square(NFOX, KT - 1)
            norm_to_h(NFOX, HFOX, 7 * KT, xt, None, hhi, hlo)
            dve.wait_ge(f_out, 1)
            done(V.tensor_tensor(t3(2), t3(0), bias_row(N_AB), ALU.add))
            settle()
            V.scalar_tensor_tensor(tiny[:, 3, :], tiny[:, 2, :], -1.0, tiny[:, 2, :], ALU.mult, ALU.max).then_inc(f_e, 1)
            dve.wait_ge(f_e, 2)
            V.scalar_tensor_tensor(tiny[:, 11, :], tiny[:, 2, :], 0.0, tiny[:, 3, :], ALU.min, ALU.subtract).then_inc(f_ready, 1)
            dve.wait_ge(spilled, 2 * 16 * KT)
            done(V.tensor_scalar(stat[:, 24:25], vc("qn_g", 0), FOX_D ** -0.5, None, ALU.mult))
            settle()
            def fox_max(g, q):
                u = NB * g + q
                z = 4 * (q % 2)
                sc = X4(3 + q % 2)
                dve.wait_ge(fx_s_mm, u + 1)
                if u >= 2:
                    dve.wait_ge(fx_turn, fox_round((u - 2) // NB, (u - 2) % NB, (u - 2) % NB // 4) + 1)
                last = q * P
                done(V.tensor_tensor_reduce(out=sc[:, last:last + P], in0=pa[:, last:last + P], in1=ck(X4(2), q), scale=1.0,
                                            scalar=-MASKED, op0=ALU.subtract, op1=ALU.max, accum_out=stat[:, 12 + z:13 + z]))
                settle()
                if q:
                    done(V.tensor_tensor_reduce(out=sc[:, 0:last], in0=pa[:, 0:last], in1=X4(1)[:, 0:last], scale=1.0,
                                                scalar=stat[:, 12 + z:13 + z], op0=ALU.subtract, op1=ALU.max,
                                                accum_out=stat[:, 13 + z:14 + z]))
                    settle()
                m = 13 + z if q else 12 + z
                V.tensor_scalar(stat[:, 14 + z:15 + z], stat[:, m:m + 1], -1.0, None, ALU.mult).then_inc(fx_s, 1)

            def fox_rescale(g, q):
                z = 4 * (q % 2)
                dve.wait_ge(fx_exp, NB * g + q + 1)
                done(V.reciprocal(stat[:, 15 + z:16 + z], stat[:, 15 + z:16 + z]))
                settle()
                p = X4(3 + q % 2)[:, 0:(q + 1) * P]
                V.tensor_scalar(p, p, stat[:, 15 + z:16 + z], None, ALU.mult).then_inc(fx_p, 1)

            def fox_gate(g, f):
                cols = slice(f * HALF, (f + 1) * HALF)
                dve.wait_ge(fx_o, NB * g + 4 * f + 4)
                dve.wait_ge(ev_act, EV_FOX + 4 * g + 4)
                V.tensor_tensor(yt[:, g, cols], pb[:, HALF:S], H[:, 2 + g % 2, cols], ALU.mult).then_inc(fx_y, 1)

            for w in range(FOX + 1):
                g, h = w - 1, w
                for s in range(64):
                    for q in range(NB):
                        if g >= 0 and q and s == 6 * q - 4:
                            fox_max(g, q)
                        if g >= 0 and s == max(6 * q - 2, 0):
                            fox_rescale(g, q)
                        if g >= 0 and q % 4 == 3 and s == 6 * q + 4:
                            fox_gate(g, q // 4)
                    if h == FOX:
                        continue
                    if s == 48:
                        dve.wait_ge(fx_root, h + 1)
                        V.reciprocal(rn[:, 0:2 * NB], rn[:, 0:2 * NB]).then_inc(fx_rstd, 1)
                    if s == 49:
                        dve.wait_ge(fx_c_mm, h + 1)
                        done(V.tensor_copy(ck(X4(1), 0), ck(pb, 0)))
                        for n in range(1, NB):
                            settle()
                            done(V.tensor_scalar(ck(X4(1), n), ck(pb, n), X4(1)[:, n * P - 1:n * P], None, ALU.add))
                        settle()
                        V.tensor_tensor(chunks(X4(2)), chunks(X4(1)), over(cn("future"), NB), ALU.add).then_inc(fx_c, 1)
                        dve.wait_ge(fx_c, h + 1)
                    if s in (51, 56):
                        j = (51, 56).index(s)
                        dve.wait_ge(fx_wide, 2 * h + j + 1)
                        qk = (H[:, h % 2, :], yt[:, h, :])[j]
                        gain = vc("kn_g", 0) if j == 0 else stat[:, 24:25]
                        V.scalar_tensor_tensor(qk, qk, gain, pa, ALU.mult, ALU.mult).then_inc(fx_qk, 1)
                    if s == 60:
                        fox_max(h, 0)
            for k in range(KT):
                lo_part(HFO, k, yt[:, k, :], hhi, hlo)
            for m in range(KT):
                add_square(NFP, m)
            post(NFP, "fox_post_g", out_ready, 64)


def kernel(**inputs):
    from concourse import bacc
    from concourse.bass_utils import run_bass_kernel_spmd

    a = {name: np.asarray(value) for name, value in inputs.items()}

    def tiles(w):
        return w.reshape(w.shape[0] // P, P, -1, P).transpose(2, 1, 0, 3)

    def cols(v):
        return v.reshape(-1, P).T

    w_in, gdn_in = tiles(a["w_in"][0]), tiles(a["gdn_w_in_2"][0][:, :4 * D])
    kv, fox_in = tiles(a["kv_w_2"][:, :2 * D]), tiles(a["fox_w_in_2"][0])
    ff_up = tiles(a["ffn_w_up"][0]).reshape(2, PAIRS, P, KT, P).transpose(1, 0, 2, 3, 4).reshape(2 * PAIRS, P, KT, P)
    ff_down = a["ffn_w_down"][0].reshape(FF_STEPS, 2, P, 2, 4, P).transpose(0, 3, 2, 4, 1, 5).reshape(FF_STEPS, 2, P, KT, P)
    steps = [ff_up[0:4]]
    for i in range(FF_STEPS):
        steps += [ff_up[4 * (i + 1):4 * (i + 2)], ff_down[i]]
    stream = [w_in[[4 * j + h for h in range(RET_HEADS) for j in range(4)]], w_in[16:20], tiles(a["w_out"][0]),
              tiles(a["xa_wkv"][0]), tiles(a["xa_wq"][0]), tiles(a["xa_wo"][0]), *steps,
              gdn_in[[8 * j + h for h in range(GDN_HEADS) for j in range(4)]], tiles(a["gdn_w_out_2"][0])]
    for h in range(FOX_HEADS):
        stream += [kv[[h]], fox_in[[h]], kv[[8 + h]], fox_in[[8 + h]]]
    stream.append(tiles(a["fox_w_out_2"][0]))
    ff_order = [v * PAIRS + p for p in range(PAIRS) for v in range(2)]
    vecs = {"mix_g": a["mix_norm_g"], "mem_g": a["mem_norm_g"], "xa_g": a["xa_norm_g"], "ffn_g": a["ffn_norm_g"],
            "final_g": a["final_norm_g"], "gdn_g": a["gdn_pre_norm_2"], "gdn_post_g": a["gdn_post_norm_2"],
            "kv_g": a["kv_norm_2"], "fox_g": a["fox_pre_norm_2"], "fox_post_g": a["fox_post_norm_2"],
            "gn_g": a["ret_gn_g"], "pool_scale": a["pool_scale"], "o_g": a["gdn_o_norm_2"], "kn_g": a["kv_k_norm_2"],
            "qn_g": a["fox_q_norm_2"], "gdn_w": a["gdn_conv_w_2"],
            "ff_b": a["ffn_conv_b"][0].reshape(-1, P)[ff_order],
            "ff_w": a["ffn_conv_w"][0].reshape(3, -1, P)[:, ff_order]}
    arrays = {
        "w_stream": np.concatenate(stream),
        "x_t": a["x"][0].T.reshape(KT, P, S),
        "mem_t": a["mem"][0].T.reshape(KT, P, N_MEM).transpose(1, 0, 2),
        "positions": a["positions"].reshape(1, S),
        "vecs": np.concatenate([cols(vecs[name]) for name, _ in VEC_NAMES], 1),
        "rows": np.concatenate([a["gdn_a_log_2"][0], a["gdn_dt_bias_2"][0], a["kv_forget_bias_2"]]).reshape(1, N_SMALL),
        "small_w": np.concatenate([a["gdn_w_in_2"][0][:, 4 * D:], a["kv_w_2"][:, 2 * D:]], 1)
        .reshape(KT, P, N_SMALL).transpose(1, 0, 2),
        "pool_w": a["pool_w"][0].transpose(1, 0, 2),
        "consts": shape_constants(),
    }
    arrays = {name: np.ascontiguousarray(v) for name, v in arrays.items()}
    nc = bacc.Bacc("TRN2", target_bir_lowering=False, num_devices=1)
    args = [nc.dram_tensor(name, v.shape, mybir.dt.from_np(v.dtype), kind="ExternalInput").ap() for name, v in arrays.items()]
    x_spill = nc.dram_tensor("x_spill", (KT, P, S), F32, kind="Internal").ap()
    out = nc.dram_tensor("out_t", (KT, P, S), F32, kind="ExternalOutput").ap()
    build(nc, *args, x_spill, out)
    got = run_bass_kernel_spmd(nc, [arrays], core_ids=[0]).results[0]["out_t"]
    return got.reshape(D, S).T.reshape(1, S, D)
```

```python
import math
from contextlib import ExitStack

import numpy as np

import concourse.bass as bass
from concourse import mybir

F32 = mybir.dt.float32
F32R = mybir.dt.float32r
I32 = mybir.dt.int32
ALU = mybir.AluOpType
ACT = mybir.ActivationFunctionType
AX_X = mybir.AxisListType.X

P = 128
S = 1024
D = 1024
KT = D // P
HALF = 512
NB = S // P
EPS = 1e-6
N_MEM = 256
RET_HEADS, RET_DH = 4, 128
XA_HEADS, XA_DH = 4, 256
POOL_WINDOWS = (16, 8, 4, 2)
PAD = 16
D_FF = 2816
PAIRS = D_FF // P
FF_STEPS = PAIRS // 2
GDN_HEADS, GDN_DK = 8, 128
FOX_HEADS, FOX_D = 8, 128
CONV_K = 4
LEVELS = (2, 4, 8, 16, 32, 64)
MASKED = 1e30

T_RET = 0
T_WOUT = T_RET + 4 * RET_HEADS + len(POOL_WINDOWS)
MIX_OUT = [("x", 0), ("x", 1), ("x", 2)]
for _w in range(3, KT):
    MIX_OUT += [("x", _w)] + [("m", 3 * (_w - 3) + _i) for _i in range(3)]
MIX_OUT.append(("m", 2 * KT - 1))
T_XQ = T_WOUT + len(MIX_OUT)
T_XO = T_XQ + KT
T_FF = T_XO + KT
T_GDN = T_FF + 2 * PAIRS + 2 * FF_STEPS
T_GO = T_GDN + 4 * GDN_HEADS
T_FOX = T_GO + KT
T_FO = T_FOX + 4 * FOX_HEADS
T_END = T_FO + KT
EV_RET, EV_MEM = 0, T_WOUT
EV_XQ = EV_MEM + 2 * KT
EV_FF = EV_XQ + KT
EV_GDN = EV_FF + 2 * PAIRS
EV_GO = EV_GDN + 4 * GDN_HEADS
EV_FOX = EV_GO + KT
EV_FO = EV_FOX + 4 * FOX_HEADS
PART = KT - 2
GO_ORDER = [(m, k) for m in range(2) for k in range(KT - 2)] + [(m, KT - 2) for m in range(2)] + \
    [(m, k) for m in range(2, KT) for k in range(KT - 1)]
FO_ORDER = [(m, k) for m in range(KT) for k in range(KT - 1)]
FINAL = [PART, PART + 1] + list(range(PART))

VEC_NAMES = (("mix_g", KT), ("mem_g", KT), ("xa_g", KT), ("ffn_g", KT), ("final_g", KT), ("gdn_g", KT),
             ("gdn_post_g", KT), ("kv_g", KT), ("fox_g", KT), ("fox_post_g", KT), ("gn_g", RET_HEADS),
             ("pool_scale", 4), ("o_g", 1), ("kn_g", 1), ("qn_g", 1), ("ff_b", 2 * PAIRS),
             ("ff_w", 3 * 2 * PAIRS), ("gdn_w", CONV_K * 3 * GDN_HEADS), ("inv_freq", 1))
VEC_AT, _n = {}, 0
for _name, _width in VEC_NAMES:
    VEC_AT[_name] = _n
    _n += _width
VEC_COLS = _n
CONST_NAMES = (("ident", P), ("triu", P), ("ones", P), ("causal", P), ("future", P),
               ("pair_t", P), ("levels", P // 2 * len(LEVELS)), ("dmat", P * RET_HEADS),
               ("xi", P * RET_HEADS), ("zeta", RET_HEADS), ("pool_rcnt", PAD * 4))
CONST_AT, _n = {}, 0
for _name, _width in CONST_NAMES:
    CONST_AT[_name] = _n
    _n += _width
CONST_COLS = _n
N_AB = 2 * GDN_HEADS
N_SMALL = N_AB + FOX_HEADS
LOG_GAMMA = np.log1p(-np.exp2(-5.0 - np.arange(RET_HEADS)))
RET_DECAY = [float(v) for v in np.exp(LOG_GAMMA * P).astype(np.float32)]
TWO_PI_HI, TWO_PI_MID = 6.28125, 1.9340515136718750e-3
TWO_PI_LO = 2 * math.pi - TWO_PI_HI - TWO_PI_MID
ROUND_MAGIC = 1.5 * 2.0 ** 23


def shape_constants():
    i = np.arange(P)
    row, col = i[:, None], i[None, :]
    c = {"ident": row == col, "triu": row <= col, "ones": np.ones((P, P)), "causal": row <= col,
         "future": MASKED * (col > row)}
    pair = (row // 2 == col // 2) & (row % 2 == 1) & (col % 2 == 0)
    c["pair_t"] = -1.0 * pair.T
    c["levels"] = np.concatenate([((row // (2 * b) == col // (2 * b)) & (row // b % 2 == 1))[:, i // b % 2 == 0]
                                  for b in LEVELS], 1)
    c["dmat"] = np.concatenate([np.where(col >= row, np.exp(lg * np.maximum(col - row, 0)), 0.0)
                                for lg in LOG_GAMMA], 1)
    c["xi"] = np.concatenate([np.exp(lg * (col + 1.0)) * np.ones((P, 1)) for lg in LOG_GAMMA], 1)
    c["zeta"] = np.exp(LOG_GAMMA[None, :] * (P - 1 - row))
    c["pool_rcnt"] = np.concatenate([1.0 / np.minimum(np.arange(PAD) + 1, w)[None, :] * np.ones((P, 1))
                                     for w in POOL_WINDOWS], 1)
    return np.concatenate([np.asarray(c[n], np.float32) for n, _ in CONST_NAMES], 1)


def build(nc, w_stream, x_t, mem_t, positions, vecs, rows, small_w, pool_w, consts, x_spill, c_rows, out):
    ctx = ExitStack()
    with ctx:
        def sb(name, shape, dt=F32):
            return ctx.enter_context(nc.sbuf_tensor(name, shape, dt))

        def sem(name):
            return ctx.enter_context(nc.semaphore(name))

        raw = [sb(f"w_raw{i}", [P, KT, P]) for i in range(2)]
        whi = [sb(f"w_hi{i}", [P, KT, P], F32R) for i in range(2)]
        wlo = [sb(f"w_lo{i}", [P, KT, P], F32R) for i in range(2)]
        const = sb("const", [P, CONST_COLS])
        vec = sb("vec", [P, VEC_COLS])
        row = sb("row", [P, N_SMALL])
        poolw = sb("poolw", [P, 4, P])
        small_raw = sb("small_raw", [P, KT, N_SMALL])
        small_hi = sb("small_hi", [P, KT, N_SMALL], F32R)
        small_lo = sb("small_lo", [P, KT, N_SMALL], F32R)
        tiny = sb("tiny", [P, 16, 64])
        stat = sb("stat", [P, 32])
        by_head = sb("gdn_cols", [P, 2, 7, NB])
        rn = sb("rstd_cols", [P, 8 * NB])
        state = sb("state", [P, P])
        rhs_r = sb("rhs_r", [P, P])
        v_new = sb("v_new", [P, P])
        eps, unit_col = sb("eps", [P, 1]), sb("unit_col", [P, 1])
        both_g = sb("both_g", [P, KT])

        hhi = sb("h_hi", [P, KT, S], F32R)
        hlo = sb("h_lo", [P, KT, S], F32R)
        xres = sb("xres", [P, KT, S])
        H = sb("head", [P, 4, S])
        N = sb("norm", [P, 4, S])
        with nc.sbuf_tensor("yt", [P, KT, S], F32) as yt:
            pass
        with nc.sbuf_tensor("memx", [P, KT, N_MEM], F32) as memx, \
                nc.sbuf_tensor("mem_hi", [P, KT, N_MEM], F32R) as mem_hi, \
                nc.sbuf_tensor("mem_lo", [P, KT, N_MEM], F32R) as mem_lo:
            pass
        with nc.sbuf_tensor("act_hi", [P, 4, S], F32R) as act_hi, \
                nc.sbuf_tensor("act_lo", [P, 4, S], F32R) as act_lo:
            pass
        X = xres[:, :, :].rearrange("p k s -> p (k s)")
        Nf = N[:, :, :].rearrange("p k s -> p (k s)")

        def X4(i):
            return X[:, i * S:(i + 1) * S]

        GP0, GP1 = X[:, 0:S + 3], X[:, S + 3:2 * (S + 3)]
        G0 = 2 * (S + 3)
        AT, MT, TI, TT, V_RAW = [X[:, G0 + i * S:G0 + (i + 1) * S] for i in range(5)]
        XB = X[:, G0 + 5 * S:G0 + 5 * S + HALF]

        K_NORM, Q_NORM, R_K, R_Q, BETA_RK, BETA_RK2, DECAY_RK = range(7)
        R_QK, R_O = rn[:, 0:2 * NB], rn[:, 2 * NB:3 * NB]
        R_H, R_H2 = rn[:, 3 * NB:4 * NB], rn[:, 4 * NB:5 * NB]
        R_FIN, R_TMP = rn[:, 5 * NB:6 * NB], rn[:, 6 * NB:7 * NB]
        WIDE_MIX, WIDE_FF, WIDE_GDN, WIDE_FOX = N[:, 3, :], N[:, 3, :], N[:, 0, :], N[:, 3, :]

        SIN, COS = yt[:, 6, :], yt[:, 7, :]
        V_FEAT, V_TOK, K_TOK, P_TOK, STATES = [X4(i) for i in range(5)]
        SWAPPED = (X4(5), X4(6))
        W_POOL = PAD + S
        POOL_U, POOL_B = [X[:, 5 * S + i * W_POOL:5 * S + (i + 1) * W_POOL] for i in range(2)]
        POOL_C, POOLED = Nf[:, 0:W_POOL], Nf[:, W_POOL:W_POOL + S]

        FP = S + 2

        gp = [ctx.enter_context(nc.psum_tensor(f"gemm{i}", [P, S], F32)) for i in range(2)]
        ps = [ctx.enter_context(nc.psum_tensor(f"small{i}", [P, S], F32)) for i in range(2)]
        pa, pb = ps[0][:, :], ps[1][:, :]

        def cn(name, i=0, width=P):
            at = CONST_AT[name] + i * width
            return const[:, at:at + width]

        def vc(name, i):
            return vec[:, VEC_AT[name] + i:VEC_AT[name] + i + 1]

        def chunks(ap):
            return ap.rearrange("p (n c) -> p n c", c=P)

        def ck(ap, n):
            return ap[:, n * P:(n + 1) * P]

        def over(ap, n):
            return ap.rearrange("p (a c) -> p a c", a=1).broadcast_to([P, n, P])

        ident, ones, triu = cn("ident"), cn("ones"), cn("triu")

        w_loaded = [sem(f"w_loaded{i}") for i in range(2)]
        vec_loaded, const_loaded = sem("vec_loaded"), sem("const_loaded")
        x_loaded = [sem(f"x_loaded{k}") for k in range(KT)]
        mem_loaded, pos_loaded = sem("mem_loaded"), sem("pos_loaded")
        spilled, stored = sem("spilled"), sem("stored")
        w_gained, w_hi_done, w_split = sem("w_gained"), sem("w_hi_done"), sem("w_split")
        small_step, small_split = sem("small_step"), sem("small_split")
        eps_set = sem("eps_set")
        pe_slot = sem("pe_slot")
        tile_out, tile_added = sem("tile_out"), sem("tile_added")
        sq_ready, sq_added = sem("sq_ready"), sem("sq_added")
        norm_mm, norm_root, norm_scaled = sem("norm_mm"), sem("norm_root"), sem("norm_scaled")
        norm_rstd, norm_wide, wide_out = sem("norm_rstd"), sem("norm_wide"), sem("wide_out")
        post_scaled, fin_scaled = sem("post_scaled"), sem("fin_scaled")
        gd_tap3, gd_z, fx_z = sem("gd_tap3"), sem("gd_z"), sem("fx_z")
        h_hi_done, h_lo_done = sem("h_hi_done"), sem("h_lo_done")
        act_step, dve_step = sem("act_step"), sem("dve_step")
        angles, rope_tab = sem("angles"), sem("rope_tab")
        roped = sem("roped")
        ret_turned, ret_kz, ret_v = sem("ret_turned"), sem("ret_kz"), sem("ret_v")
        ret_scores, ret_probs = sem("ret_scores"), sem("ret_probs")
        ret_kv, ret_states, ret_out = sem("ret_kv"), sem("ret_states"), sem("ret_out")
        y_squared, y_sums, y_root, y_done = sem("y_squared"), sem("y_sums"), sem("y_root"), sem("y_done")
        ret_gate, y_rstd, y_wide = sem("ret_gate"), sem("y_rstd"), sem("y_wide")
        pads_zero, pool_in, pool_mm, pool_y = sem("pads_zero"), sem("pool_in"), sem("pool_mm"), sem("pool_y")
        mem_turned, mem_v = sem("mem_turned"), sem("mem_v")
        xa_scores, xa_max, xa_exp, xa_probs = sem("xa_scores"), sem("xa_max"), sem("xa_exp"), sem("xa_probs")
        xa_turned, xa_pt, xa_out, xa_y = sem("xa_turned"), sem("xa_pt"), sem("xa_out"), sem("xa_y")
        ff_taps, ff_conv, ff_gate, ff_prod = sem("ff_taps"), sem("ff_conv"), sem("ff_gate"), sem("ff_prod")
        act_hi_done, act_lo_done = sem("act_hi_done"), sem("act_lo_done")
        down_mm, down_ev = sem("down_mm"), sem("down_ev")
        ab_mm, ab_out, ab_e, ab_ready = sem("ab_mm"), sem("ab_out"), sem("ab_e"), sem("ab_ready")
        gc_mm, gc_out, gc_diff, gc_ready = sem("gc_mm"), sem("gc_out"), sem("gc_diff"), sem("gc_ready")
        gd_conv, gd_silu, gd_sq, gd_ss, gd_root = (sem("gd_conv"), sem("gd_silu"), sem("gd_sq"), sem("gd_ss"),
                                                   sem("gd_root"))
        gd_gr, gd_diff, gd_exp = sem("gd_gr"), sem("gd_diff"), sem("gd_exp")
        gd_kk, gd_mt, gd_attn_mm, gd_attn = sem("gd_kk"), sem("gd_mt"), sem("gd_attn_mm"), sem("gd_attn")
        gd_kturn, gd_kdec, gd_vturn, gd_vb = sem("gd_kturn"), sem("gd_kdec"), sem("gd_vturn"), sem("gd_vb")
        gd_t0, gd_tturn, gd_ti = sem("gd_t0"), sem("gd_tturn"), sem("gd_ti")
        gd_cols, go_scaled, gd_o = sem("gd_cols"), sem("go_scaled"), sem("gd_o")
        go_ss, go_root, go_rstd, go_wide, go_used = sem("go_ss"), sem("go_root"), sem("go_rstd"), sem("go_wide"), sem("go_used")
        inv_turn, inv_tt = sem("inv_turn"), sem("inv_tt")
        inv_x_mm, inv_x, inv_y_mm, inv_t = sem("inv_x_mm"), sem("inv_x"), sem("inv_y_mm"), sem("inv_t")
        ch_ks, ch_r, ch_vn_mm, ch_vn, ch_s_mm, ch_s = (sem("ch_ks"), sem("ch_r"), sem("ch_vn_mm"), sem("ch_vn"),
                                                       sem("ch_s_mm"), sem("ch_s"))
        f_mm, f_out, f_e, f_ready = sem("f_mm"), sem("f_out"), sem("f_e"), sem("f_ready")
        fx_sq, fx_ss, fx_root, fx_qk = sem("fx_sq"), sem("fx_ss"), sem("fx_root"), sem("fx_qk")
        fx_vturn, fx_v = sem("fx_vturn"), sem("fx_v")
        share_mm, share_added = sem("share_mm"), sem("share_added")
        c_mm, c_ready, c_out, c_moved = sem("c_mm"), sem("c_ready"), sem("c_out"), sem("c_moved")
        fx_s_mm, fx_s, fx_exp, fx_p = sem("fx_s_mm"), sem("fx_s"), sem("fx_exp"), sem("fx_p")
        fx_turn, fx_pt, fx_o, fx_y = sem("fx_turn"), sem("fx_pt"), sem("fx_o"), sem("fx_y")
        fx_rstd, fx_wide = sem("fx_rstd"), sem("fx_wide")
        out_ready = sem("out_ready")
        RET, GDN, FOX = RET_HEADS, GDN_HEADS, FOX_HEADS
        NMIX, NMEM, NXA, NFF, NFIN, NGDN, NGP, NFOX, NFP = range(9)
        S_MIX, S_FF, S_GDN, S_GP, S_FOX, S_FP = range(6)
        W_MIX, W_FF, W_GDN, W_FIN, W_GP, W_FOX, W_FP = range(7)
        HMIX, HRET, HMEM, HXA, HXO, HFF, HGDN, HGO, HFOX, HFO = range(10)
        Y_GDN = RET
        XO_EARLY = 2 * 2 * (KT - 2)
        N_GROUPS = 2 * KT * (KT - 1)
        OUT_POOL = KT - 2
        GO_LATE, FO_FROM, FO_TO = 22, 4, 58

        def go_groups(w, s):
            first, late = 4 * (KT - 2), GO_LATE
            if s < 0 or w < GDN:
                return 0 if w <= GDN else N_GROUPS - late
            if w == GDN:
                return first * min(s, 21) // 21 + (N_GROUPS - late - first) * min(max(s - 21, 0), 42) // 42
            return N_GROUPS - late + late * min(max(s - 1, 0), 13) // 13

        def fo_groups(s):
            return N_GROUPS * min(max(s - FO_FROM, 0), FO_TO - FO_FROM) // (FO_TO - FO_FROM)

        def parts_done(order, lo, hi):
            return [m for m in range(PART) if lo <= 2 * order.index((m, KT - 2)) + 1 < hi]

        def squares(j, k):
            if j == NMEM:
                return H[:, 0, (k % 2) * N_MEM:(k % 2 + 1) * N_MEM]
            return yt[:, 6 + k % 2, :] if j == NXA else N[:, k % 2, :]

        def cols_of_head(h, i, n):
            return by_head[:, h % 2, i:i + n, :].rearrange("p a n -> p (a n)")

        def gdn_dst(h, j):
            return (yt[:, h, :], H[:, h % 2, :], V_RAW)[j]

        def fox_round(g, q, r):
            return 12 * g + (q if q < 4 else 2 * q - 4) + r

        block = ctx.enter_context(nc.Block())

        @block.sync
        def _(sp):
            for t in range(2):
                sp.dma_start(raw[t][:, :, :], w_stream[t]).then_inc(w_loaded[t], 16)
                if t == 0:
                    for k in range(KT):
                        sp.dma_start(xres[:, k, :], x_t[k]).then_inc(x_loaded[k], 16)
            with sp.Fori(1, T_END // 2) as i:
                for t in range(2):
                    sp.wait_ge(w_split, 2 * i + t - 1)
                    sp.dma_start(raw[t][:, :, :], w_stream[2 * i + t]).then_inc(w_loaded[t], 16)

        @block.gpsimd
        def _(pool):
            nc.gpsimd.memset(unit_col[:, :], 1.0).then_inc(eps_set, 1)
            nc.gpsimd.memset(eps[:, :], EPS).then_inc(eps_set, 1)
            pool.dma_start(vec[:, :], vecs).then_inc(vec_loaded, 16)
            pool.dma_start(H[:, 3, :].bitcast(I32), positions.broadcast_to([P, S])).then_inc(pos_loaded, 16)
            for dst, src in ((const[:, :], consts), (row[:, :], rows.broadcast_to([P, N_SMALL])),
                             (small_raw[:, :, :], small_w), (poolw[:, :, :], pool_w)):
                pool.dma_start(dst, src).then_inc(const_loaded, 16)
            unit = unit_col[:, 0:1].rearrange("p (a b) -> p a b", a=1).broadcast_to([P, KT, P])

            def split_slot(t, s, turn):
                pool.wait_ge(w_loaded[s], 16 * turn)
                nc.gpsimd.tensor_tensor(whi[s][:, :, :], raw[s][:, :, :], unit, ALU.mult).then_inc(w_hi_done, 1)
                pool.wait_ge(w_hi_done, t + 1)
                nc.gpsimd.tensor_tensor(wlo[s][:, :, :], raw[s][:, :, :], whi[s][:, :, :].bitcast(F32),
                                        ALU.subtract).then_inc(w_split, 1)

            pool.wait_ge(eps_set, 2)
            for s in range(2):
                split_slot(s, s, 1)

            pool.wait_ge(vec_loaded, 16)
            pool.wait_ge(const_loaded, 64)
            fcols = small_raw[:, :, N_AB:N_SMALL]
            gain = vec[:, VEC_AT["kv_g"]:VEC_AT["kv_g"] + KT].rearrange("p (k a) -> p k a", a=1)
            nc.gpsimd.tensor_tensor(fcols, fcols, gain.broadcast_to([P, KT, FOX]), ALU.mult).then_inc(small_step, 1)
            pool.wait_ge(small_step, 1)
            nc.gpsimd.tensor_copy(small_hi[:, :, :], small_raw[:, :, :]).then_inc(small_step, 1)
            pool.wait_ge(small_step, 2)
            nc.gpsimd.tensor_tensor(small_lo[:, :, :], small_raw[:, :, :], small_hi[:, :, :].bitcast(F32),
                                    ALU.subtract).then_inc(small_split, 1)

            with pool.Fori(1, T_FOX // 2) as i:
                for s in range(2):
                    pool.wait_ge(pe_slot, 2 * i + s - 1)
                    split_slot(2 * i + s, s, i + 1)
            def fox_slot(i, j):
                t, s, name = T_FOX + j, j % 2, ("kv_g", "fox_g", "kv_g", "fox_g")[j]
                gain = vec[:, VEC_AT[name]:VEC_AT[name] + KT].rearrange("p (k a) -> p k a", a=1)
                pool.wait_ge(w_loaded[s], 32 * i + 16 * (t // 2 + 1))
                nc.gpsimd.tensor_tensor(raw[s][:, :, :], raw[s][:, :, :], gain.broadcast_to([P, KT, P]),
                                        ALU.mult).then_inc(w_gained, 1)
                pool.wait_ge(w_gained, 4 * i + (j + 1))
                pool.wait_ge(pe_slot, 4 * i + (t - 1))
                nc.gpsimd.tensor_tensor(whi[s][:, :, :], raw[s][:, :, :], unit, ALU.mult).then_inc(w_hi_done, 1)
                pool.wait_ge(w_hi_done, 4 * i + (t + 1))
                nc.gpsimd.tensor_tensor(wlo[s][:, :, :], raw[s][:, :, :], whi[s][:, :, :].bitcast(F32),
                                        ALU.subtract).then_inc(w_split, 1)

            def add_y(n, signal, tiles):
                for k in range(tiles):
                    pool.wait_ge(post_scaled, KT * n + k + 1)
                    nc.gpsimd.tensor_tensor(xres[:, k, :], xres[:, k, :], yt[:, k, :], ALU.add).then_inc(signal, 1)

            for j in range(4):
                if j == 2:
                    add_y(0, tile_added, KT)
                fox_slot(0, j)
            with pool.Fori(1, FOX) as i:
                for j in range(4):
                    fox_slot(i, j)
            with pool.Fori(T_FO // 2, T_END // 2) as i:
                for s in range(2):
                    pool.wait_ge(pe_slot, 2 * i + s - 1)
                    split_slot(2 * i + s, s, i + 1)
            add_y(1, out_ready, OUT_POOL)

        @block.tensor
        def _(pe):
            mm = nc.tensor.matmul

            def dot3(dst, w_hi, w_lo, a_hi, a_lo, first, last):
                mm(dst, w_hi, a_hi, start=first, stop=False)
                mm(dst, w_hi, a_lo, start=False, stop=False)
                return mm(dst, w_lo, a_hi, start=False, stop=last)

            def gemm_tile(t, b, a_hi, a_lo, width, fresh=None, among=None, s0=0):
                pe.wait_ge(w_split, t + 1)
                for k in range(KT):
                    if fresh is not None:
                        pe.wait_ge(h_lo_done, KT * fresh + k + 1)
                    for c in range(0, width, HALF):
                        w = min(HALF, width)
                        last = dot3(gp[b][:, c:c + w], whi[b][:, k, :], wlo[b][:, k, :],
                                    a_hi[:, k, c:c + w], a_lo[:, k, c:c + w], k == 0, k == KT - 1)
                        if k == KT - 1 and c + w == width:
                            last.then_inc(pe_slot, 1)
                        if among is not None:
                            among(s0 + 2 * k + c // HALF)

            def early_group(t0, prod, i, n_k=KT - 1):
                m, k, c = i // (2 * n_k), i % (2 * n_k) // 2, i % 2 * HALF
                if k == c == 0:
                    pe.wait_ge(w_split, t0 + m + 1)
                pe.wait_ge(h_lo_done, KT * prod + k + 1)
                dot3(gp[m][:, c:c + HALF], whi[m][:, k, :], wlo[m][:, k, :], hhi[:, k, c:c + HALF], hlo[:, k, c:c + HALF],
                     k == 0, False)

            def last_groups(t0, prod, m, n_k=KT - 1):
                for k in range(n_k, KT):
                    pe.wait_ge(h_lo_done, KT * prod + k + 1)
                    for c in range(0, S, HALF):
                        last = dot3(gp[m][:, c:c + HALF], whi[m][:, k, :], wlo[m][:, k, :], hhi[:, k, c:c + HALF],
                                    hlo[:, k, c:c + HALF], False, k == KT - 1)
                last.then_inc(pe_slot, 1)

            def part_groups(t0, prod, order, ev, lo, hi):
                for i in range(lo, hi):
                    slab, c = i // 2, i % 2 * HALF
                    (m, k), b = order[slab], slab // KT % 2
                    if c == 0:
                        if slab % KT == 0:
                            pe.wait_ge(w_split, t0 + slab // KT + 1)
                        if k == 0 and m >= 2:
                            pe.wait_ge(tile_out, ev + m - 1)
                        pe.wait_ge(h_lo_done, KT * prod + k + 1)
                    last = dot3(gp[m % 2][:, c:c + HALF], whi[b][:, slab % KT, :], wlo[b][:, slab % KT, :],
                                hhi[:, k, c:c + HALF], hlo[:, k, c:c + HALF], k == 0, k == KT - 2 and m < PART)
                    if c and slab % KT == KT - 1:
                        last.then_inc(pe_slot, 1)
                    if c and k == KT - 2 and m < PART:
                        last.then_inc(share_mm, 1)

            def last_shares(t0, prod, ev, n):
                pe.wait_ge(w_split, t0 + KT)
                pe.wait_ge(h_lo_done, KT * (prod + 1))
                for f, m in enumerate(FINAL):
                    if 2 <= f < 4:
                        pe.wait_ge(tile_out, ev + PART + f - 1)
                    if f >= 4:
                        pe.wait_ge(share_added, PART * n + f - 3)
                    for c in range(0, S, HALF):
                        last = dot3(gp[m % 2][:, c:c + HALF], whi[1][:, f, :], wlo[1][:, f, :], hhi[:, KT - 1, c:c + HALF],
                                    hlo[:, KT - 1, c:c + HALF], m < PART, True)
                    last.then_inc(pe_slot if f == KT - 1 else share_mm, 1)

            def token_sums(dst, src):
                for n in range(NB):
                    last = mm(dst[:, n:n + 1], ck(src, n), ones[:, 0:1], start=True, stop=True)
                return last

            def spread(dst, cols):
                for n in range(NB):
                    last = mm(ck(dst, n), cols[:, n:n + 1].broadcast_to([P, P]), ident, start=True, stop=True)
                return last

            def norm_sum(j, width=S):
                pe.wait_ge(sq_added, KT * (j + 1))
                src = N[:, 2, :] if j != NMEM else H[:, 1, 0:N_MEM]
                for c in range(2):
                    w = width // 2
                    last = mm(pa[:, c * w:c * w + w], ones, src[:, c * w:c * w + w], start=True, stop=True)
                last.then_inc(norm_mm, 1)

            def sums(dst, src, done):
                for c in range(2):
                    last = mm(dst[:, c * HALF:(c + 1) * HALF], ones, src[:, c * HALF:(c + 1) * HALF],
                              start=True, stop=True)
                last.then_inc(done, 1)

            def turn8(dst, src, done):
                for n in range(NB):
                    last = nc.tensor.transpose(ck(dst, n), ck(src, n), ident)
                last.then_inc(done, 1)

            def ret_head(g, s):
                q, k = yt[:, g, :], H[:, g % 2, :]
                if s == 0:
                    pe.wait_ge(roped, 2 * g + 2)
                    if g:
                        pe.wait_ge(y_done, g)
                    turn8(pa, k, ret_turned)
                    pe.wait_ge(tile_out, 4 * g + 3)
                    turn8(pb, V_FEAT, ret_turned)
                if s == 3:
                    pe.wait_ge(ret_kz, g + 1)
                    for n in range(NB):
                        last = mm(ck(pa, n), ck(k, n), ck(q, n), start=True, stop=True)
                    last.then_inc(ret_scores, 1)
                if s == 5:
                    pe.wait_ge(ret_v, g + 1)
                    for n in range(NB - 1):
                        last = mm(ck(pb, n), ck(K_TOK, n), ck(V_TOK, n), start=True, stop=True)
                    last.then_inc(ret_kv, 1)
                if s == 12:
                    pe.wait_ge(ret_probs, g + 1)
                    pe.wait_ge(ret_states, g + 1)
                    for n in range(NB):
                        last = mm(ck(pa, n), ck(V_TOK, n), ck(P_TOK, n), start=True, stop=(n == 0))
                        if n:
                            last = mm(ck(pa, n), ck(STATES, n), ck(N[:, 0, :], n), start=False, stop=True)
                    last.then_inc(ret_out, 1)
                if s == 17:
                    pe.wait_ge(y_squared, g + 1)
                    token_sums(pb[:, 0:NB], N[:, 1, :]).then_inc(y_sums, 1)
                if s == 19:
                    pe.wait_ge(y_rstd, g + 1)
                    spread(pb, R_O).then_inc(y_wide, 1)

            def pool_product(j):
                pe.wait_ge(pool_in, j + 1)
                if j:
                    pe.wait_ge(pool_y, j)
                for c in range(0, S, HALF):
                    last = mm(pa[:, c:c + HALF], poolw[:, j, :], POOLED[:, c:c + HALF], start=True, stop=True)
                last.then_inc(pool_mm, 1)

            def ret_among(w):
                def at(s):
                    if w == 0 and s == 28:
                        pe.wait_ge(const_loaded, 64)
                        pe.wait_ge(sq_added, KT * (NMIX + 1))
                        token_sums(pa[:, 0:NB], N[:, 2, :]).then_inc(norm_mm, 1)
                    if w == 0 and s == 31:
                        pe.wait_ge(norm_rstd, S_MIX + 1)
                        spread(pa, R_H).then_inc(norm_wide, 1)
                    if w == 1 and s == 0:
                        pe.wait_ge(wide_out, 1)
                    if w:
                        ret_head(w - 1, s)
                    if w == RET and s in (28, 44, 60):
                        pool_product(s // 16 - 1)

                return at

            for w in range(RET + 1):
                among = ret_among(w)
                for j in range(4):
                    t = T_RET + 4 * w + j
                    if t >= 2:
                        pe.wait_ge(tile_out, t - 1)
                    gemm_tile(t, t % 2, hhi, hlo, S, HMIX if t == 0 else None, among, 16 * j)

            def pool_last(s):
                if s == 2 * (KT - 1) - 1:
                    pool_product(3)

            pe.wait_ge(tile_out, T_WOUT)
            for i, (kind, m) in enumerate(MIX_OUT):
                t = T_WOUT + i
                if i >= 2:
                    kind_out, m_out = MIX_OUT[i - 2]
                    if kind_out == "x":
                        pe.wait_ge(tile_added, m_out + 1)
                    else:
                        pe.wait_ge(tile_out, EV_MEM + m_out + 1)
                if kind == "x":
                    gemm_tile(t, t % 2, hhi, hlo, S, HRET if i == 0 else None, pool_last if i == 0 else None)
                else:
                    gemm_tile(t, t % 2, mem_hi, mem_lo, N_MEM, HMEM if m == 0 else None)
                if i == 2:
                    norm_sum(NMEM, N_MEM)

            def xa_scores_of(g, f):
                u = 2 * g + f
                if u:
                    pe.wait_ge(xa_y, u)
                else:
                    pe.wait_ge(mem_v, 2)
                pe.wait_ge(tile_out, EV_XQ + 2 * g + 2)
                for q in range(4):
                    for j in range(2):
                        last = mm(pa[:, q * N_MEM:(q + 1) * N_MEM], ck(yt[:, 2 * g + j, :], 4 * f + q),
                                  Nf[:, (2 * g + j) * N_MEM:(2 * g + j + 1) * N_MEM], start=(j == 0), stop=(j == 1))
                last.then_inc(xa_scores, 1)

            def xa_turn(g, f):
                u = 2 * g + f
                pe.wait_ge(xa_probs, u + 1)
                pe.wait_ge(xa_pt, u) if u else pe.wait_ge(mem_v, 2)
                for b in range(2):
                    for q in range(4):
                        last = nc.tensor.transpose(pb[:, b * HALF + q * P:b * HALF + (q + 1) * P],
                                                   H[:, 2, q * N_MEM + b * P:q * N_MEM + (b + 1) * P], ident)
                last.then_inc(xa_turned, 1)

            def xa_out_of(g, f):
                pe.wait_ge(xa_pt, 2 * g + f + 1)
                for d in range(2):
                    for b in range(2):
                        at = 2 * S + b * D + g * XA_DH + d * P
                        last = mm(pa[:, d * HALF:(d + 1) * HALF], Nf[:, at:at + P], H[:, 3, b * HALF:(b + 1) * HALF],
                                  start=(b == 0), stop=(b == 1))
                last.then_inc(xa_out, 1)

            def xa_among(w):
                def at(s):
                    if w == 0 and s == 14:
                        pe.wait_ge(sq_added, KT * (NXA + 1))
                        token_sums(pa[:, 0:NB], H[:, 0, :]).then_inc(norm_mm, 1)
                    if w == 0 and s == 18:
                        pe.wait_ge(norm_root, NXA + 1)
                        pe.wait_ge(tile_out, EV_MEM + 2 * KT)
                        for b in range(2):
                            for k in range(KT):
                                last = nc.tensor.transpose(ck(ps[b][:, :], k),
                                                           H[:, 2:4, :].rearrange("p a (k m) -> p (a k) m", m=N_MEM)[:, k, b * P:(b + 1) * P],
                                                           ident)
                            last.then_inc(mem_turned, 1)
                    if w and s % 16 == 0:
                        xa_scores_of(w - 1, s // 16)
                    if w and s % 16 == 9:
                        xa_turn(w - 1, s // 16)
                    if w and s % 16 == 12:
                        xa_out_of(w - 1, s // 16)

                return at

            for w in range(XA_HEADS + 1):
                among = xa_among(w)
                if w < XA_HEADS:
                    for j in range(2):
                        t = T_XQ + 2 * w + j
                        pe.wait_ge(tile_out, EV_XQ + 2 * w + j - 1)
                        gemm_tile(t, t % 2, hhi, hlo, S, HXA if w == j == 0 else None, among, 16 * j)
                else:
                    pe.wait_ge(tile_out, EV_XQ + KT)
                    for s in range(32):
                        among(s)
                        if s < XO_EARLY:
                            early_group(T_XO, HXO, s, KT - 2)
            for m in range(KT):
                t = T_XO + m
                if m >= 2:
                    pe.wait_ge(tile_added, KT + m - 1)
                if m < 2:
                    last_groups(T_XO, HXO, m, KT - 2)
                else:
                    gemm_tile(t, t % 2, hhi, hlo, S)
            def up_at(i):
                for q in range(4):
                    pe.wait_ge(tile_out, 4 * i + (EV_FF + q - 1))
                    gemm_tile(6 * i + (T_FF - 2 + q), q % 2, hhi, hlo, S)

            def down_at(i, b, t0):
                for a in range(2):
                    t = t0 + a
                    pe.wait_ge(w_split, t + 1)
                    for q in range(4):
                        m = 4 * a + q
                        if a == q == 0:
                            pe.wait_ge(act_lo_done, 2 * i + 2)
                        if not (isinstance(i, int) and 8 * i + m < 2):
                            pe.wait_ge(down_ev, 8 * i + (m - 1))
                        for k in range(2):
                            for c in range(2):
                                last = dot3(ps[m % 2][:, c * HALF:(c + 1) * HALF], whi[a][:, 2 * q + k, :], wlo[a][:, 2 * q + k, :],
                                            act_hi[:, 2 * b + k, c * HALF:(c + 1) * HALF],
                                            act_lo[:, 2 * b + k, c * HALF:(c + 1) * HALF], k == 0, k == 1)
                        last.then_inc(pe_slot if q == 3 else down_mm, 1)

            pe.wait_ge(tile_added, 2 * KT)
            for q in range(4):
                if q >= 2:
                    pe.wait_ge(tile_out, EV_FF + q - 1)
                gemm_tile(T_FF + q, q % 2, hhi, hlo, S, HFF if q == 0 else None)
                if q == 1:
                    pe.wait_ge(sq_added, KT * (NFF + 1))
                    token_sums(pa[:, 0:NB], N[:, 2, :]).then_inc(norm_mm, 1)
                    pe.wait_ge(norm_rstd, S_FF + 1)
                    spread(pa, R_H).then_inc(norm_wide, 1)
            pe.wait_ge(wide_out, 2)
            up_at(1)
            down_at(0, 0, T_FF + 8)
            up_at(2)
            down_at(1, 1, T_FF + 14)
            with pe.Fori(1, FF_STEPS // 2) as r:
                for b in range(2):
                    up_at(2 * r + b + 1)
                    down_at(2 * r + b, b, 12 * r + (6 * b + T_FF + 8))
            down_at(FF_STEPS - 1, (FF_STEPS - 1) % 2, T_GDN - 2)
            pe.wait_ge(down_ev, 8 * FF_STEPS)
            def narrow(c0, c1, done):
                pe.wait_ge(small_split, 1)
                for k in range(KT):
                    for c in range(0, S, HALF):
                        last = dot3(pa[0:c1 - c0, c:c + HALF], small_hi[:, k, c0:c1], small_lo[:, k, c0:c1],
                                    hhi[:, k, c:c + HALF], hlo[:, k, c:c + HALF], k == 0, k == KT - 1)
                last.then_inc(done, 1)

            def narrow_turn(w, src, done):
                for n in range(NB):
                    last = nc.tensor.transpose(pb[:, n * w:(n + 1) * w], ck(src[0:w, :], n), ident[0:w, 0:w])
                last.then_inc(done, 1)

            def gdn_start(s):
                if s == 30:
                    pe.wait_ge(sq_added, KT * (NGDN + 1))
                    token_sums(pa[:, 0:NB], N[:, 2, :])
                    token_sums(pa[:, NB:2 * NB], N[:, 3, :]).then_inc(norm_mm, 2)
                if s == 31:
                    pe.wait_ge(norm_rstd, S_GDN + 1)
                    spread(pb, R_H).then_inc(norm_wide, 1)
                if s == 36:
                    narrow(0, N_AB, ab_mm)
                if s == 38:
                    pe.wait_ge(wide_out, 3)
                    pe.wait_ge(ab_out, 1)
                    narrow_turn(N_AB, N[:, 1, :], ab_mm)
                if s == 46:
                    pe.wait_ge(ab_ready, 1)
                    mm(pb[:, 0:64], triu, tiny[:, 5, :], start=True, stop=True)
                    mm(pb[:, 64:128], ones, tiny[:, 5, :], start=True, stop=True).then_inc(gc_mm, 1)

            NL = len(LEVELS)

            def even(ap, b):
                return ap.rearrange("p (a two b) -> p a two b", two=2, b=b)[:, :, 0, :]

            def gdn_chunk(g, n, step):
                u, k = NB * g + n, H[:, g % 2, :]
                if step == 0 and n:
                    pe.wait_ge(ch_s, u)
                    mm(pa[:, 0:P], ck(k, n), state[:, :], start=True, stop=True).then_inc(ch_ks, 1)
                if step == 1:
                    pe.wait_ge(ch_r, u + 1)
                    mm(pa[:, HALF:HALF + P], ck(TT, n), rhs_r[:, :], start=True, stop=True).then_inc(ch_vn_mm, 1)
                    if n:
                        mm(ck(pb, n), state[:, :], ck(N[:, 1, :], n), start=True, stop=False)
                if step == 2:
                    pe.wait_ge(ch_vn, u + 1)
                    mm(ck(pb, n), v_new[:, :], ck(AT, n), start=(n == 0), stop=True)
                    mm(pa[:, P:2 * P], ck(N[:, 2, :], n), v_new[:, :], start=True, stop=True).then_inc(ch_s_mm, 1)

            def gdn_rule(g, s):
                q, k = yt[:, g, :], H[:, g % 2, :]
                if s == 0:
                    pe.wait_ge(gd_root, g + 1)
                    for n in range(NB):
                        col = n * GDN + g
                        last = mm(ck(pa, n), tiny[:, 5, col:col + 1].broadcast_to([P, P]), triu, start=True, stop=True)
                    last.then_inc(gd_gr, 1)
                if s == 5:
                    pe.wait_ge(gd_silu, 3 * g + 3)
                    if g:
                        pe.wait_ge(go_scaled, g)
                    for n in range(NB):
                        last = mm(ck(pb, n), ck(k, n), ck(k, n), start=True, stop=True)
                    last.then_inc(gd_kk, 1)
                if s == 6:
                    pe.wait_ge(gd_exp, 2 * g + 2)
                    for n in range(NB):
                        last = mm(ck(pa, n), ck(k, n), ck(q, n), start=True, stop=True)
                    last.then_inc(gd_attn_mm, 1)
                if s == 8:
                    pe.wait_ge(gd_mt, g + 1)
                    turn8(pb, V_RAW, gd_vturn)
                if s == 9:
                    pe.wait_ge(gd_attn, g + 1)
                    turn8(pa, k, gd_kturn)
                if s == 11:
                    pe.wait_ge(gd_vb, g + 1)
                    pe.wait_ge(gd_t0, g + 1)
                    turn8(pb, TT, gd_tturn)
                for l, b in enumerate(LEVELS):
                    if s == 13 + 4 * l:
                        if l:
                            pe.wait_ge(inv_t, NL * g + l)
                        else:
                            pe.wait_ge(gd_ti, g + 1)
                            pe.wait_ge(gd_kdec, g + 1)
                        for n in range(NB):
                            last = mm(pa[:, n * 64:n * 64 + 64], ck(MT, n), even(ck(TI, n), b), start=True, stop=True)
                        last.then_inc(inv_x_mm, 1)
                    if s == 15 + 4 * l:
                        pe.wait_ge(inv_x, NL * g + l + 1)
                        if l:
                            pe.wait_ge(inv_tt, NL * g + l)
                        for n in range(NB):
                            last = mm(pa[:, HALF + n * 64:HALF + n * 64 + 64], ck(TT, n), XB[:, n * 64:n * 64 + 64],
                                      start=True, stop=True)
                        last.then_inc(inv_y_mm, 1)
                    if s == 17 + 4 * l:
                        pe.wait_ge(inv_t, NL * g + l + 1)
                        if l:
                            pe.wait_ge(inv_tt, NL * g + l)
                        elif g:
                            pe.wait_ge(go_used, g)
                        turn8(pb, TI, inv_turn)
                if s == 39:
                    pe.wait_ge(inv_tt, NL * (g + 1))
                if s >= 38 and (s - 38) // 3 < NB:
                    gdn_chunk(g, (s - 38) // 3, (s - 38) % 3)

            def gdn_among(w):
                g, h = w - 1, w

                def at(s):
                    if w == 0:
                        gdn_start(s)
                    if 0 <= g < GDN:
                        gdn_rule(g, s)
                    if g >= 1 and s == 14:
                        pe.wait_ge(go_rstd, g)
                        if g < GDN:
                            pe.wait_ge(gd_ti, g + 1)
                        spread(pb, R_O).then_inc(go_wide, 1)
                    if h < GDN and s == 63:
                        pe.wait_ge(gd_sq, 2 * h + 2)
                        if h:
                            pe.wait_ge(ch_s, NB * h)
                        else:
                            pe.wait_ge(gc_ready, 1)
                        token_sums(pa[:, 0:NB], TI)
                        token_sums(pa[:, NB:2 * NB], MT).then_inc(gd_ss, 1)
                    if g >= 1 and s == 2:
                        pe.wait_ge(y_squared, Y_GDN + g)
                        token_sums(pb[:, 0:NB], TT).then_inc(go_ss, 1)

                return at

            for w in range(GDN + 2):
                among = gdn_among(w)
                if w < GDN:
                    for j in range(4):
                        t = T_GDN + 4 * w + j
                        pe.wait_ge(tile_out, EV_GDN + 4 * w + j - 1)
                        gemm_tile(t, t % 2, hhi, hlo, S, HGDN if w == j == 0 else None, among, 16 * j)
                else:
                    if w == GDN:
                        pe.wait_ge(tile_out, EV_GO)
                    for s in range(64):
                        among(s)
                        part_groups(T_GO, HGO, GO_ORDER, EV_GO, go_groups(w, s - 1), go_groups(w, s))
            pe.wait_ge(go_used, GDN)
            spread(pb, R_FIN).then_inc(norm_wide, 1)
            last_shares(T_GO, HGO, EV_GO, 0)
            pe.wait_ge(sq_added, KT * (NGP + 1))
            token_sums(pa[:, 0:NB], N[:, 2, :]).then_inc(norm_mm, 1)
            pe.wait_ge(norm_rstd, S_GP + 1)
            spread(pa, R_TMP).then_inc(norm_wide, 1)

            def fox_start(s):
                if s == 30:
                    pe.wait_ge(sq_added, KT * (NFOX + 1))
                    pe.wait_ge(tile_added, 3 * KT)
                    token_sums(pa[:, 0:NB], N[:, 2, :]).then_inc(norm_mm, 1)
                if s == 31:
                    pe.wait_ge(norm_rstd, S_FOX + 1)
                    spread(pb, R_H).then_inc(norm_wide, 1)
                if s == 36:
                    narrow(N_AB, N_SMALL, f_mm)
                if s == 38:
                    pe.wait_ge(wide_out, 4)
                    pe.wait_ge(f_out, 1)
                    narrow_turn(FOX, N[:, 2, :], f_mm)
                if s == 40:
                    pe.wait_ge(f_ready, 1)
                    mm(pb[:, 0:64], triu, tiny[:, 11, :], start=True, stop=True)
                    mm(pb[:, 64:128], ones, tiny[:, 11, :], start=True, stop=True).then_inc(c_mm, 1)
                if s == 44:
                    pe.wait_ge(c_ready, 1)
                    nc.tensor.transpose(pb[0:64, 128:256], tiny[:, 13, :], ident).then_inc(c_mm, 1)

            def fox_scores(g, q):
                if q:
                    pe.wait_ge(fx_s, NB * g + q)
                else:
                    pe.wait_ge(fx_qk, g + 1)
                for c in range(0, (q + 1) * P, HALF):
                    w = min(HALF, (q + 1) * P - c)
                    last = mm(pa[:, c:c + w], ck(yt[:, g, :], q), H[:, g % 2, c:c + w], start=True, stop=True)
                last.then_inc(fx_s_mm, 1)

            def fox_turn(g, q, r):
                if r == 0:
                    pe.wait_ge(fx_p, NB * g + q + 1)
                if fox_round(g, q, r):
                    pe.wait_ge(fx_pt, fox_round(g, q, r))
                for b in range(4 * r, min(q + 1, 4 * r + 4)):
                    last = nc.tensor.transpose(ck(pb, b - 4 * r), X4(3 + q % 2)[:, b * P:(b + 1) * P], ident)
                last.then_inc(fx_turn, 1)

            def fox_out(g, q):
                pe.wait_ge(fx_pt, fox_round(g, q, q // 4) + 1)
                if q == 0:
                    pe.wait_ge(fx_v, g + 1)
                if q % 4 == 0 and (g or q):
                    pe.wait_ge(fx_y, 2 * g + q // 4)
                for b in range(q + 1):
                    last = mm(ck(pb, 4 + q % 4), ck(X4(0), b), ck(X4(5), b), start=(b == 0), stop=(b == q))
                last.then_inc(fx_o, 1)

            def fox_among(w):
                g, h = w - 1, w

                def at(s):
                    if w == 0:
                        fox_start(s)
                    for q in range(NB):
                        if g >= 0 and q and s == 6 * q - 4:
                            fox_scores(g, q)
                        if g >= 0 and s == 6 * q + 1:
                            fox_turn(g, q, 0)
                        if g >= 0 and q >= 4 and s == 6 * q + 2:
                            fox_turn(g, q, 1)
                        if g >= 0 and s == 6 * q + 4:
                            fox_out(g, q)
                    if h == FOX:
                        return
                    if s == 48:
                        pe.wait_ge(fx_sq, 2 * h + 2)
                        if h:
                            pe.wait_ge(fx_s, NB * h)
                        token_sums(pa[:, 0:NB], N[:, 0, :])
                        token_sums(pa[:, NB:2 * NB], N[:, 1, :]).then_inc(fx_ss, 1)
                    if s == 51:
                        pe.wait_ge(fx_rstd, 2 * h + 2)
                        spread(pa, rn[:, 0:NB]).then_inc(fx_wide, 1)
                    if s == 53:
                        pe.wait_ge(tile_out, EV_FOX + 4 * h + 3)
                        if h:
                            pe.wait_ge(fx_pt, fox_round(h, 0, 0))
                            pe.wait_ge(fx_y, 2 * h)
                        else:
                            pe.wait_ge(c_out, 1)
                        turn8(pb, X4(6), fx_vturn)
                    if s == 60:
                        fox_scores(h, 0)

                return at

            for w in range(FOX + 1):
                among = fox_among(w)
                if w < FOX:
                    for j in range(4):
                        t = T_FOX + 4 * w + j
                        pe.wait_ge(tile_out, EV_FOX + 4 * w + j - 1)
                        gemm_tile(t, t % 2, hhi, hlo, S, HFOX if w == j == 0 else None, among, 16 * j)
                else:
                    pe.wait_ge(tile_out, EV_FO)
                    for s in range(64):
                        among(s)
                        part_groups(T_FO, HFO, FO_ORDER, EV_FO, fo_groups(s - 1), fo_groups(s))
            last_shares(T_FO, HFO, EV_FO, 1)
            pe.wait_ge(sq_added, KT * (NFP + 1))
            token_sums(pa[:, 0:NB], N[:, 2, :]).then_inc(norm_mm, 1)
            pe.wait_ge(norm_rstd, S_FP + 1)
            spread(pa, R_TMP).then_inc(norm_wide, 1)

        @block.scalar
        def _(act):
            A = nc.scalar.activation
            steps = [0]

            def done(ins):
                steps[0] += 1
                ins.then_inc(act_step, 1)

            def settle():
                act.wait_ge(act_step, steps[0])

            def square(j, k, src):
                n = KT * j + k
                if n >= 2:
                    act.wait_ge(sq_added, n - 1)
                A(squares(j, k), src, ACT.Square).then_inc(sq_ready, 1)

            def root(j, width=S):
                act.wait_ge(norm_mm, j + 1)
                dst = N[:, 3, :] if j != NMEM else H[:, 1, N_MEM:2 * N_MEM]
                A(dst, pa[:, 0:width], ACT.Sqrt, bias=eps[:, 0:1], scale=1.0 / D).then_inc(norm_root, 1)

            def hi_parts(p, srcs, dst, waits=None, free=None):
                for k in range(KT):
                    if k == 0 and free is not None:
                        act.wait_ge(pe_slot, free)
                    if waits is not None:
                        act.wait_ge(waits[0], waits[1] + k)
                    A(dst[:, k, :], srcs(k), ACT.Copy).then_inc(h_hi_done, 1)

            def evac(t, ev, dst, b, func=ACT.Copy, width=S):
                act.wait_ge(pe_slot, t + 1)
                A(dst, gp[b][:, 0:width], func).then_inc(tile_out, 1)

            def part_out(order, lo, hi, n):
                for m in parts_done(order, lo, hi):
                    act.wait_ge(share_mm, (PART + KT - 1) * n + m + 1)
                    A(yt[:, m, :], gp[m % 2][:, :], ACT.Copy).then_inc(tile_out, 1)

            def shares_out(ev, n, norm):
                for f, m in enumerate(FINAL):
                    if f < 2:
                        act.wait_ge(share_mm, (PART + KT - 1) * n + PART + f + 1)
                        A(yt[:, m, :], gp[m % 2][:, :], ACT.Copy).then_inc(tile_out, 1)
                        act.wait_ge(tile_out, ev + PART + f + 1)
                    else:
                        act.wait_ge(share_added, PART * n + f - 1)
                    square(norm, f, yt[:, m, :])

            def nt(k):
                return N[:, k % 2, :]

            act.wait_ge(eps_set, 2)
            act.wait_ge(vec_loaded, 16)
            for k in range(KT):
                act.wait_ge(x_loaded[k], 16)
                A(hhi[:, k, :], xres[:, k, :], ACT.Copy, scale=vc("mix_g", k)).then_inc(h_hi_done, 1)
            for k in range(KT):
                square(NMIX, k, xres[:, k, :])
            act.wait_ge(const_loaded, 64)
            act.wait_ge(h_lo_done, KT * (HMIX + 1))

            def ret_tile(h, j):
                t = T_RET + 4 * h + j
                if j < 2:
                    dst = (yt[:, h, :], H[:, h % 2, :])[j]
                    act.wait_ge(pe_slot, t + 1)
                    if h:
                        act.wait_ge(roped, 2 * (h - 1) + j + 1)
                    if j == 1 and h >= 2:
                        act.wait_ge(ret_scores, h - 1)
                    A(dst, gp[t % 2][:, :], ACT.Copy)
                    A(SWAPPED[j][0:64, :], gp[t % 2][64:P, :], ACT.Copy)
                    A(SWAPPED[j][64:P, :], gp[t % 2][0:64, :], ACT.Copy).then_inc(tile_out, 1)
                elif j == 2:
                    if h:
                        act.wait_ge(ret_turned, 2 * h)
                    evac(t, 0, V_FEAT, t % 2)
                else:
                    act.wait_ge(tile_out, t + 1)
                    A(H[:, 2 + h % 2, :], H[:, 2 + h % 2, :], ACT.Silu).then_inc(ret_gate, 1)

            def pool_scaled(j):
                act.wait_ge(pool_mm, j + 1)
                act.wait_ge(roped, 2 * RET)
                A(yt[:, 4 + j, :], pa, ACT.Copy, scale=vc("pool_scale", j)).then_inc(pool_y, 1)

            for w in range(RET + 1):
                g, h = w - 1, w
                for s in range(65):
                    if h < RET and s in (16, 32, 48, 64):
                        ret_tile(h, s // 16 - 1)
                    if w == 0 and s == 28:
                        act.wait_ge(norm_mm, NMIX + 1)
                        A(R_H, pa[:, 0:NB], ACT.Sqrt, bias=eps[:, 0:1], scale=1.0 / D).then_inc(norm_root, 1)
                    if w == 0 and s == 31:
                        act.wait_ge(norm_wide, W_MIX + 1)
                        A(WIDE_MIX, pa, ACT.Copy).then_inc(wide_out, 1)
                    if w == 0 and s == 40:
                        act.wait_ge(angles, 1)
                        A(SIN[0:64, :], SIN[0:64, :], ACT.Sin, scale=-1.0)
                        A(SIN[64:P, :], SIN[64:P, :], ACT.Sin)
                        A(COS, COS, ACT.Sin).then_inc(rope_tab, 1)
                    if w == RET and s in (28, 44, 60):
                        pool_scaled(s // 16 - 1)
                    if g < 0:
                        continue
                    if s == 0:
                        act.wait_ge(ret_turned, 2 * g + 1)
                        if g:
                            act.wait_ge(ret_kv, g)
                        A(K_TOK, pa, ACT.Copy, scale=cn("zeta", g, 1)).then_inc(ret_kz, 1)
                    if s == 12:
                        act.wait_ge(ret_out, g + 1)
                        done(A(yt[:, g, :], pa, ACT.Copy))
                        settle()
                        if g:
                            act.wait_ge(y_sums, g)
                        A(N[:, 1, :], yt[:, g, :], ACT.Square).then_inc(y_squared, 1)
                    if s == 17:
                        act.wait_ge(y_sums, g + 1)
                        if g:
                            act.wait_ge(y_wide, g)
                        A(R_O, pb[:, 0:NB], ACT.Sqrt, bias=eps[:, 0:1], scale=1.0 / RET_DH).then_inc(y_root, 1)
            for k in range(KT):
                if k == 0:
                    act.wait_ge(pe_slot, T_WOUT)
                if k < RET:
                    act.wait_ge(y_done, k + 1)
                else:
                    if k == KT - 1:
                        pool_scaled(3)
                    act.wait_ge(pool_y, k - RET + 1)
                A(hhi[:, k, :], yt[:, k, :], ACT.Copy).then_inc(h_hi_done, 1)
            act.wait_ge(h_lo_done, KT * (HRET + 1))
            act.dma_start(memx[:, :, :], mem_t).then_inc(mem_loaded, 16)
            for k in range(KT):
                act.dma_start(xres[:, k, :], x_t[k]).then_inc(x_loaded[k], 16)
            act.wait_ge(mem_loaded, 16)
            for k in range(KT):
                square(NMEM, k, memx[:, k, :])
            root(NMEM, N_MEM)
            hi_parts(HMEM, lambda k: H[:, 0, (k % 2) * N_MEM:(k % 2 + 1) * N_MEM], mem_hi, (norm_scaled, 1))
            def hi_gained(k):
                A(hhi[:, k, :], xres[:, k, :], ACT.Copy, scale=vc("xa_g", k)).then_inc(h_hi_done, 1)

            w_last = MIX_OUT.index(("x", KT - 1))
            for i, (kind, m) in enumerate(MIX_OUT):
                if kind == "x":
                    act.wait_ge(tile_added, m + 1)
                    square(NXA, m, xres[:, m, :])
                else:
                    if i > w_last:
                        act.wait_ge(pe_slot, T_WOUT + w_last + 1)
                        for k in range(2 * (i - w_last - 1), 2 * (i - w_last)):
                            hi_gained(k)
                    dst = Nf[:, m * N_MEM:(m + 1) * N_MEM] if m < KT else \
                        H[:, 2:4, :].rearrange("p a (k m) -> p (a k) m", m=N_MEM)[:, m - KT, :]
                    evac(T_WOUT + i, 0, dst, (T_WOUT + i) % 2, ACT.Copy, N_MEM)

            def hi_y(k):
                if k == 0:
                    act.wait_ge(pe_slot, T_XO)
                act.wait_ge(xa_y, 2 * (k // 2) + 2)
                A(hhi[:, k, :], yt[:, k, :], ACT.Copy).then_inc(h_hi_done, 1)

            for w in range(XA_HEADS + 1):
                g, h = w - 1, w
                for s in range(33):
                    if h < XA_HEADS and s in (16, 32):
                        j = s // 16 - 1
                        evac(T_XQ + 2 * h + j, 0, yt[:, 2 * h + j, :], (T_XQ + j) % 2)
                    if w == 0 and s == 14:
                        act.wait_ge(norm_mm, NXA + 1)
                        A(R_H, pa[:, 0:NB], ACT.Sqrt, bias=eps[:, 0:1], scale=1.0 / D).then_inc(norm_root, 1)
                    if w == 0 and s == 18:
                        for b in range(2):
                            act.wait_ge(mem_turned, b + 1)
                            A(N[:, 2 + b, :], ps[b][:, :], ACT.Copy).then_inc(mem_v, 1)
                    if w == XA_HEADS and s < KT - 2:
                        hi_y(s)
                    if g < 0 or s == 32:
                        continue
                    f = s // 16
                    u = 2 * g + f
                    if s % 16 == 2:
                        act.wait_ge(xa_max, u + 1)
                        if u:
                            act.wait_ge(xa_turned, u)
                        for q in range(4):
                            last = A(H[:, 2, q * N_MEM:(q + 1) * N_MEM], pa[:, q * N_MEM:(q + 1) * N_MEM], ACT.Exp,
                                     bias=stat[:, 4 + q:5 + q], scale=R_H2[:, 4 * f + q:4 * f + q + 1], accum_out=stat[:, 8 + q:9 + q])
                        last.then_inc(xa_exp, 1)
                    if s % 16 == 9:
                        act.wait_ge(xa_turned, u + 1)
                        if u:
                            act.wait_ge(xa_out, u)
                        A(H[:, 3, :], pb, ACT.Copy).then_inc(xa_pt, 1)
                    if s % 16 == 12:
                        act.wait_ge(xa_out, u + 1)
                        for d in range(2):
                            last = A(yt[:, 2 * g + d, f * HALF:(f + 1) * HALF], pa[:, d * HALF:(d + 1) * HALF], ACT.Copy)
                        last.then_inc(xa_y, 1)
            for k in range(KT - 2, KT):
                hi_y(k)
            for m in range(KT):
                if m == KT - 1:
                    act.wait_ge(pe_slot, T_FF)
                    for k in range(KT):
                        if k == KT - 1:
                            act.wait_ge(tile_added, 2 * KT)
                        A(hhi[:, k, :], xres[:, k, :], ACT.Copy, scale=vc("ffn_g", k)).then_inc(h_hi_done, 1)
                act.wait_ge(tile_added, KT + m + 1)
                square(NFF, m, xres[:, m, :])
            act.wait_ge(norm_mm, NFF + 1)
            A(R_H, pa[:, 0:NB], ACT.Sqrt, bias=eps[:, 0:1], scale=1.0 / D).then_inc(norm_root, 1)
            act.wait_ge(norm_wide, W_FF + 1)
            A(WIDE_FF, pa, ACT.Copy).then_inc(wide_out, 1)

            def up(i, b):
                for j in range(2):
                    act.wait_ge(ff_conv, 4 * i + (2 * j + 1))
                    A(H[:, 2 * j, :], H[:, 2 * j, :], ACT.Silu).then_inc(ff_gate, 1)
                    if j == 0 and not (isinstance(i, int) and i < 2):
                        act.wait_ge(pe_slot, 6 * i + (T_FF - 2))
                    act.wait_ge(ff_prod, 2 * i + (j + 1))
                    A(act_hi[:, 2 * b + j, :], H[:, 2 * j, :], ACT.Copy).then_inc(act_hi_done, 1)

            up(0, 0)
            up(1, 1)
            with act.Fori(1, FF_STEPS // 2) as r:
                for b in range(2):
                    up(2 * r + b, b)
            up(FF_STEPS - 1, 0)
            act.wait_ge(fin_scaled, 1)
            for k in range(KT):
                act.wait_ge(down_ev, 8 * (FF_STEPS - 1) + k + 1)
                if k == 0:
                    act.wait_ge(pe_slot, T_GDN - 2)
                A(hhi[:, k, :], xres[:, k, :], ACT.Copy, scale=both_g[:, k:k + 1]).then_inc(h_hi_done, 1)
                act.dma_start(x_spill[k], xres[:, k, :]).then_inc(spilled, 16)
            for k in range(KT):
                square(NFIN, k, xres[:, k, :])
            for k in range(KT):
                n = KT * NGDN + k
                act.wait_ge(sq_added, n - 1)
                A(N[:, k % 2, :], xres[:, k, :], ACT.Square, scale=vc("final_g", k)).then_inc(sq_ready, 1)
            act.wait_ge(norm_mm, NGDN + 1)
            A(R_FIN, pa[:, 0:NB], ACT.Sqrt, bias=eps[:, 0:1], scale=1.0 / D).then_inc(norm_root, 1)
            act.wait_ge(fin_scaled, 2)
            A(R_TMP, R_TMP, ACT.Sqrt, bias=eps[:, 0:1], scale=1.0 / D).then_inc(norm_root, 1)
            act.wait_ge(norm_wide, W_GDN + 1)
            A(WIDE_GDN, pb, ACT.Copy).then_inc(wide_out, 1)
            def gdn_gates():
                act.wait_ge(ab_mm, 1)
                A(N[0:N_AB, 1, :], pa[0:N_AB, :], ACT.Copy).then_inc(ab_out, 1)
                act.wait_ge(ab_mm, 2)
                A(tiny[:, 0:2, :], pb[:, 0:NB * N_AB].rearrange("p (n c) -> p n c", c=64), ACT.Copy).then_inc(ab_out, 1)
                act.wait_ge(ab_e, 1)
                done(A(tiny[:, 3, :], tiny[:, 3, :], ACT.Exp, scale=-1.0))
                done(A(tiny[:, 6, :], tiny[:, 6, :], ACT.Exp, scale=-1.0))
                done(A(row[:, 0:GDN], row[:, 0:GDN], ACT.Exp))
                settle()
                A(tiny[:, 3, :], tiny[:, 3, :], ACT.Ln, bias=1.0).then_inc(ab_e, 1)

            def gdn_decays():
                act.wait_ge(gc_mm, 1)
                A(tiny[:, 7, :], pb[:, 0:64], ACT.Copy)
                A(tiny[:, 8, :], pb[:, 64:128], ACT.Copy).then_inc(gc_out, 1)
                act.wait_ge(gc_diff, 1)
                A(tiny[:, 9, :], tiny[:, 9, :], ACT.Exp)
                A(tiny[:, 8, :], tiny[:, 8, :], ACT.Exp)
                A(tiny[:, 10, :], tiny[:, 7, :], ACT.Exp).then_inc(gc_out, 1)

            NL = len(LEVELS)

            def gdn_tile(h, j):
                n = 3 * h + j
                act.wait_ge(tile_out, EV_GDN + 4 * h + j + 1)
                if j == 3:
                    A(H[:, 2 + h % 2, :], H[:, 2 + h % 2, :], ACT.Silu).then_inc(gd_z, 1)
                    return
                if j == 1 and h >= 2:
                    act.wait_ge(ch_s_mm, NB * (h - 1))
                if j == 2 and h:
                    act.wait_ge(gd_vturn, h)
                A(gdn_dst(h, j), (GP0, GP1)[n % 2][:, 3:3 + S], ACT.Copy,
                  scale=vc("gdn_w", (3 * 3 + j) * GDN + h)).then_inc(gd_tap3, 1)

            def hi_y(k):
                if k == 0:
                    act.wait_ge(pe_slot, T_GO)
                act.wait_ge(y_done, Y_GDN + k + 1)
                A(hhi[:, k, :], yt[:, k, :], ACT.Copy).then_inc(h_hi_done, 1)

            def gdn_silu(h, j):
                act.wait_ge(gd_conv, 3 * h + j + 1)
                A(gdn_dst(h, j), gdn_dst(h, j), ACT.Silu).then_inc(gd_silu, 1)

            for w in range(GDN + 2):
                g, h = w - 1, w
                for s in range(65):
                    if h < GDN and s in (16, 32, 49, 64):
                        gdn_tile(h, s // 16 - 1)
                    if w == GDN and s < KT - 2:
                        hi_y(s)
                    if (w, s) in ((GDN, 20), (GDN + 1, 20)):
                        hi_y(w - 2)
                    if w == 0 and s == 36:
                        gdn_gates()
                    if w == 0 and s == 46:
                        gdn_decays()
                    if g >= 1 and s == 2:
                        act.wait_ge(go_scaled, g)
                        A(R_O, R_O, ACT.Sqrt, bias=eps[:, 0:1], scale=1.0 / GDN_DK).then_inc(go_root, 1)
                    if 0 <= g < GDN:
                        if s == 0:
                            act.wait_ge(gd_diff, g + 1)
                            A(TI, TI, ACT.Exp).then_inc(gd_exp, 1)
                            A(N[:, 1, :], pa, ACT.Exp).then_inc(gd_exp, 1)
                        if s == 8:
                            act.wait_ge(gd_vturn, g + 1)
                            for n in range(NB):
                                last = A(ck(N[:, 3, :], n), ck(pb, n), ACT.Copy, scale=by_head[:, g % 2, K_NORM, n:n + 1])
                            last.then_inc(gd_vb, 1)
                        if s == 9:
                            act.wait_ge(gd_kturn, g + 1)
                            act.wait_ge(gd_cols, g + 1)
                            for n in range(NB):
                                last = A(ck(N[:, 2, :], n), ck(pa, n), ACT.Copy, scale=by_head[:, g % 2, DECAY_RK, n:n + 1])
                            last.then_inc(gd_kdec, 1)
                        if s == 11:
                            act.wait_ge(gd_tturn, g + 1)
                            A(TI, pb, ACT.Copy).then_inc(gd_ti, 1)
                        if s >= 17 and (s - 17) % 4 == 0 and (s - 17) // 4 < NL:
                            l = (s - 17) // 4
                            act.wait_ge(inv_turn, NL * g + l + 1)
                            act.wait_ge(inv_y_mm, NL * g + l + 1)
                            A(TT, pb, ACT.Copy).then_inc(inv_tt, 1)
                        if s >= 39 and (s - 39) % 3 == 0 and (s - 39) // 3 < NB:
                            u = NB * g + (s - 39) // 3
                            act.wait_ge(ch_vn_mm, u + 1)
                            if u:
                                act.wait_ge(ch_s_mm, u)
                            n = (s - 39) // 3
                            A(v_new[:, :], pa[:, HALF:HALF + P], ACT.Copy, scale=by_head[:, g % 2, BETA_RK, n:n + 1]).then_inc(ch_vn, 1)
                        if s == 62:
                            act.wait_ge(ch_s_mm, NB * (g + 1))
                            A(yt[:, g, :], pb, ACT.Copy).then_inc(gd_o, 1)
                    if h < GDN:
                        if s == 27:
                            gdn_silu(h, 0)
                        if s == 39:
                            gdn_silu(h, 1)
                        if s == 42:
                            act.wait_ge(gd_silu, 3 * h + 2)
                            if h:
                                act.wait_ge(inv_turn, NL * h)
                            for j in range(2):
                                A((MT, TI)[j], gdn_dst(h, j), ACT.Square).then_inc(gd_sq, 1)
                        if s == 57:
                            gdn_silu(h, 2)
                        if s == 62:
                            act.wait_ge(gd_ss, h + 1)
                            if h >= 2:
                                act.wait_ge(go_rstd, h - 1)
                            A(cols_of_head(h, K_NORM, 2), pa[:, 0:2 * NB], ACT.Sqrt, bias=eps[:, 0:1]).then_inc(gd_root, 1)
                    if 0 <= g < GDN and s == 62:
                        act.wait_ge(gd_o, g + 1)
                        A(TT, yt[:, g, :], ACT.Square).then_inc(y_squared, 1)
                    part_out(GO_ORDER, go_groups(w, s - 1), go_groups(w, s), 0)
            act.wait_ge(h_lo_done, KT * (HGO + 1))
            act.wait_ge(spilled, 16 * KT)
            for k in range(KT):
                act.dma_start(xres[:, k, :], x_spill[k]).then_inc(x_loaded[k], 16)
            shares_out(EV_GO, 0, NGP)

            def tokens_root(j, cols):
                act.wait_ge(norm_mm, j + 1)
                A(cols, pa[:, 0:NB], ACT.Sqrt, bias=eps[:, 0:1], scale=1.0 / D).then_inc(norm_root, 1)

            tokens_root(NGP, R_TMP)
            for k in range(KT):
                act.wait_ge(tile_added, 2 * KT + k + 1)
                if k == 0:
                    act.wait_ge(pe_slot, T_FOX)
                A(hhi[:, k, :], xres[:, k, :], ACT.Copy).then_inc(h_hi_done, 1)
                act.dma_start(x_spill[k], xres[:, k, :]).then_inc(spilled, 16)
            for k in range(KT):
                square(NFOX, k, xres[:, k, :])
            tokens_root(NFOX, R_H)
            act.wait_ge(norm_wide, W_FOX + 1)
            A(WIDE_FOX, pb, ACT.Copy).then_inc(wide_out, 1)

            def hi_y(k):
                if k == 0:
                    act.wait_ge(pe_slot, T_FO)
                act.wait_ge(fx_y, 2 * k + 2)
                A(hhi[:, k, :], yt[:, k, :], ACT.Copy).then_inc(h_hi_done, 1)

            def fox_exp(g, q):
                z, sc = 4 * (q % 2), X4(3 + q % 2)[:, 0:(q + 1) * P]
                act.wait_ge(fx_s, NB * g + q + 1)
                A(sc, sc, ACT.Exp, bias=stat[:, 14 + z:15 + z], accum_out=stat[:, 15 + z:16 + z]).then_inc(fx_exp, 1)

            def fox_gates():
                act.wait_ge(f_mm, 1)
                A(N[0:FOX, 2, :], pa[0:FOX, :], ACT.Copy).then_inc(f_out, 1)
                act.wait_ge(f_mm, 2)
                A(tiny[:, 0, :], pb[:, 0:NB * FOX], ACT.Copy).then_inc(f_out, 1)
                act.wait_ge(f_e, 1)
                done(A(tiny[:, 3, :], tiny[:, 3, :], ACT.Exp, scale=-1.0))
                settle()
                A(tiny[:, 3, :], tiny[:, 3, :], ACT.Ln, bias=1.0).then_inc(f_e, 1)

            for w in range(FOX + 1):
                g, h = w - 1, w
                for s in range(65):
                    if w == FOX and s < KT - 1:
                        hi_y(s)
                    if w == 0 and s == 36:
                        fox_gates()
                    if w == 0 and s == 44:
                        act.wait_ge(c_mm, 2)
                        A(N[0:64, 2, 0:P], pb[0:64, P:2 * P], ACT.Copy).then_inc(c_out, 1)
                        act.wait_ge(c_out, 1)
                        for n in range(NB):
                            act.dma_start(c_rows[:, n, :], N[n * FOX:(n + 1) * FOX, 2, 0:P]).then_inc(c_moved, 16)
                    if h < FOX and s == 50:
                        if h:
                            act.wait_ge(fx_s, NB * h)
                        else:
                            act.wait_ge(c_moved, 16 * NB)
                        act.dma_start(X4(1), c_rows[h:h + 1].rearrange("a n t -> a (n t)").broadcast_to([P, S])).then_inc(c_moved, 16)
                    if h < FOX and s in (16, 32, 48, 64):
                        j = s // 16 - 1
                        t = T_FOX + 4 * h + j
                        if j == 0:
                            if h >= 2:
                                act.wait_ge(fx_s_mm, NB * (h - 1))
                            evac(t, 0, H[:, h % 2, :], t % 2)
                        elif j == 1:
                            evac(t, 0, yt[:, h, :], t % 2)
                        elif j == 2:
                            if h:
                                act.wait_ge(fx_vturn, h)
                            else:
                                act.wait_ge(spilled, 2 * 16 * KT)
                            evac(t, 0, X4(6), t % 2)
                        else:
                            act.wait_ge(tile_out, EV_FOX + 4 * h + 4)
                            A(H[:, 2 + h % 2, :], H[:, 2 + h % 2, :], ACT.Silu).then_inc(fx_z, 1)
                        if j < 2:
                            act.wait_ge(tile_out, EV_FOX + 4 * h + j + 1)
                            if h:
                                act.wait_ge(fx_ss, h)
                            A(N[:, j, :], (H[:, h % 2, :], yt[:, h, :])[j], ACT.Square).then_inc(fx_sq, 1)
                    if h < FOX and s == 48:
                        act.wait_ge(fx_rstd, 2 * h + 1)
                        A(R_QK, R_QK, ACT.Sqrt, bias=eps[:, 0:1], scale=1.0 / FOX_D).then_inc(fx_root, 1)
                    if h < FOX and s == 62:
                        fox_exp(h, 0)
                    for q in range(NB):
                        if g >= 0 and q and s == 6 * q - 3:
                            fox_exp(g, q)
                        for r in range(q // 4 + 1):
                            if g >= 0 and s == 6 * q + 1 + r:
                                act.wait_ge(fx_turn, fox_round(g, q, r) + 1)
                                if r == 0 and g + q:
                                    act.wait_ge(fx_o, NB * g + q)
                                n = min(q + 1 - 4 * r, 4) * P
                                A(X4(5)[:, r * HALF:r * HALF + n], pb[:, 0:n], ACT.Copy).then_inc(fx_pt, 1)
                    if w == FOX:
                        part_out(FO_ORDER, fo_groups(s - 1), fo_groups(s), 1)
            act.wait_ge(fx_y, 2 * FOX)
            hi_y(KT - 1)
            act.wait_ge(h_lo_done, KT * (HFO + 1))
            act.wait_ge(spilled, 2 * 16 * KT)
            for k in range(KT):
                act.dma_start(xres[:, k, :], x_spill[k]).then_inc(x_loaded[k], 16)
            shares_out(EV_FO, 1, NFP)
            tokens_root(NFP, R_TMP)
            for k in range(KT):
                if k < OUT_POOL:
                    act.wait_ge(out_ready, k + 1)
                else:
                    act.wait_ge(tile_added, 3 * KT + k - OUT_POOL + 1)
                act.dma_start(out[k], xres[:, k, :]).then_inc(stored, 16)
            act.wait_ge(stored, 16 * KT)

        @block.vector
        def _(dve):
            V = nc.vector
            steps = [0]

            def done(ins):
                steps[0] += 1
                ins.then_inc(dve_step, 1)

            def settle():
                dve.wait_ge(dve_step, steps[0])

            def add_square(j, k):
                n = KT * j + k
                wide = j != NMEM
                ssq = H[:, 0, :] if j == NXA else N[:, 2, :] if wide else H[:, 1, 0:N_MEM]
                src = squares(j, k)
                dve.wait_ge(sq_ready, n + 1)
                if k == 0:
                    if j:
                        dve.wait_ge(norm_mm, j)
                    V.tensor_copy(ssq, src).then_inc(sq_added, 1)
                else:
                    dve.wait_ge(sq_added, n)
                    V.tensor_tensor(ssq, ssq, src, ALU.add).then_inc(sq_added, 1)

            def rstd(j):
                dve.wait_ge(norm_root, j + 1)
                r = N[:, 3, :] if j != NMEM else H[:, 1, N_MEM:2 * N_MEM]
                done(V.reciprocal(r, r))
                settle()

            def lo_part(p, k, src, dst_hi, dst_lo):
                dve.wait_ge(h_hi_done, KT * p + k + 1)
                V.tensor_tensor(dst_lo[:, k, :], src, dst_hi[:, k, :].bitcast(F32), ALU.subtract).then_inc(h_lo_done, 1)

            def norm_to_h(j, p, c, src, gain, dst_hi, dst_lo):
                rstd(j)
                wide = j != NMEM
                r = N[:, 3, :] if wide else H[:, 1, N_MEM:2 * N_MEM]

                def t(k):
                    return N[:, k % 2, :] if wide else H[:, 0, (k % 2) * N_MEM:(k % 2 + 1) * N_MEM]

                for k in range(KT):
                    if k >= 2:
                        dve.wait_ge(h_lo_done, KT * p + k - 1)
                    if gain is None:
                        V.tensor_tensor(t(k), src(k), r, ALU.mult).then_inc(norm_scaled, 1)
                    else:
                        V.scalar_tensor_tensor(t(k), src(k), vc(gain, k), r, ALU.mult, ALU.mult).then_inc(norm_scaled, 1)
                    if k:
                        lo_part(p, k - 1, t(k - 1), dst_hi, dst_lo)
                lo_part(p, KT - 1, t(KT - 1), dst_hi, dst_lo)

            def xt(k):
                return xres[:, k, :]

            dve.wait_ge(vec_loaded, 16)
            def by_token(ap, r):
                return r.rearrange("p (n a) -> p n a", a=1).broadcast_to([P, NB, ap.shape[-1]])

            dve.wait_ge(pos_loaded, 16)
            done(V.tensor_copy(yt[:, 5, :], H[:, 3, :].bitcast(I32)))
            settle()
            done(V.tensor_scalar(yt[:, 5, :], yt[:, 5, :], vc("inv_freq", 0), None, ALU.mult))
            settle()
            for dst, shift in ((SIN, 0.0), (COS, 0.25)):
                done(V.tensor_scalar(yt[:, 4, :], yt[:, 5, :], 1.0 / (2 * math.pi), shift, ALU.mult, ALU.add))
                settle()
                done(V.tensor_scalar(yt[:, 4, :], yt[:, 4, :], ROUND_MAGIC, ROUND_MAGIC, ALU.add, ALU.subtract))
                settle()
                done(V.scalar_tensor_tensor(dst, yt[:, 4, :], -TWO_PI_HI, yt[:, 5, :], ALU.mult, ALU.add))
                settle()
                for part in (TWO_PI_MID, TWO_PI_LO):
                    done(V.scalar_tensor_tensor(dst, yt[:, 4, :], -part, dst, ALU.mult, ALU.add))
                    settle()
                done(V.tensor_scalar(dst, dst, shift * 2 * math.pi, math.pi, ALU.add, ALU.min))
                settle()
                if shift:
                    V.tensor_scalar(dst, dst, -math.pi, None, ALU.max).then_inc(angles, 1)
                else:
                    done(V.tensor_scalar(dst, dst, -math.pi, None, ALU.max))
                    for k in range(KT):
                        dve.wait_ge(h_hi_done, KT * HMIX + k + 1)
                        V.scalar_tensor_tensor(hlo[:, k, :], xres[:, k, :], vc("mix_g", k), hhi[:, k, :].bitcast(F32), ALU.mult,
                                               ALU.subtract).then_inc(h_lo_done, 1)
                    for k in range(KT):
                        add_square(NMIX, k)
                    dve.wait_ge(norm_root, NMIX + 1)
                    V.reciprocal(R_H, R_H).then_inc(norm_rstd, 1)
                    settle()
            dve.wait_ge(const_loaded, 64)
            dve.wait_ge(rope_tab, 1)
            dve.wait_ge(wide_out, 1)
            for table in (SIN, COS):
                done(V.tensor_tensor(table, table, WIDE_MIX, ALU.mult))
            settle()

            def rope(h, j):
                x = (yt[:, h, :], H[:, h % 2, :])[j]
                scale = (1.0, RET_DH ** -0.5)[j]
                dve.wait_ge(tile_out, 4 * h + j + 1)
                done(V.scalar_tensor_tensor(x, x, scale, COS, ALU.mult, ALU.mult))
                done(V.scalar_tensor_tensor(SWAPPED[j], SWAPPED[j], scale, SIN, ALU.mult, ALU.mult))
                settle()
                V.tensor_tensor(x, x, SWAPPED[j], ALU.add).then_inc(roped, 1)
                if j == 0:
                    dve.wait_ge(roped, 2 * h + 1)
                    if h:
                        dve.wait_ge(ret_out, h)
                    done(V.tensor_tensor(chunks(N[:, 0, :]), chunks(x), over(cn("xi", h), NB), ALU.mult))

            def ret_head(g, s):
                if s == 0:
                    dve.wait_ge(ret_turned, 2 * g + 2)
                    if g:
                        dve.wait_ge(ret_out, g)
                    V.tensor_tensor(chunks(V_TOK), chunks(pb), by_token(chunks(pb), R_H), ALU.mult).then_inc(ret_v, 1)
                if s == 3:
                    dve.wait_ge(ret_scores, g + 1)
                    settle()
                    V.tensor_tensor(chunks(P_TOK), chunks(pa), over(cn("dmat", g), NB), ALU.mult).then_inc(ret_probs, 1)
                if s == 5:
                    dve.wait_ge(ret_kv, g + 1)
                    for n in range(NB - 1):
                        if n == 0:
                            done(V.tensor_copy(ck(STATES, 1), ck(pb, 0)))
                        else:
                            settle()
                            last = V.scalar_tensor_tensor(ck(STATES, n + 1), ck(STATES, n), RET_DECAY[g], ck(pb, n), ALU.mult, ALU.add)
                            if n < NB - 2:
                                done(last)
                    last.then_inc(ret_states, 1)
                if s == 17:
                    dve.wait_ge(y_root, g + 1)
                    V.reciprocal(R_O, R_O).then_inc(y_rstd, 1)
                if s == 19:
                    y = yt[:, g, :]
                    dve.wait_ge(y_wide, g + 1)
                    done(V.scalar_tensor_tensor(y, y, vc("gn_g", g), pb, ALU.mult, ALU.mult))
                    dve.wait_ge(ret_gate, g + 1)
                    settle()
                    V.tensor_tensor(y, y, H[:, 2 + g % 2, :], ALU.mult).then_inc(y_done, 1)

            def pool(j, win):
                t, W = T_RET + 4 * RET + j, W_POOL
                dve.wait_ge(pe_slot, t + 1)
                if j:
                    dve.wait_ge(pool_in, j)
                V.tensor_tensor(POOL_U[:, PAD:], gp[t % 2][:, :], WIDE_MIX, ALU.mult).then_inc(tile_out, 1)
                dve.wait_ge(tile_out, t + 1)
                src, dst, step = POOL_U, POOL_B, 1
                while step < win:
                    done(V.tensor_tensor(dst[:, PAD:], src[:, PAD:], src[:, PAD - step:W - step], ALU.add))
                    settle()
                    src, dst = dst, (POOL_C if dst is POOL_B else POOL_B)
                    step *= 2
                if j:
                    dve.wait_ge(pool_mm, j)
                else:
                    dve.wait_ge(y_sums, RET)
                done(V.scalar_tensor_tensor(POOLED[:, PAD:], src[:, 2 * PAD:], 1.0 / win, POOL_U[:, 2 * PAD:], ALU.mult, ALU.subtract))
                done(V.tensor_tensor(POOLED[:, 0:PAD], src[:, PAD:2 * PAD], cn("pool_rcnt", j, PAD), ALU.mult))
                settle()
                V.tensor_tensor(POOLED[:, 0:PAD], POOLED[:, 0:PAD], POOL_U[:, PAD:2 * PAD], ALU.subtract).then_inc(pool_in, 1)

            for w in range(RET + 1):
                g, h = w - 1, w
                for s in range(69):
                    if g >= 0:
                        ret_head(g, s)
                    if h < RET and s in (24, 40):
                        rope(h, s // 40)
                    if h < RET and s == 64:
                        t = T_RET + 4 * h + 3
                        dve.wait_ge(pe_slot, t + 1)
                        dve.wait_ge(tile_out, t)
                        if h >= 2:
                            dve.wait_ge(y_done, h - 1)
                        V.tensor_tensor(H[:, 2 + h % 2, :], gp[t % 2][:, :], WIDE_MIX, ALU.mult).then_inc(tile_out, 1)
                    if w == RET and s == 13:
                        dve.wait_ge(ret_out, RET)
                        dve.wait_ge(roped, 2 * RET)
                        V.memset(POOL_U[:, 0:PAD], 0.0)
                        V.memset(POOL_B[:, 0:PAD], 0.0)
                        V.memset(POOL_C[:, 0:PAD], 0.0).then_inc(pads_zero, 1)
                        dve.wait_ge(pads_zero, 1)
                    if w == RET and s in (20, 36, 52, 68):
                        pool(s // 16 - 1, POOL_WINDOWS[s // 16 - 1])
            for k in range(KT):
                lo_part(HRET, k, yt[:, k, :], hhi, hlo)
            for k in range(KT):
                add_square(NMEM, k)
            def add_x(i, m):
                dve.wait_ge(pe_slot, T_WOUT + i + 1)
                dve.wait_ge(x_loaded[m], 32)
                V.tensor_tensor(xres[:, m, :], gp[(T_WOUT + i) % 2][:, :], xres[:, m, :], ALU.add).then_inc(tile_added, 1)

            for m in range(2):
                add_x(m, m)
            norm_to_h(NMEM, HMEM, KT, lambda k: memx[:, k, :], "mem_g", mem_hi, mem_lo)

            dve.wait_ge(h_lo_done, KT * (HMEM + 1))
            add_square(NXA, 0)
            for i, (kind, m) in enumerate(MIX_OUT):
                if kind == "x" and m >= 2:
                    add_x(i, m)
                    add_square(NXA, m - 1)
            for k in range(KT):
                dve.wait_ge(h_hi_done, KT * HXA + k + 1)
                V.scalar_tensor_tensor(hlo[:, k, :], xres[:, k, :], vc("xa_g", k), hhi[:, k, :].bitcast(F32), ALU.mult,
                                       ALU.subtract).then_inc(h_lo_done, 1)
            add_square(NXA, KT - 1)
            dve.wait_ge(norm_root, NXA + 1)
            done(V.reciprocal(R_H, R_H))
            settle()
            done(V.tensor_scalar(R_H2, R_H, XA_DH ** -0.5, None, ALU.mult))
            settle()
            for w in range(XA_HEADS + 1):
                for s in range(32):
                    if w == XA_HEADS and 1 <= s < KT - 1:
                        lo_part(HXO, s - 1, yt[:, s - 1, :], hhi, hlo)
                    f = s // 16
                    u = 2 * (w - 1) + f
                    if w and s % 16 == 0:
                        dve.wait_ge(xa_scores, u + 1)
                        done(V.tensor_reduce(stat[:, 0:4], pa.rearrange("p (q m) -> p q m", m=N_MEM), AX_X, ALU.max))
                        settle()
                        V.scalar_tensor_tensor(stat[:, 4:8], stat[:, 0:4], -1.0, R_H2[:, 4 * f:4 * f + 4], ALU.mult,
                                               ALU.mult).then_inc(xa_max, 1)
                    if w and s % 16 == 3:
                        dve.wait_ge(xa_exp, u + 1)
                        done(V.reciprocal(stat[:, 8:12], stat[:, 8:12]))
                        settle()
                        p3 = H[:, 2, :].rearrange("p (q m) -> p q m", m=N_MEM)
                        r3 = stat[:, 8:12].rearrange("p (q a) -> p q a", a=1).broadcast_to([P, 4, N_MEM])
                        V.tensor_tensor(p3, p3, r3, ALU.mult).then_inc(xa_probs, 1)
            for k in range(KT - 2, KT):
                lo_part(HXO, k, yt[:, k, :], hhi, hlo)

            for m in range(KT):
                dve.wait_ge(pe_slot, T_XO + m + 1)
                V.tensor_tensor(xres[:, m, :], gp[m % 2][:, :], xres[:, m, :], ALU.add).then_inc(tile_added, 1)
                if m:
                    add_square(NFF, m - 1)
            dve.wait_ge(tile_added, 2 * KT)
            for k in range(KT):
                dve.wait_ge(h_hi_done, KT * HFF + k + 1)
                V.scalar_tensor_tensor(hlo[:, k, :], xres[:, k, :], vc("ffn_g", k), hhi[:, k, :].bitcast(F32), ALU.mult,
                                       ALU.subtract).then_inc(h_lo_done, 1)
            add_square(NFF, KT - 1)
            dve.wait_ge(norm_root, NFF + 1)
            V.reciprocal(R_H, R_H).then_inc(norm_rstd, 1)
            dve.wait_ge(sq_added, KT * (NFF + 1))
            V.memset(Nf[:, 0:2], 0.0)
            V.memset(Nf[:, FP:FP + 2], 0.0).then_inc(pads_zero, 1)

            def conv(i, j, v, cols, t_down=None):
                q = 2 * j + v
                a = Nf[:, v * FP:(v + 1) * FP]
                c = H[:, q, :]
                at = lambda name, n: vec[:, cols(name, n)]
                if isinstance(i, int) and i == 0:
                    dve.wait_ge(pe_slot, T_FF + q + 1)
                    if q >= 2:
                        dve.wait_ge(ff_conv, q - 1)
                    else:
                        dve.wait_ge(wide_out, 2)
                else:
                    dve.wait_ge(pe_slot, 6 * i + (T_FF + q - 1))
                    dve.wait_ge(ff_conv, 4 * i + (q - 1))
                V.tensor_tensor(a[:, 2:2 + S], gp[v][:, :], WIDE_FF, ALU.mult).then_inc(tile_out, 1)
                dve.wait_ge(tile_out, 4 * i + (EV_FF + q + 1))
                if not (isinstance(i, int) and i == 0):
                    dve.wait_ge(act_lo_done, 2 * i + (j - 1))
                V.tensor_scalar(c, a[:, 2:2 + S], at("ff_w", 2 * 2 * PAIRS + q), at("ff_b", q), ALU.mult, ALU.add).then_inc(ff_taps, 1)
                if t_down is not None:
                    down_add(i - 1, t_down, 0)
                dve.wait_ge(ff_taps, 8 * i + (2 * q + 1))
                V.scalar_tensor_tensor(c, a[:, 1:1 + S], at("ff_w", 2 * PAIRS + q), c, ALU.mult, ALU.add).then_inc(ff_taps, 1)
                if t_down is not None:
                    down_add(i - 1, t_down, 1)
                dve.wait_ge(ff_taps, 8 * i + (2 * q + 2))
                V.scalar_tensor_tensor(c, a[:, 0:S], at("ff_w", q), c, ALU.mult, ALU.add).then_inc(ff_conv, 1)

            def product(i, j):
                dve.wait_ge(ff_gate, 2 * i + (j + 1))
                dve.wait_ge(ff_conv, 4 * i + (2 * j + 2))
                V.tensor_tensor(H[:, 2 * j, :], H[:, 2 * j, :], H[:, 2 * j + 1, :], ALU.mult).then_inc(ff_prod, 1)

            def act_low(i, b, j):
                dve.wait_ge(act_hi_done, 2 * i + (j + 1))
                V.tensor_tensor(act_lo[:, 2 * b + j, :], H[:, 2 * j, :], act_hi[:, 2 * b + j, :].bitcast(F32),
                                ALU.subtract).then_inc(act_lo_done, 1)

            def down_add(i, t0, m):
                a, q = m // 4, m % 4
                if q == 3:
                    dve.wait_ge(pe_slot, t0 + (a + 1))
                else:
                    dve.wait_ge(down_mm, 6 * i + (3 * a + q + 1))
                V.tensor_tensor(xres[:, m, :], ps[m % 2][:, :], xres[:, m, :], ALU.add).then_inc(down_ev, 1)

            def cols_of(i):
                def cols(name, n):
                    at = 4 * i + (VEC_AT[name] + n)
                    return slice(at, at + 1) if isinstance(at, int) else bass.ds(at, 1)
                return cols

            def ff_step(i, b, t_down):
                cols = cols_of(i)
                conv(i, 0, 0, cols)
                conv(i, 0, 1, cols)
                product(i, 0)
                conv(i, 1, 0, cols)
                act_low(i, b, 0)
                conv(i, 1, 1, cols, t_down)
                down_add(i - 1, t_down, 2)
                product(i, 1)
                down_add(i - 1, t_down, 3)
                act_low(i, b, 1)
                for m in range(4, KT):
                    down_add(i - 1, t_down, m)

            cols = cols_of(0)
            for j in range(2):
                conv(0, j, 0, cols)
                conv(0, j, 1, cols)
                product(0, j)
                act_low(0, 0, j)
            ff_step(1, 1, T_FF + 8)
            with dve.Fori(1, FF_STEPS // 2) as r:
                for b in range(2):
                    ff_step(2 * r + b, b, 12 * r + (6 * b + T_FF + 2))
            ff_step(FF_STEPS - 1, 0, T_FF + 6 * (FF_STEPS - 1) + 2)
            dve.wait_ge(tile_out, EV_GDN)
            V.tensor_tensor(both_g[:, :], vec[:, VEC_AT["final_g"]:VEC_AT["final_g"] + KT],
                            vec[:, VEC_AT["gdn_g"]:VEC_AT["gdn_g"] + KT], ALU.mult).then_inc(fin_scaled, 1)
            dve.wait_ge(fin_scaled, 1)

            def lo_gained(k):
                dve.wait_ge(h_hi_done, KT * HGDN + k + 1)
                V.scalar_tensor_tensor(hlo[:, k, :], xres[:, k, :], both_g[:, k:k + 1], hhi[:, k, :].bitcast(F32), ALU.mult,
                                       ALU.subtract).then_inc(h_lo_done, 1)

            for m in range(KT):
                down_add(FF_STEPS - 1, T_GDN - 2, m)
                if m:
                    lo_gained(m - 1)
            lo_gained(KT - 1)
            for j, ssq in ((NFIN, N[:, 2, :]), (NGDN, N[:, 3, :])):
                for k in range(KT):
                    n = KT * j + k
                    dve.wait_ge(sq_ready, n + 1)
                    dve.wait_ge(sq_added, n)
                    if k:
                        V.tensor_tensor(ssq, ssq, N[:, k % 2, :], ALU.add).then_inc(sq_added, 1)
                    else:
                        V.tensor_copy(ssq, N[:, k % 2, :]).then_inc(sq_added, 1)
            dve.wait_ge(norm_root, NFIN + 1)
            done(V.reciprocal(R_FIN, R_FIN))
            settle()
            done(V.tensor_tensor(R_TMP, R_FIN, R_FIN, ALU.mult))
            settle()
            V.tensor_tensor(R_TMP, R_TMP, pa[:, NB:2 * NB], ALU.mult).then_inc(fin_scaled, 1)
            dve.wait_ge(norm_root, NGDN + 1)
            done(V.reciprocal(R_TMP, R_TMP))
            settle()
            V.tensor_tensor(R_H, R_TMP, R_FIN, ALU.mult).then_inc(norm_rstd, 1)
            dve.wait_ge(norm_rstd, S_GDN + 1)

            def t3(i):
                return tiny[:, i, :].rearrange("p (n h) -> p n h", h=8)

            def bias_row(at):
                return row[:, at:at + 8].rearrange("p (a h) -> p a h", a=1).broadcast_to([P, NB, 8])

            def gdn_gates():
                ab = tiny[:, 0:2, :].rearrange("p a c -> p (a c)").rearrange("p (n c) -> p n c", c=N_AB)
                dve.wait_ge(ab_out, 2)
                done(V.tensor_tensor(ab, ab, R_H.rearrange("p (n a) -> p n a", a=1).broadcast_to([P, NB, N_AB]), ALU.mult))
                settle()
                done(V.tensor_tensor(t3(2), ab[:, :, 0:GDN], bias_row(GDN), ALU.add))
                done(V.tensor_copy(t3(6), ab[:, :, GDN:N_AB]))
                settle()
                V.scalar_tensor_tensor(tiny[:, 3, :], tiny[:, 2, :], -1.0, tiny[:, 2, :], ALU.mult, ALU.max).then_inc(ab_e, 1)
                dve.wait_ge(ab_e, 2)
                done(V.scalar_tensor_tensor(tiny[:, 4, :], tiny[:, 2, :], 0.0, tiny[:, 3, :], ALU.max, ALU.add))
                done(V.tensor_scalar(tiny[:, 6, :], tiny[:, 6, :], 1.0, None, ALU.add))
                settle()
                done(V.reciprocal(tiny[:, 6, :], tiny[:, 6, :]))
                settle()
                V.scalar_tensor_tensor(t3(5), t3(4), -1.0, bias_row(0), ALU.mult, ALU.mult).then_inc(ab_ready, 1)

            def gdn_decays():
                dve.wait_ge(gc_out, 1)
                V.tensor_tensor(tiny[:, 9, :], tiny[:, 8, :], tiny[:, 7, :], ALU.subtract).then_inc(gc_diff, 1)
                dve.wait_ge(gc_out, 2)
                V.tensor_scalar(tiny[:, 10, :], tiny[:, 10, :], -1.0, None, ALU.mult).then_inc(gc_ready, 1)
                dve.wait_ge(gc_ready, 1)

            dve.wait_ge(spilled, 16 * KT)
            V.memset(GP0[:, 0:3], 0.0)
            V.memset(GP1[:, 0:3], 0.0).then_inc(pads_zero, 1)
            NL = len(LEVELS)

            def even(ap, b):
                return ap.rearrange("p (a two b) -> p a two b", two=2, b=b)[:, :, 0, :]

            def gdn_tile(h, j):
                t, n = T_GDN + 4 * h + j, 3 * h + j
                dve.wait_ge(pe_slot, t + 1)
                if h == j == 0:
                    dve.wait_ge(wide_out, 3)
                dst = (GP0, GP1)[n % 2][:, 3:3 + S] if j < 3 else H[:, 2 + h % 2, :]
                settle()
                V.tensor_tensor(dst, gp[t % 2][:, :], WIDE_GDN, ALU.mult).then_inc(tile_out, 1)

            def tap(h, j, i):
                n, c = 3 * h + j, gdn_dst(h, j)
                if i == 2:
                    dve.wait_ge(gd_tap3, n + 1)
                settle()
                last = V.scalar_tensor_tensor(c, (GP0, GP1)[n % 2][:, i:i + S], vc("gdn_w", (i * 3 + j) * GDN + h), c,
                                              ALU.mult, ALU.add)
                if i:
                    done(last)
                else:
                    last.then_inc(gd_conv, 1)

            def gdn_rule(g, s):
                if s == 0:
                    dve.wait_ge(gd_gr, g + 1)
                    for n in range(NB):
                        col = n * GDN + g
                        last = V.tensor_scalar(ck(TI, n), ck(pa, n), tiny[:, 7, col:col + 1], 0.0, ALU.subtract, ALU.min)
                    last.then_inc(gd_diff, 1)
                    dve.wait_ge(gd_exp, 2 * g + 1)
                    done(V.tensor_tensor(chunks(AT), chunks(TI), over(cn("causal"), NB), ALU.mult))
                if s == 5:
                    dve.wait_ge(gd_kk, g + 1)
                    for n in range(NB):
                        last = V.scalar_tensor_tensor(ck(MT, n), ck(pb, n), by_head[:, g % 2, BETA_RK2, n:n + 1], ck(TI, n), ALU.mult,
                                                      ALU.mult)
                    last.then_inc(gd_mt, 1)
                if s == 6:
                    dve.wait_ge(gd_attn_mm, g + 1)
                    settle()
                    for n in range(NB):
                        last = V.scalar_tensor_tensor(ck(AT, n), ck(pa, n), by_head[:, g % 2, R_K, n:n + 1], ck(AT, n), ALU.mult,
                                                      ALU.mult)
                    last.then_inc(gd_attn, 1)
                if s == 7:
                    dve.wait_ge(gd_mt, g + 1)
                    done(V.tensor_tensor(chunks(TT), chunks(MT), over(cn("pair_t"), NB), ALU.mult))
                    settle()
                    V.tensor_tensor(chunks(TT), chunks(TT), over(ident, NB), ALU.add).then_inc(gd_t0, 1)
                if s == 20:
                    dve.wait_ge(gd_exp, 2 * g + 2)
                    dve.wait_ge(gd_silu, 3 * g + 1)
                    done(V.tensor_tensor(N[:, 1, :], N[:, 1, :], yt[:, g, :], ALU.mult))
                for l, b in enumerate(LEVELS):
                    if s == 13 + 4 * l:
                        dve.wait_ge(inv_x_mm, NL * g + l + 1)
                        mask = cn("levels", l, P // 2).rearrange("p (a c) -> p a c", a=1).broadcast_to([P, NB, P // 2])
                        V.tensor_tensor(XB.rearrange("p (n c) -> p n c", c=P // 2),
                                        pa[:, 0:HALF].rearrange("p (n c) -> p n c", c=P // 2), mask, ALU.mult).then_inc(inv_x, 1)
                    if s == 15 + 4 * l:
                        dve.wait_ge(inv_y_mm, NL * g + l + 1)
                        if l:
                            dve.wait_ge(inv_turn, NL * g + l)
                        V.tensor_tensor(even(TI, b), even(TI, b), pa[:, HALF:S].rearrange("p (a b) -> p a b", b=b),
                                        ALU.subtract).then_inc(inv_t, 1)
                        dve.wait_ge(inv_t, NL * g + l + 1)
                if s >= 38 and (s - 38) // 3 < NB:
                    n = (s - 38) // 3
                    u, col = NB * g + n, n * GDN + g
                    if (s - 38) % 3 == 0:
                        if u:
                            dve.wait_ge(ch_vn_mm, u)
                        if n == 0:
                            dve.wait_ge(gd_vb, g + 1)
                            V.tensor_copy(rhs_r[:, :], ck(N[:, 3, :], 0)).then_inc(ch_r, 1)
                        else:
                            dve.wait_ge(ch_ks, (NB - 1) * g + n)
                            V.scalar_tensor_tensor(rhs_r[:, :], pa[:, 0:P], tiny[:, 10, col:col + 1], ck(N[:, 3, :], n), ALU.mult,
                                                   ALU.add).then_inc(ch_r, 1)
                    if (s - 38) % 3 == 2:
                        dve.wait_ge(ch_s_mm, u + 1)
                        if n == 0:
                            V.tensor_copy(state[:, :], pa[:, P:2 * P]).then_inc(ch_s, 1)
                        else:
                            dve.wait_ge(ch_s, u)
                            V.scalar_tensor_tensor(state[:, :], state[:, :], tiny[:, 8, col:col + 1], pa[:, P:2 * P], ALU.mult,
                                                   ALU.add).then_inc(ch_s, 1)

            for w in range(GDN + 2):
                g, h = w - 1, w
                for s in range(65):
                    if w == GDN and 2 <= s < KT:
                        lo_part(HGO, s - 2, yt[:, s - 2, :], hhi, hlo)
                    if (w, s) in ((GDN, 21), (GDN + 1, 21)):
                        lo_part(HGO, w - 2, yt[:, w - 2, :], hhi, hlo)
                    if h < GDN and s in (16, 32, 48, 64):
                        gdn_tile(h, s // 16 - 1)
                    if w == 0 and s == 36:
                        gdn_gates()
                    if w == 0 and s == 46:
                        gdn_decays()
                    if 0 <= g < GDN:
                        gdn_rule(g, s)
                    if g >= 1 and s == 2:
                        dve.wait_ge(go_ss, g)
                        if g >= 2:
                            dve.wait_ge(go_wide, g - 1)
                        r_q = by_head[:, (g - 1) % 2, R_Q, :]
                        done(V.tensor_tensor(R_O, pb[:, 0:NB], r_q, ALU.mult))
                        settle()
                        V.tensor_tensor(R_O, R_O, r_q, ALU.mult).then_inc(go_scaled, 1)
                    if g >= 1 and s == 5:
                        dve.wait_ge(go_root, g)
                        done(V.reciprocal(R_O, R_O))
                        settle()
                        V.tensor_tensor(R_O, R_O, by_head[:, (g - 1) % 2, R_Q, :], ALU.mult).then_inc(go_rstd, 1)
                    if g >= 1 and s == 14:
                        o = yt[:, g - 1, :]
                        dve.wait_ge(go_wide, g)
                        V.scalar_tensor_tensor(o, o, vc("o_g", 0), pb, ALU.mult, ALU.mult).then_inc(go_used, 1)
                    if g >= 1 and s == 19:
                        o = yt[:, g - 1, :]
                        dve.wait_ge(gd_z, g)
                        dve.wait_ge(go_used, g)
                        V.tensor_tensor(o, o, H[:, 2 + (g - 1) % 2, :], ALU.mult).then_inc(y_done, 1)
                    if h >= GDN:
                        continue
                    if s in (18, 22, 26):
                        tap(h, 0, (26 - s) // 4)
                    if s in (34, 36, 38):
                        tap(h, 1, 2 - (34, 36, 38).index(s))
                    if s in (50, 53, 56):
                        tap(h, 2, (56 - s) // 3)
                    if s == 62:
                        dve.wait_ge(gd_root, h + 1)
                        done(V.reciprocal(cols_of_head(h, R_K, 2), cols_of_head(h, K_NORM, 2)))
                        settle()
                        r_k, r_q = by_head[:, h % 2, R_K, :], by_head[:, h % 2, R_Q, :]
                        done(V.tensor_tensor(by_head[:, h % 2, BETA_RK, :], t3(6)[:, :, h], r_k, ALU.mult))
                        done(V.tensor_tensor(by_head[:, h % 2, DECAY_RK, :], t3(9)[:, :, h], r_k, ALU.mult))
                        done(V.tensor_scalar(r_q, r_q, GDN_DK ** -0.5, None, ALU.mult))
                        settle()
                        V.tensor_tensor(by_head[:, h % 2, BETA_RK2, :], by_head[:, h % 2, BETA_RK, :], r_k, ALU.mult).then_inc(gd_cols, 1)
                        dve.wait_ge(gd_cols, h + 1)
            def add_shares(t0, ev, n, norm):
                for f, m in enumerate(FINAL):
                    if f >= 2:
                        if f < KT - 1:
                            dve.wait_ge(share_mm, (PART + KT - 1) * n + PART + f + 1)
                        else:
                            dve.wait_ge(pe_slot, t0 + KT)
                        dve.wait_ge(tile_out, ev + m + 1)
                        V.tensor_tensor(yt[:, m, :], yt[:, m, :], gp[m % 2][:, :], ALU.add).then_inc(share_added, 1)
                    if f:
                        add_square(norm, f - 1)
                add_square(norm, KT - 1)

            def post_root(j):
                dve.wait_ge(norm_root, j + 1)
                V.reciprocal(R_TMP, R_TMP).then_inc(norm_rstd, 1)

            def post_scale(k, gain, reload):
                dve.wait_ge(x_loaded[k], reload)
                V.scalar_tensor_tensor(yt[:, k, :], yt[:, k, :], vc(gain, k), pa, ALU.mult, ALU.mult).then_inc(post_scaled, 1)

            add_shares(T_GO, EV_GO, 0, NGP)
            dve.wait_ge(norm_wide, W_FIN + 1)
            for k in range(KT):
                if k == 3:
                    post_root(NGP)
                dve.wait_ge(x_loaded[k], 48)
                done(V.scalar_tensor_tensor(xres[:, k, :], xres[:, k, :], vc("final_g", k), pb, ALU.mult, ALU.mult))
            settle()
            dve.wait_ge(norm_wide, W_GP + 1)
            LAG = 3
            for k in range(KT + LAG):
                if k < KT:
                    post_scale(k, "gdn_post_g", 48)
                if k >= LAG:
                    lo_part(HFOX, k - LAG, xres[:, k - LAG, :], hhi, hlo)
            for k in range(KT):
                add_square(NFOX, k)
            dve.wait_ge(norm_root, NFOX + 1)
            V.reciprocal(R_H, R_H).then_inc(norm_rstd, 1)
            dve.wait_ge(norm_rstd, S_FOX + 1)
            done(V.tensor_tensor(R_H2, R_H, R_H, ALU.mult))
            settle()

            def fox_gates():
                dve.wait_ge(f_out, 2)
                done(V.tensor_tensor(t3(0), t3(0), by_token(t3(0), R_H), ALU.mult))
                settle()
                done(V.tensor_tensor(t3(2), t3(0), bias_row(N_AB), ALU.add))
                settle()
                V.scalar_tensor_tensor(tiny[:, 3, :], tiny[:, 2, :], -1.0, tiny[:, 2, :], ALU.mult, ALU.max).then_inc(f_e, 1)
                dve.wait_ge(f_e, 2)
                V.scalar_tensor_tensor(tiny[:, 11, :], tiny[:, 2, :], 0.0, tiny[:, 3, :], ALU.min, ALU.subtract).then_inc(f_ready, 1)

            def fox_sums():
                dve.wait_ge(c_mm, 1)
                within, total = [pb[:, i * 64:(i + 1) * 64].rearrange("p (n h) -> p n h", h=FOX) for i in range(2)]
                done(V.tensor_copy(t3(12)[:, 0, :], total[:, 0, :]))
                for n in range(1, NB - 1):
                    settle()
                    done(V.tensor_tensor(t3(12)[:, n, :], t3(12)[:, n - 1, :], total[:, n, :], ALU.add))
                done(V.tensor_copy(t3(13)[:, 0, :], within[:, 0, :]))
                settle()
                V.tensor_tensor(t3(13)[:, 1:NB, :], within[:, 1:NB, :], t3(12)[:, 0:NB - 1, :], ALU.add).then_inc(c_ready, 1)

            dve.wait_ge(spilled, 2 * 16 * KT)
            done(V.scalar_tensor_tensor(stat[:, 24:25], vc("qn_g", 0), FOX_D ** -0.5, vc("kn_g", 0), ALU.mult, ALU.mult))
            settle()
            def fox_max(g, q):
                u = NB * g + q
                z = 4 * (q % 2)
                sc = X4(3 + q % 2)
                dve.wait_ge(fx_s_mm, u + 1)
                if u >= 2:
                    dve.wait_ge(fx_turn, fox_round((u - 2) // NB, (u - 2) % NB, (u - 2) % NB // 4) + 1)
                last = q * P
                r_q = R_QK[:, NB + q:NB + q + 1]
                done(V.scalar_tensor_tensor(sc[:, last:last + P], pa[:, last:last + P], r_q, ck(X4(2), q), ALU.mult, ALU.subtract))
                if q:
                    done(V.scalar_tensor_tensor(sc[:, 0:last], pa[:, 0:last], r_q, X4(1)[:, 0:last], ALU.mult, ALU.subtract))
                settle()
                done(V.tensor_reduce(stat[:, 12 + z:13 + z], sc[:, 0:last + P], AX_X, ALU.max))
                settle()
                V.tensor_scalar(stat[:, 14 + z:15 + z], stat[:, 12 + z:13 + z], -1.0, None, ALU.mult).then_inc(fx_s, 1)

            def fox_rescale(g, q):
                z = 4 * (q % 2)
                dve.wait_ge(fx_exp, NB * g + q + 1)
                done(V.reciprocal(stat[:, 15 + z:16 + z], stat[:, 15 + z:16 + z]))
                settle()
                p = X4(3 + q % 2)[:, 0:(q + 1) * P]
                V.tensor_scalar(p, p, stat[:, 15 + z:16 + z], None, ALU.mult).then_inc(fx_p, 1)

            def fox_gate(g, f):
                cols = slice(f * HALF, (f + 1) * HALF)
                dve.wait_ge(fx_o, NB * g + 4 * f + 4)
                dve.wait_ge(fx_z, g + 1)
                V.tensor_tensor(yt[:, g, cols], pb[:, HALF:S], H[:, 2 + g % 2, cols], ALU.mult).then_inc(fx_y, 1)

            for w in range(FOX + 1):
                g, h = w - 1, w
                for s in range(65):
                    if w == FOX and 1 <= s < KT:
                        lo_part(HFO, s - 1, yt[:, s - 1, :], hhi, hlo)
                    if w == 0 and s == 36:
                        fox_gates()
                    if w == 0 and s == 40:
                        fox_sums()
                    if h < FOX and s == 64:
                        t = T_FOX + 4 * h + 3
                        dve.wait_ge(pe_slot, t + 1)
                        dve.wait_ge(tile_out, EV_FOX + 4 * h + 3)
                        if h == 0:
                            dve.wait_ge(wide_out, 4)
                        V.tensor_tensor(H[:, 2 + h % 2, :], gp[t % 2][:, :], WIDE_FOX, ALU.mult).then_inc(tile_out, 1)
                    for q in range(NB):
                        if g >= 0 and q and s == 6 * q - 4:
                            fox_max(g, q)
                        if g >= 0 and q and s == 6 * q - 2:
                            fox_rescale(g, q)
                        if g >= 0 and q % 4 == 3 and s == 6 * q + 4:
                            fox_gate(g, q // 4)
                    if h == FOX:
                        continue
                    if s == 48:
                        dve.wait_ge(fx_ss, h + 1)
                        if h:
                            dve.wait_ge(fx_wide, h)
                        V.tensor_tensor(R_QK.rearrange("p (j n) -> p j n", j=2), pa[:, 0:2 * NB].rearrange("p (j n) -> p j n", j=2),
                                        R_H2.rearrange("p (a n) -> p a n", a=1).broadcast_to([P, 2, NB]), ALU.mult).then_inc(fx_rstd, 1)
                        dve.wait_ge(fx_root, h + 1)
                        done(V.reciprocal(R_QK, R_QK))
                        settle()
                        V.tensor_tensor(R_QK.rearrange("p (j n) -> p j n", j=2), R_QK.rearrange("p (j n) -> p j n", j=2),
                                        R_H.rearrange("p (a n) -> p a n", a=1).broadcast_to([P, 2, NB]), ALU.mult).then_inc(fx_rstd, 1)
                    if s == 53:
                        dve.wait_ge(fx_vturn, h + 1)
                        if h:
                            dve.wait_ge(fx_o, NB * h)
                        V.tensor_tensor(chunks(X4(0)), chunks(pb), by_token(chunks(pb), R_H), ALU.mult).then_inc(fx_v, 1)
                    if s == 58:
                        dve.wait_ge(c_moved, 16 * (NB + h + 1))
                        done(V.tensor_tensor(chunks(X4(2)), chunks(X4(1)), over(cn("future"), NB), ALU.add))
                        settle()
                    if s == 51:
                        k = H[:, h % 2, :]
                        dve.wait_ge(fx_wide, h + 1)
                        V.scalar_tensor_tensor(k, k, stat[:, 24:25], pa, ALU.mult, ALU.mult).then_inc(fx_qk, 1)
                    if s == 60:
                        fox_max(h, 0)
                    if s == 62:
                        fox_rescale(h, 0)
            lo_part(HFO, KT - 1, yt[:, KT - 1, :], hhi, hlo)
            add_shares(T_FO, EV_FO, 1, NFP)
            post_root(NFP)
            dve.wait_ge(norm_wide, W_FP + 1)
            for k in range(KT):
                post_scale(k, "fox_post_g", 64)
            for k in range(OUT_POOL, KT):
                dve.wait_ge(post_scaled, KT + k + 1)
                V.tensor_tensor(xres[:, k, :], xres[:, k, :], yt[:, k, :], ALU.add).then_inc(tile_added, 1)


def kernel(**inputs):
    from concourse import bacc
    from concourse.bass_utils import run_bass_kernel_spmd

    a = {name: np.asarray(value) for name, value in inputs.items()}

    def tiles(w):
        return w.reshape(w.shape[0] // P, P, -1, P).transpose(2, 1, 0, 3)

    def by_head(w, order):
        blocks = w.reshape(KT, P, KT, P)
        slabs = np.stack([blocks[k, :, m] for m, k in order + [(m, KT - 1) for m in FINAL]], 1)
        return slabs.reshape(P, KT, KT, P).transpose(1, 0, 2, 3)

    def cols(v):
        return v.reshape(-1, P).T

    w_in, gdn_in = tiles(a["w_in"][0]), tiles(a["gdn_w_in_2"][0][:, :4 * D])
    kv, fox_in = tiles(a["kv_w_2"][:, :2 * D]), tiles(a["fox_w_in_2"][0])
    ff_up = tiles(a["ffn_w_up"][0]).reshape(2, PAIRS, P, KT, P).transpose(1, 0, 2, 3, 4).reshape(2 * PAIRS, P, KT, P)
    ff_down = a["ffn_w_down"][0].reshape(FF_STEPS, 2, P, 2, 4, P).transpose(0, 3, 2, 4, 1, 5).reshape(FF_STEPS, 2, P, KT, P)
    steps = [ff_up[0:4]]
    for i in range(FF_STEPS):
        steps += [ff_up[4 * (i + 1):4 * (i + 2)], ff_down[i]]
    w_out = tiles(a["w_out"][0])[:, :, [0, 1, 2, 3, 7, 6, 5, 4]]
    xa_kv = tiles(a["xa_wkv"][0])
    mix_out = np.stack([(w_out if kind == "x" else xa_kv)[m] for kind, m in MIX_OUT])
    stream = [w_in[[4 * j + h for h in range(RET_HEADS) for j in range(4)]], w_in[19:15:-1], mix_out,
              tiles(a["xa_wq"][0]), tiles(a["xa_wo"][0]), *steps,
              gdn_in[[8 * j + h for h in range(GDN_HEADS) for j in range(4)]], by_head(a["gdn_w_out_2"][0], GO_ORDER)]
    for h in range(FOX_HEADS):
        stream += [kv[[h]], fox_in[[h]], kv[[8 + h]], fox_in[[8 + h]]]
    stream.append(by_head(a["fox_w_out_2"][0], FO_ORDER))
    ff_order = [v * PAIRS + p for p in range(PAIRS) for v in range(2)]
    vecs = {"mix_g": a["mix_norm_g"], "mem_g": a["mem_norm_g"], "xa_g": a["xa_norm_g"], "ffn_g": a["ffn_norm_g"],
            "final_g": a["final_norm_g"], "gdn_g": a["gdn_pre_norm_2"], "gdn_post_g": a["gdn_post_norm_2"],
            "kv_g": a["kv_norm_2"], "fox_g": a["fox_pre_norm_2"], "fox_post_g": a["fox_post_norm_2"],
            "gn_g": a["ret_gn_g"], "pool_scale": a["pool_scale"].reshape(4, P)[::-1], "o_g": a["gdn_o_norm_2"], "kn_g": a["kv_k_norm_2"],
            "qn_g": a["fox_q_norm_2"], "gdn_w": a["gdn_conv_w_2"],
            "ff_b": a["ffn_conv_b"][0].reshape(-1, P)[ff_order],
            "ff_w": a["ffn_conv_w"][0].reshape(3, -1, P)[:, ff_order]}
    vecs["inv_freq"] = np.exp(-math.log(10000.0) * (np.arange(P) % 64) * 2 / RET_DH).astype(np.float32)
    arrays = {
        "w_stream": np.concatenate(stream),
        "x_t": a["x"][0].T.reshape(KT, P, S),
        "mem_t": a["mem"][0].T.reshape(KT, P, N_MEM).transpose(1, 0, 2),
        "positions": a["positions"].reshape(1, S),
        "vecs": np.concatenate([cols(vecs[name]) for name, _ in VEC_NAMES], 1),
        "rows": np.concatenate([a["gdn_a_log_2"][0], a["gdn_dt_bias_2"][0], a["kv_forget_bias_2"]]).reshape(1, N_SMALL),
        "small_w": np.concatenate([a["gdn_w_in_2"][0][:, 4 * D:], a["kv_w_2"][:, 2 * D:]], 1)
        .reshape(KT, P, N_SMALL).transpose(1, 0, 2),
        "pool_w": a["pool_w"][0][::-1].transpose(1, 0, 2),
        "consts": shape_constants(),
    }
    arrays = {name: np.ascontiguousarray(v) for name, v in arrays.items()}
    nc = bacc.Bacc("TRN2", target_bir_lowering=False, num_devices=1)
    args = [nc.dram_tensor(name, v.shape, mybir.dt.from_np(v.dtype), kind="ExternalInput").ap() for name, v in arrays.items()]
    c_rows = nc.dram_tensor("c_rows", (FOX_HEADS, NB, P), F32, kind="Internal").ap()
    x_spill = nc.dram_tensor("x_spill", (KT, P, S), F32, kind="Internal").ap()
    out = nc.dram_tensor("out_t", (KT, P, S), F32, kind="ExternalOutput").ap()
    build(nc, *args, x_spill, c_rows, out)
    got = run_bass_kernel_spmd(nc, [arrays], core_ids=[0]).results[0]["out_t"]
    return got.reshape(D, S).T.reshape(1, S, D)
```
